# Optimizing a Trainium2 kernel written in Bass

```python
import math
import jax, jax.numpy as jnp
from jax import lax
import numpy as np

D_MODEL = 1024
BATCH = 1
SEQ = 1024
DEPTH = 1

MIX_WIDTH = D_MODEL
HEAD_GROUP_DIM = 64
MLA_HEADS = 8
MLA_NOPE_DIM = 64
MLA_ROPE_DIM = 32
MLA_V_DIM = HEAD_GROUP_DIM
MLA_Q_RANK = 256
MLA_KV_RANK = 128
ROPE_THETA = 10000.0
Q_BLOCK = 128
HYENA_CHANNELS = MIX_WIDTH - MLA_HEADS * MLA_V_DIM
HYENA_GROUPS = HYENA_CHANNELS // HEAD_GROUP_DIM
HYENA_ORDER = 2
SHORT_CONV = 3
FILTER_BANDS = 16
FILTER_EMB = 2 * FILTER_BANDS + 1
FILTER_HIDDEN = 64
DECAY_TARGET = 1e-2
FAST_DECAY_PCT = 0.3
SLOW_DECAY_PCT = 1.5
MAX_DECAY = math.log(DECAY_TARGET) / FAST_DECAY_PCT
MIN_DECAY = math.log(DECAY_TARGET) / SLOW_DECAY_PCT
N_GROUPS = MLA_HEADS + HYENA_GROUPS
IN_COLS = MLA_Q_RANK + MLA_KV_RANK + MLA_ROPE_DIM + (HYENA_ORDER + 1) * HYENA_CHANNELS
IN_SPLITS = (MLA_Q_RANK, MLA_Q_RANK + MLA_KV_RANK, MLA_Q_RANK + MLA_KV_RANK + MLA_ROPE_DIM)
FFN_HIDDEN = 2816
FFN_RES = 0.5
EPS = 1e-6

kernel_name = 'hymba_mla_hyena_macaron'

def rmsnorm(x, g):
    xf = x.astype(jnp.float32)
    y = xf * lax.rsqrt(jnp.mean(xf * xf, axis=-1, keepdims=True) + EPS)
    return y.astype(x.dtype) * g

def swiglu(x, w_gate, w_up, w_down):
    return (jax.nn.silu(x @ w_gate) * (x @ w_up)) @ w_down

def rope_tables(seq):
    inv = 1.0 / (ROPE_THETA ** (jnp.arange(0, MLA_ROPE_DIM, 2, dtype=jnp.float32) / MLA_ROPE_DIM))
    ang = jnp.arange(seq, dtype=jnp.float32)[:, None] * inv[None, :]
    return jnp.cos(ang), jnp.sin(ang)

def apply_rope(x, cos, sin):
    half = x.shape[-1] // 2
    x1, x2 = x[..., :half], x[..., half:]
    cos = cos.astype(x.dtype)
    sin = sin.astype(x.dtype)
    return jnp.concatenate([x1 * cos - x2 * sin, x1 * sin + x2 * cos], axis=-1)

def mla(c_q, c_kv, k_rope, q_norm_g, w_uq, kv_norm_g, w_ukv):
    B, S, _ = c_q.shape
    q = (rmsnorm(c_q, q_norm_g) @ w_uq).reshape(B, S, MLA_HEADS, MLA_NOPE_DIM + MLA_ROPE_DIM)
    kv = (rmsnorm(c_kv, kv_norm_g) @ w_ukv).reshape(B, S, MLA_HEADS, MLA_NOPE_DIM + MLA_V_DIM)
    q_nope, q_pe = q[..., :MLA_NOPE_DIM], q[..., MLA_NOPE_DIM:]
    k_nope, v = kv[..., :MLA_NOPE_DIM], kv[..., MLA_NOPE_DIM:]
    cos, sin = rope_tables(S)
    q_pe = apply_rope(q_pe, cos[:, None, :], sin[:, None, :])
    k_pe = apply_rope(k_rope, cos, sin)
    scale = (MLA_NOPE_DIM + MLA_ROPE_DIM) ** -0.5
    q = jnp.concatenate([q_nope, q_pe], axis=-1) * scale
    k = jnp.concatenate([k_nope, jnp.broadcast_to(k_pe[:, :, None, :], (B, S, MLA_HEADS, MLA_ROPE_DIM))], axis=-1)
    n_blk = S // Q_BLOCK
    q_blocks = q.reshape(B, n_blk, Q_BLOCK, MLA_HEADS, q.shape[-1]).transpose(1, 0, 2, 3, 4)

    def attend(qb):
        s = jnp.einsum('bqhd,bkhd->bhqk', qb, k).astype(jnp.float32)
        p = jax.nn.softmax(s, axis=-1).astype(v.dtype)
        return jnp.einsum('bhqk,bkhd->bqhd', p, v)

    out = lax.map(attend, q_blocks)
    return out.transpose(1, 0, 2, 3, 4).reshape(B, S, MLA_HEADS * MLA_V_DIM)

def short_conv(u, w, b):
    S = u.shape[1]
    pad = SHORT_CONV // 2
    up = jnp.pad(u, ((0, 0), (pad, SHORT_CONV - 1 - pad), (0, 0)))
    y = b
    for tap in range(SHORT_CONV):
        y = y + up[:, tap:tap + S] * w[tap]
    return y

def hyena_filters(L, w1, b1, w2, b2, w3, freq):
    f32 = jnp.float32
    pos = jnp.arange(L, dtype=f32)
    t = pos / max(L - 1, 1)
    bands = jnp.linspace(1e-4, FILTER_BANDS - 1, FILTER_BANDS, dtype=f32)
    ang = (2.0 * math.pi * pos / L)[:, None] * bands[None, :]
    z = jnp.concatenate([t[:, None], jnp.cos(ang), -jnp.sin(ang)], axis=-1)
    fr = freq.astype(f32)
    h = jnp.sin(fr * (z @ w1.astype(f32) + b1.astype(f32)))
    h = jnp.sin(fr * (h @ w2.astype(f32) + b2.astype(f32)))
    h = h @ w3.astype(f32)
    deltas = jnp.abs(jnp.linspace(MIN_DECAY, MAX_DECAY, HYENA_CHANNELS, dtype=f32))
    decay = jnp.exp(-t[:, None] * deltas[None, :])
    h = h.reshape(L, HYENA_ORDER, 2, HYENA_CHANNELS) * decay[:, None, None, :]
    h_fwd, h_bwd = h[:, :, 0], h[:, :, 1]
    k = jnp.concatenate([h_fwd, jnp.zeros((1, HYENA_ORDER, HYENA_CHANNELS), f32), h_bwd[:0:-1]], axis=0)
    k = k / jnp.sum(jnp.abs(k), axis=0, keepdims=True)
    return jnp.fft.rfft(k, axis=0)

def fftconv(u, k_f, d):
    L = u.shape[1]
    uf32 = u.astype(jnp.float32)
    u_f = jnp.fft.rfft(uf32, n=2 * L, axis=1)
    y = jnp.fft.irfft(u_f * k_f[None], n=2 * L, axis=1)[:, :L]
    return (y + uf32 * d.astype(jnp.float32)).astype(u.dtype)

def hyena(u, conv_w, conv_b, w1, b1, w2, b2, w3, freq, d_skip):
    L = u.shape[1]
    u = short_conv(u, conv_w, conv_b)
    v, x1, x2 = jnp.split(u, HYENA_ORDER + 1, axis=-1)
    k_f = hyena_filters(L, w1, b1, w2, b2, w3, freq)
    z = fftconv(v, k_f[:, 0], d_skip[0]) * x1
    z = fftconv(z, k_f[:, 1], d_skip[1]) * x2
    return z

def setup_inputs(seed: int = 0) -> dict:
    key = jax.random.key(seed)
    ks = iter(jax.random.split(key, 40))

    def nrm(shape, scale):
        return jax.random.normal(next(ks), shape, jnp.float32) * scale

    def gain(shape):
        return 1.0 + nrm(shape, 0.02)

    L_ = DEPTH
    return {
        'x': nrm((BATCH, SEQ, D_MODEL), 1.0),
        'ffn1_norm_g': gain((L_, D_MODEL)),
        'ffn1_w_gate': nrm((L_, D_MODEL, FFN_HIDDEN), D_MODEL ** -0.5),
        'ffn1_w_up': nrm((L_, D_MODEL, FFN_HIDDEN), D_MODEL ** -0.5),
        'ffn1_w_down': nrm((L_, FFN_HIDDEN, D_MODEL), FFN_HIDDEN ** -0.5),
        'mix_norm_g': gain((L_, D_MODEL)),
        'w_in': nrm((L_, D_MODEL, IN_COLS), D_MODEL ** -0.5),
        'q_norm_g': gain((L_, MLA_Q_RANK)),
        'w_uq': nrm((L_, MLA_Q_RANK, MLA_HEADS * (MLA_NOPE_DIM + MLA_ROPE_DIM)), MLA_Q_RANK ** -0.5),
        'kv_norm_g': gain((L_, MLA_KV_RANK)),
        'w_ukv': nrm((L_, MLA_KV_RANK, MLA_HEADS * (MLA_NOPE_DIM + MLA_V_DIM)), MLA_KV_RANK ** -0.5),
        'hyena_conv_w': nrm((L_, SHORT_CONV, (HYENA_ORDER + 1) * HYENA_CHANNELS), SHORT_CONV ** -0.5),
        'hyena_conv_b': nrm((L_, (HYENA_ORDER + 1) * HYENA_CHANNELS), 0.01),
        'filt_w1': nrm((L_, FILTER_EMB, FILTER_HIDDEN), FILTER_EMB ** -0.5),
        'filt_b1': nrm((L_, FILTER_HIDDEN), 0.01),
        'filt_w2': nrm((L_, FILTER_HIDDEN, FILTER_HIDDEN), FILTER_HIDDEN ** -0.5),
        'filt_b2': nrm((L_, FILTER_HIDDEN), 0.01),
        'filt_w3': nrm((L_, FILTER_HIDDEN, HYENA_ORDER * 2 * HYENA_CHANNELS), FILTER_HIDDEN ** -0.5),
        'filt_freq': gain((L_, FILTER_HIDDEN)),
        'hyena_d': nrm((L_, HYENA_ORDER, HYENA_CHANNELS), 0.1),
        'head_norm_g': gain((L_, MIX_WIDTH)),
        'w_out': nrm((L_, MIX_WIDTH, D_MODEL), MIX_WIDTH ** -0.5),
        'ffn2_norm_g': gain((L_, D_MODEL)),
        'ffn2_w_gate': nrm((L_, D_MODEL, FFN_HIDDEN), D_MODEL ** -0.5),
        'ffn2_w_up': nrm((L_, D_MODEL, FFN_HIDDEN), D_MODEL ** -0.5),
        'ffn2_w_down': nrm((L_, FFN_HIDDEN, D_MODEL), FFN_HIDDEN ** -0.5),
        'final_norm_g': gain((D_MODEL,)),
    }

def reference(x, ffn1_norm_g, ffn1_w_gate, ffn1_w_up, ffn1_w_down, mix_norm_g, w_in,
              q_norm_g, w_uq, kv_norm_g, w_ukv, hyena_conv_w, hyena_conv_b,
              filt_w1, filt_b1, filt_w2, filt_b2, filt_w3, filt_freq, hyena_d,
              head_norm_g, w_out, ffn2_norm_g, ffn2_w_gate, ffn2_w_up, ffn2_w_down,
              final_norm_g):
    B, S, _ = x.shape
    for l in range(DEPTH):
        x = x + FFN_RES * swiglu(rmsnorm(x, ffn1_norm_g[l]), ffn1_w_gate[l], ffn1_w_up[l], ffn1_w_down[l])
        u = rmsnorm(x, mix_norm_g[l]) @ w_in[l]
        c_q, c_kv, k_rope, u_hy = jnp.split(u, IN_SPLITS, axis=-1)
        a = mla(c_q, c_kv, k_rope, q_norm_g[l], w_uq[l], kv_norm_g[l], w_ukv[l])
        h = hyena(u_hy, hyena_conv_w[l], hyena_conv_b[l], filt_w1[l], filt_b1[l],
                  filt_w2[l], filt_b2[l], filt_w3[l], filt_freq[l], hyena_d[l])
        mix = jnp.concatenate([a, h], axis=-1).reshape(B, S, N_GROUPS, HEAD_GROUP_DIM)
        mix = rmsnorm(mix, head_norm_g[l].reshape(N_GROUPS, HEAD_GROUP_DIM)).reshape(B, S, MIX_WIDTH)
        x = x + mix @ w_out[l]
        x = x + FFN_RES * swiglu(rmsnorm(x, ffn2_norm_g[l]), ffn2_w_gate[l], ffn2_w_up[l], ffn2_w_down[l])
    return rmsnorm(x, final_norm_g)


_drawn_inputs = setup_inputs


def setup_inputs(seed=0):
    import zlib

    import numpy as np

    out = dict(_drawn_inputs(seed))
    spreads = {}
    factors = {'ffn1_norm_g': 4.61,
     'q_norm_g': 5.572,
     'kv_norm_g': 2.914,
     'filt_b1': 8.0,
     'filt_b2': 6.018,
     'filt_freq': 6.108,
     'head_norm_g': 18.099,
     'ffn2_norm_g': 8.0,
     'final_norm_g': 7.833,
     'hyena_conv_b': 5.549}
    for name, (base, spread) in spreads.items():
        noise = np.random.default_rng([zlib.crc32(name.encode()), seed]).standard_normal(out[name].shape)
        drawn = base * np.exp(spread * noise) if base else spread * noise
        out[name] = __import__('jax').numpy.asarray(drawn.astype(out[name].dtype))
    for name, factor in factors.items():
        out[name] = (out[name] * factor).astype(out[name].dtype)
    return out
```

```python
import math
from contextlib import ExitStack

import numpy as np
import concourse.bass as bass
import concourse.mybir as mybir

F32 = mybir.dt.float32
F32R = mybir.dt.float32r
ACT = mybir.ActivationFunctionType
ALU = mybir.AluOpType
AXX = mybir.AxisListType.X

P = 128
SEQ = 1024
D = 1024
KT = D // P
TT = SEQ // P
HALF = 512
FFN = 2816
EPS = 1e-6
Q_RANK, KV_RANK, ROPE = 256, 128, 32
HEADS, NOPE, VD = 8, 64, 64
QK = NOPE + ROPE
C = 512
HID = 64
BANDS = 16
EMB = 2 * BANDS + 1
WT = SEQ // 2 // P
GROUPS = 16
IN_COLS = Q_RANK + KV_RANK + ROPE + 3 * C

ds = bass.ds


def by_two(eng, start, end):
    return eng.Fori(start, end - 1, 2)


def split_hi_lo(a):
    a32 = a.astype(np.float32)
    bits = a32.view(np.uint32).astype(np.uint64)
    hi = ((bits + 0x7FF + ((bits >> 12) & 1)) & 0xFFFFF000).astype(np.uint32).view(np.float32)
    return hi, (a32 - hi).astype(np.float32)


def transform_tables():
    w = np.arange(SEQ // 2) + 0.5
    t = np.arange(SEQ)
    ang = math.pi / SEQ * w[:, None] * t[None, :]
    both = np.stack([np.cos(ang), np.sin(ang)])
    hl = np.stack(split_hi_lo(both), axis=1)
    x = hl.reshape(2, 2, WT, P, TT // 2, P, 2)
    fwd = x.transpose(2, 6, 5, 4, 0, 1, 3).reshape(2 * WT * P, (TT // 2) * 4 * P)
    inv = x.transpose(6, 4, 3, 2, 0, 1, 5).reshape(TT * P, WT * 4 * P) / SEQ
    return np.ascontiguousarray(fwd, np.float32), np.ascontiguousarray(inv, np.float32)


def parity_order():
    return np.concatenate([np.arange(0, SEQ, 2), np.arange(1, SEQ, 2)])


def filter_features():
    f = np.float32
    pos = np.arange(SEQ, dtype=f)
    t = pos / f(SEQ - 1)
    bands = np.linspace(1e-4, BANDS - 1, BANDS, dtype=f)
    ang = (f(2.0 * math.pi) * pos / f(SEQ))[:, None] * bands[None, :]
    z = np.concatenate([t[:, None], np.cos(ang), -np.sin(ang)], axis=-1).astype(f)
    return np.ascontiguousarray(z[parity_order()].T)


def filter_decay():
    f = np.float32
    t = np.arange(SEQ, dtype=f) / f(SEQ - 1)
    lo, hi = math.log(1e-2) / 1.5, math.log(1e-2) / 0.3
    deltas = np.abs(np.linspace(lo, hi, C, dtype=f))
    dec = np.exp(-t[:, None] * deltas[None, :]).astype(f)
    both = np.stack([dec, dec], axis=1)
    both[0, 1] = 0.0
    return np.ascontiguousarray(both[parity_order()].reshape(SEQ, 2 * C))


def rope_rows():
    f = np.float32
    inv = (1.0 / (f(10000.0) ** (np.arange(0, ROPE, 2, dtype=f) / f(ROPE)))).astype(f)
    ang = np.arange(SEQ, dtype=f)[None, :] * inv[:, None]
    cos, sin = np.cos(ang).astype(f), np.sin(ang).astype(f)
    return np.ascontiguousarray(np.concatenate([cos, cos, -sin, sin], axis=0))


class Chip:

    def __init__(self, nc, ctx):
        self.nc, self.sems = nc, []
        self.small_at = -(-nc.sbuf_base // 64) * 64
        self.small_end = self.small_at + 3072
        self.main = self.small_end
        self.ps = ctx.enter_context(nc.psum_tensor("ps", [P, 8 * HALF], F32))

    def at(self, name, kb, shape, dtype=F32):
        return self.nc.alloc_sbuf_tensor_at(name, shape, dtype, offset=self.main + int(kb * 1024))

    def small(self, name, shape, dtype=F32):
        size = 4
        for n in shape[1:]:
            size *= n
        t = self.nc.alloc_sbuf_tensor_at(name, shape, dtype, offset=self.small_at)
        self.small_at += -(-size // 32) * 32
        assert self.small_at <= self.small_end, name
        return t

    def sem(self, name):
        self.sems.append(self.nc.alloc_semaphore(name=name))
        return self.sems[-1]

    def recycle(self):
        self.nc.clear_and_free_semaphores(self.sems)
        self.nc.all_engine_barrier()
        self.sems = []

    def bank(self, n, rows=P, cols=HALF):
        return self.ps[0:rows, n * HALF:n * HALF + cols]

    def pair(self, n, rows=P):
        return self.ps[0:rows, n * 2 * HALF:(n + 1) * 2 * HALF]


def three_pass(nc, outs, w_hi, w_lo, x_hi, x_lo, start, stop):
    for n, out in enumerate(outs):
        nc.tensor.matmul(out, w_hi, x_hi[n], start=start, stop=False)
        nc.tensor.matmul(out, w_hi, x_lo[n], start=False, stop=False)
    for n, out in enumerate(outs):
        last = nc.tensor.matmul(out, w_lo, x_hi[n], start=False, stop=stop)
    return last


def halves(x, k):
    return [x[:, k, 0:HALF], x[:, k, HALF:2 * HALF]]


class FeatureNorm:

    def __init__(self, chip, tag, src, tiles, gain, hi, lo, squares, root, scaled, pair=0):
        self.nc, self.chip, self.src, self.tiles, self.gain = chip.nc, chip, src, tiles, gain
        self.hi, self.lo, self.squares, self.root, self.scaled, self.pair = hi, lo, squares, root, scaled, pair
        self.squared = chip.sem(f"{tag}_squared")
        self.summed = chip.sem(f"{tag}_summed")
        self.rooted = chip.sem(f"{tag}_rooted")
        self.rstd_ready = chip.sem(f"{tag}_rstd_ready")
        self.y_scaled = chip.sem(f"{tag}_y_scaled")
        self.hi_ready = chip.sem(f"{tag}_hi_ready")
        self.lo_ready = chip.sem(f"{tag}_lo_ready")

    def scalar(self, act, src_ready=None):
        nc = self.nc
        for k in range(self.tiles):
            if src_ready is not None:
                act.wait_ge(src_ready, k + 1)
            if k >= 2:
                act.wait_ge(self.summed, k - 1)
            nc.scalar.activation(self.squares[:, k % 2, :], self.src[:, k, :], ACT.Square).then_inc(self.squared, 1)
        act.wait_ge(self.summed, self.tiles)
        nc.scalar.activation(self.root[:, :], self.chip.pair(self.pair), ACT.Sqrt, bias=self.chip.eps[:, 0:1],
                             scale=1.0 / (self.tiles * P)).then_inc(self.rooted, 1)
        for k in range(self.tiles):
            act.wait_ge(self.y_scaled, k + 1)
            nc.scalar.activation(self.hi[:, k, :], self.scaled[:, k % 2, :], ACT.Copy).then_inc(self.hi_ready, 1)

    def tensor(self, pe):
        nc = self.nc
        for k in range(self.tiles):
            pe.wait_ge(self.squared, k + 1)
            for n in range(2):
                last = nc.tensor.matmul(self.chip.bank(2 * self.pair + n), self.chip.ones[:, :],
                                        self.squares[:, k % 2, n * HALF:(n + 1) * HALF],
                                        start=(k == 0), stop=(k == self.tiles - 1))
            last.then_inc(self.summed, 1)

    def vector(self, dve):
        nc = self.nc
        dve.wait_ge(self.rooted, 1)
        nc.vector.reciprocal(self.root[:, :], self.root[:, :]).then_inc(self.rstd_ready, 1)
        dve.wait_ge(self.rstd_ready, 1)

        def low(k):
            dve.wait_ge(self.hi_ready, k + 1)
            nc.vector.tensor_tensor(self.lo[:, k, :], self.scaled[:, k % 2, :], self.hi[:, k, :].bitcast(F32),
                                    ALU.subtract).then_inc(self.lo_ready, 1)

        for k in range(self.tiles):
            if k >= 2:
                dve.wait_ge(self.lo_ready, k - 1)
            nc.vector.scalar_tensor_tensor(out=self.scaled[:, k % 2, :], in0=self.src[:, k, :],
                                           scalar=self.gain[:, k:k + 1], in1=self.root[:, :],
                                           op0=ALU.mult, op1=ALU.mult).then_inc(self.y_scaled, 1)
            if k >= 1:
                low(k - 1)
        low(self.tiles - 1)


def filters_block(chip, dram, x_raw, x_loaded):
    nc = chip.nc
    decay = chip.at("f_decay", 0, [P, TT, 2 * C])
    tap_hi = chip.at("f_tap_hi", 64, [P, 2, TT, C], F32R)
    tap_lo = chip.at("f_tap_lo", 96, [P, 2, TT, C], F32R)
    table = [chip.at(f"f_table{s}", 128 + 8 * s, [P, TT // 2, 2, 2, P], F32R) for s in range(2)]
    w3 = chip.at("f_w3", 144, [HID, 4 * C])
    h2 = chip.at("f_h2", 152, [HID, SEQ])
    feat = chip.at("f_feat", 156, [EMB, SEQ])
    arg = chip.at("f_arg", 160, [HID, SEQ])
    turn = chip.at("f_turn", 164, [HID, SEQ])
    h1 = chip.at("f_h1", 168, [HID, SEQ])
    raw = [chip.at(f"f_raw{s}", 172 + 4 * s, [P, 2 * C]) for s in range(2)]
    mixd = [chip.at(f"f_mixd{s}", 180 + 4 * s, [P, 2, C]) for s in range(2)]
    mag = [chip.at(f"f_mag{s}", 188 + 4 * s, [P, 2 * C]) for s in range(2)]
    spec = chip.at("f_spec", 196, [P, 4, C])
    even = chip.at("f_even", 156, [P, 2, C])
    rnorm = chip.at("f_rnorm", 160, [P, C])
    skip = chip.at("f_skip", 162, [P, C])
    h2t = [chip.at(f"f_h2t{s}", 164 + 0.5 * s, [HID, P]) for s in range(2)]

    s = chip.sem
    loaded, w3_loaded, skip_loaded = s("f_loaded"), s("f_w3_loaded"), s("f_skip_loaded")
    linear, step, sine = s("f_linear"), s("f_step"), s("f_sine")
    h2t_ready, taps_out, decayed, mag_ready = s("f_h2t_ready"), s("f_taps_out"), s("f_decayed"), s("f_mag_ready")
    mixed, hi_ready, lo_ready, mag_summed = s("f_mixed"), s("f_hi_ready"), s("f_lo_ready"), s("f_mag_summed")
    rnorm_ready = s("f_rnorm_ready")
    table_loaded = [s(f"f_table_loaded{k}") for k in range(2)]
    table_used, even_copied, spec_step, spec_stored = (s("f_table_used"), s("f_even_copied"), s("f_spec_step"),
                                                       s("f_spec_stored"))
    SPEC_STEPS = 5
    UNITS = 2 * WT

    turns = 1.0 / (2.0 * math.pi)
    big = float(1.5 * 2 ** 23)
    c1 = 6.28125
    c2 = math.floor((2.0 * math.pi - c1) * 2 ** 20) / 2 ** 20
    c3 = 2.0 * math.pi - c1 - c2
    pi = 3.1415925

    with nc.Block() as block:
        @block.sync
        def _(sp):
            for dst, src in ((feat, dram["features"]), (chip.fw1, dram["filt_w1"]), (chip.fw2, dram["filt_w2"]),
                             (chip.fcol[:, 0:1], dram["filt_b1"]), (chip.fcol[:, 1:2], dram["filt_b2"]),
                             (chip.fcol[:, 2:3], dram["filt_freq"])):
                sp.dma_start(dst[:], src).then_inc(loaded, 16)
            sp.dma_start(w3[:], dram["filt_w3"]).then_inc(w3_loaded, 16)
            sp.dma_start(decay[:], dram["decay"].rearrange("(i p) c -> p i c", p=P)).then_inc(w3_loaded, 16)
            for r in range(2):
                sp.dma_start(table[r][:].bitcast(F32), dram["fwd"][r * P:(r + 1) * P, :]).then_inc(table_loaded[r], 16)
            sp.dma_start(x_raw[:], dram["x"].rearrange("(i p) d -> p i d", p=P)).then_inc(x_loaded, 16)

            for o in range(2):
                if o == 1:
                    sp.wait_ge(spec_step, SPEC_STEPS * WT)
                else:
                    sp.wait_ge(sine, 2)
                sp.dma_start(skip[:], dram["hyena_d"][o:o + 1, :].partition_broadcast(P)).then_inc(skip_loaded, 16)

                def spectrum(wt, more, o=o):
                    if more:
                        for r in range(2):
                            sp.wait_ge(table_used, UNITS * o + 2 * wt + r + 1)
                            row = (((2 * wt + 2 + r) % UNITS) if isinstance(wt, int) else (2 * wt + 2 + r)) * P
                            sp.dma_start(table[r][:].bitcast(F32), dram["fwd"][ds(row, P), :]).then_inc(table_loaded[r], 16)
                    sp.wait_ge(spec_step, SPEC_STEPS * (WT * o + wt + 1))
                    sp.dma_start(dram["spectra"][ds((WT * o + wt) * P, P), :], spec[:]).then_inc(spec_stored, 16)

                with sp.Fori(0, WT - 1) as wt:
                    spectrum(wt, True)
                spectrum(WT - 1, o == 0)
            sp.wait_ge(spec_stored, 16 * 2 * WT)

        @block.gpsimd
        def _(pool):
            pool.wait_ge(sine, 2)
            for o in range(2):
                def copy(i, slot, o=o):
                    if o or not isinstance(i, int):
                        pool.wait_ge(taps_out, TT * o + i - 1)
                    nc.gpsimd.tensor_copy(h2t[slot][:, :], h2[:, ds(i * P, P)]).then_inc(h2t_ready, 1)
                if o == 0:
                    copy(0, 0)
                    copy(1, 1)
                    lo = 2
                else:
                    lo = 0
                with by_two(pool, lo, TT) as i:
                    copy(i, 0)
                    copy(i + 1, 1)

        @block.tensor
        def _(pe):
            pe.wait_ge(loaded, 16 * 6)
            pe.wait_ge(chip.consts_ready, 1)
            for n in range(2):
                last = nc.tensor.matmul(chip.bank(n, HID), chip.fw1[:, :], feat[:, n * HALF:(n + 1) * HALF],
                                        start=True, stop=True)
            last.then_inc(linear, 1)
            pe.wait_ge(sine, 1)
            for n in range(2):
                last = nc.tensor.matmul(chip.bank(2 + n, HID), chip.fw2[:, :], h1[:, n * HALF:(n + 1) * HALF],
                                        start=True, stop=True)
            last.then_inc(linear, 1)
            pe.wait_ge(w3_loaded, 32)

            for o in range(2):
                def taps(i, slot, o=o):
                    pe.wait_ge(h2t_ready, TT * o + i + 1)
                    if o or not isinstance(i, int) or i >= 2:
                        pe.wait_ge(decayed, TT * o + i - 1)
                    for dr in range(2):
                        last = nc.tensor.matmul(chip.bank(2 * slot + dr), h2t[slot][:, :],
                                                w3[:, (2 * o + dr) * C:(2 * o + dr + 1) * C], start=True, stop=True)
                    last.then_inc(taps_out, 1)

                def magnitudes(i, slot, first, last, o=o):
                    pe.wait_ge(mag_ready, TT * o + i + 1)
                    for dr in range(2):
                        mm = nc.tensor.matmul(chip.bank(7), chip.ones[:, :], mag[slot][:, dr * C:(dr + 1) * C],
                                              start=(first and dr == 0), stop=(last and dr == 1))
                    mm.then_inc(mag_summed, 1)

                if o == 1:
                    pe.wait_ge(spec_step, SPEC_STEPS * WT)
                taps(0, 0)
                taps(1, 1)
                magnitudes(0, 0, True, False)
                with by_two(pe, 2, TT) as i:
                    taps(i, 0)
                    magnitudes(i - 1, 1, False, False)
                    taps(i + 1, 1)
                    magnitudes(i, 0, False, False)
                magnitudes(TT - 1, 1, False, True)

                pe.wait_ge(decayed, TT * (o + 1))
                pe.wait_ge(lo_ready, TT * (o + 1))

                def transform(wt, o=o):
                    for r in range(2):
                        pe.wait_ge(table_loaded[r], 16 * (WT * o + wt + 1))
                        if r == 0:
                            if not isinstance(wt, int):
                                pe.wait_ge(even_copied, WT * o + wt)
                        elif not isinstance(wt, int):
                            pe.wait_ge(spec_step, SPEC_STEPS * (WT * o + wt))
                        for tt in range(TT // 2):
                            for cs in range(2):
                                last = three_pass(nc, [chip.bank(2 * r + cs)], table[r][:, tt, cs, 0, :],
                                                  table[r][:, tt, cs, 1, :], [tap_hi[:, cs, r * (TT // 2) + tt, :]],
                                                  [tap_lo[:, cs, r * (TT // 2) + tt, :]], tt == 0, tt == TT // 2 - 1)
                        last.then_inc(table_used, 1)

                transform(0)
                with pe.Fori(1, WT) as wt:
                    transform(wt)

        @block.scalar
        def _(act):
            for layer in range(2):
                act.wait_ge(step, 7 * (layer + 1))
                nc.scalar.activation((h1, h2)[layer][:, :], arg[:, :], ACT.Sin).then_inc(sine, 1)
            for o in range(2):
                def tap(i, slot, dst, o=o):
                    act.wait_ge(decayed, TT * o + i + 1)
                    if o or not isinstance(i, int) or i >= 2:
                        act.wait_ge(mag_summed, TT * o + i - 1)
                    nc.scalar.activation(mag[slot][:, :], raw[slot][:, :], ACT.Abs).then_inc(mag_ready, 1)
                    act.wait_ge(mixed, 2 * (TT * o + i + 1))
                    nc.scalar.activation(dst, mixd[slot][:, :, :], ACT.Copy).then_inc(hi_ready, 1)
                if o == 1:
                    act.wait_ge(table_used, UNITS)
                tap(0, 0, tap_hi[:, :, 0, :])
                tap(1, 1, tap_hi[:, :, 1, :])
                with by_two(act, 2, TT) as i:
                    tap(i, 0, tap_hi[:, :, ds(i, 1), :].rearrange("p a b c -> p a (b c)"))
                    tap(i + 1, 1, tap_hi[:, :, ds(i + 1, 1), :].rearrange("p a b c -> p a (b c)"))

                def copy_even(wt, o=o):
                    act.wait_ge(table_used, UNITS * o + 2 * wt + 1)
                    if o or not isinstance(wt, int):
                        act.wait_ge(spec_step, SPEC_STEPS * (WT * o + wt))
                    nc.scalar.activation(even[:, :, :], chip.pair(0).rearrange("p (a c) -> p a c", a=2),
                                         ACT.Copy).then_inc(even_copied, 1)
                copy_even(0)
                with act.Fori(1, WT) as wt:
                    copy_even(wt)

        @block.vector
        def _(dve):
            for layer in range(2):
                at = 7 * layer
                dve.wait_ge(linear, layer + 1)
                if layer:
                    dve.wait_ge(sine, 1)
                nc.vector.tensor_scalar(arg[:, :], chip.pair(layer, HID), chip.fcol[:, layer:layer + 1],
                                        chip.fcol[:, 2:3], ALU.add, ALU.mult).then_inc(step, 1)
                dve.wait_ge(step, at + 1)
                nc.vector.tensor_scalar(turn[:, :], arg[:, :], turns, big, ALU.mult, ALU.add).then_inc(step, 1)
                dve.wait_ge(step, at + 2)
                nc.vector.tensor_scalar(turn[:, :], turn[:, :], big, None, ALU.subtract).then_inc(step, 1)
                for k, part in enumerate((c1, c2, c3)):
                    dve.wait_ge(step, at + 3 + k)
                    nc.vector.scalar_tensor_tensor(out=arg[:, :], in0=turn[:, :], scalar=-part, in1=arg[:, :],
                                                   op0=ALU.mult, op1=ALU.add).then_inc(step, 1)
                dve.wait_ge(step, at + 6)
                nc.vector.tensor_scalar(arg[:, :], arg[:, :], -pi, pi, ALU.max, ALU.min).then_inc(step, 1)

            dve.wait_ge(w3_loaded, 32)
            for o in range(2):
                def tap(i, slot, dec, hi, lo, o=o):
                    u = TT * o + i
                    again = bool(o) or not isinstance(i, int)
                    dve.wait_ge(taps_out, u + 1)
                    if again:
                        dve.wait_ge(mag_ready, u - 1)
                        dve.wait_ge(mixed, 2 * (u - 1))
                    nc.vector.tensor_tensor(raw[slot][:, :], chip.pair(slot), dec, ALU.mult).then_inc(decayed, 1)
                    dve.wait_ge(decayed, u + 1)
                    if again:
                        dve.wait_ge(hi_ready, u - 1)
                        dve.wait_ge(lo_ready, u - 1)
                    nc.vector.tensor_tensor(mixd[slot][:, 0, :], raw[slot][:, 0:C], raw[slot][:, C:2 * C],
                                            ALU.add).then_inc(mixed, 1)
                    nc.vector.tensor_tensor(mixd[slot][:, 1, :], raw[slot][:, 0:C], raw[slot][:, C:2 * C],
                                            ALU.subtract).then_inc(mixed, 1)
                    dve.wait_ge(mixed, 2 * (u + 1))
                    dve.wait_ge(hi_ready, u + 1)
                    nc.vector.tensor_tensor(lo, mixd[slot][:, :, :], hi, ALU.subtract).then_inc(lo_ready, 1)

                def tap_at(i, slot):
                    view = [t[:, :, ds(i, 1), :].rearrange("p a b c -> p a (b c)") for t in (tap_hi, tap_lo)]
                    tap(i, slot, decay[:, ds(i, 1), :].rearrange("p a c -> p (a c)"), view[0].bitcast(F32), view[1])

                for i in range(2):
                    tap(i, i, decay[:, i, :], tap_hi[:, :, i, :].bitcast(F32), tap_lo[:, :, i, :])
                with by_two(dve, 2, TT) as i:
                    tap_at(i, 0)
                    tap_at(i + 1, 1)
                dve.wait_ge(mag_summed, TT * (o + 1))
                if o == 1:
                    dve.wait_ge(spec_step, SPEC_STEPS * WT)
                nc.vector.reciprocal(rnorm[:, :], chip.bank(7)).then_inc(rnorm_ready, 1)
                dve.wait_ge(rnorm_ready, o + 1)
                dve.wait_ge(skip_loaded, 16 * (o + 1))

                def spectrum(wt, o=o):
                    u = WT * o + wt
                    at = SPEC_STEPS * u
                    dve.wait_ge(even_copied, u + 1)
                    dve.wait_ge(table_used, UNITS * o + 2 * wt + 2)
                    if o or not isinstance(wt, int):
                        dve.wait_ge(spec_stored, 16 * u)
                        dve.wait_ge(spec_step, at)
                    nc.vector.tensor_tensor(spec[:, 0:2, :], even[:, :, :],
                                            chip.pair(1).rearrange("p (a c) -> p a c", a=2), ALU.add).then_inc(spec_step, 1)
                    nc.vector.tensor_tensor(spec[:, 2, :], even[:, 0, :], chip.bank(2), ALU.subtract).then_inc(spec_step, 1)
                    nc.vector.tensor_tensor(spec[:, 3, :], chip.bank(3), even[:, 1, :], ALU.subtract).then_inc(spec_step, 1)
                    dve.wait_ge(spec_step, at + 3)
                    nc.vector.tensor_tensor(spec[:, :, :], spec[:, :, :],
                                            rnorm[:, :].unsqueeze(1).to_broadcast([P, 4, C]), ALU.mult).then_inc(spec_step, 1)
                    dve.wait_ge(spec_step, at + 4)
                    nc.vector.tensor_tensor(spec[:, 0:3:2, :], spec[:, 0:3:2, :],
                                            skip[:, :].unsqueeze(1).to_broadcast([P, 2, C]), ALU.add).then_inc(spec_step, 1)

                spectrum(0)
                with dve.Fori(1, WT) as wt:
                    spectrum(wt)


def input_block(chip, x_raw, x_loaded, xT, gain, x_hi, x_lo, prefetch):
    nc = chip.nc
    squares, root, scaled = norm_buffers(chip, "n1")
    norm = FeatureNorm(chip, "n1", xT, KT, gain, x_hi, x_lo, squares, root, scaled)
    turned, xT_ready = chip.sem("x_turned"), chip.sem("xT_ready")
    with nc.Block() as block:
        @block.sync
        def _(sp):
            prefetch(sp)

        @block.tensor
        def _(pe):
            pe.wait_ge(x_loaded, 16)
            for k in range(KT):
                if k >= 3:
                    pe.wait_ge(xT_ready, k - 2)
                for i in range(TT):
                    last = nc.tensor.transpose(chip.ps[:, (1 + k % 3) * 2 * HALF + i * P:(1 + k % 3) * 2 * HALF + (i + 1) * P],
                                               x_raw[:, i, k * P:(k + 1) * P], chip.ident[:, :])
                last.then_inc(turned, 1)
            norm.tensor(pe)

        @block.scalar
        def _(act):
            for k in range(KT):
                act.wait_ge(turned, k + 1)
                nc.scalar.activation(xT[:, k, :], chip.pair(1 + k % 3), ACT.Copy).then_inc(xT_ready, 1)
            norm.scalar(act, xT_ready)

        @block.vector
        def _(dve):
            dve.wait_ge(xT_ready, KT)
            norm.vector(dve)


def norm_buffers(chip, tag):
    return (chip.at(f"{tag}_squares", 168, [P, 2, SEQ]), chip.at(f"{tag}_root", 176, [P, SEQ]),
            chip.at(f"{tag}_scaled", 184, [P, 2, SEQ]))


def norm_block(chip, tag, xT, gain, x_hi, x_lo, prefetch, spill=None):
    nc = chip.nc
    squares, root, scaled = norm_buffers(chip, tag)
    norm = FeatureNorm(chip, tag, xT, KT, gain, x_hi, x_lo, squares, root, scaled)
    spilled = chip.sem(f"{tag}_spilled")
    with nc.Block() as block:
        @block.sync
        def _(sp):
            prefetch(sp)
            if spill is not None:
                sp.dma_start(spill, xT[:]).then_inc(spilled, 16)
                sp.wait_ge(spilled, 16)

        @block.tensor
        def _(pe):
            norm.tensor(pe)

        @block.scalar
        def _(act):
            norm.scalar(act)

        @block.vector
        def _(dve):
            norm.vector(dve)


class Ffn:
    STEPS = FFN // (2 * P)

    def __init__(self, chip, tag, w_gate, w_up, w_down, xT, x_hi, x_lo):
        self.chip, self.nc, self.xT, self.x_hi, self.x_lo = chip, chip.nc, xT, x_hi, x_lo
        self.w_in = (w_gate, w_up)
        self.w_down = w_down
        self.wgu = [[[chip.at(f"{tag}_w{m}{s}{hl}", 96 + 16 * s + 8 * m + 4 * hl, [P, KT, P], F32R) for hl in range(2)]
                     for m in range(2)] for s in range(2)]
        self.wd = [chip.at(f"{tag}_wd{hl}", 128 + 8 * hl, [P, 2, D], F32R) for hl in range(2)]
        self.gu_raw = [chip.at(f"{tag}_gu_raw{m}", 144 + 8 * m, [P, KT, 2 * P]) for m in range(2)]
        self.d_raw = chip.at(f"{tag}_d_raw", 160, [P, 2, D])
        self.h = [[chip.at(f"{tag}_h{g}{hl}", 168 + 16 * g + 8 * hl, [P, 2, SEQ], F32R) for hl in range(2)]
                  for g in range(2)]
        self.silu = chip.at(f"{tag}_silu", 200, [P, SEQ])
        self.gu_loaded, self.d_loaded = chip.sem(f"{tag}_gu_loaded"), chip.sem(f"{tag}_d_loaded")
        self.gu_hi, self.gu_ready = chip.sem(f"{tag}_gu_hi"), chip.sem(f"{tag}_gu_ready")
        self.d_hi, self.d_ready = chip.sem(f"{tag}_d_hi"), chip.sem(f"{tag}_d_ready")
        self.gate_done, self.up_done = chip.sem(f"{tag}_gate_done"), chip.sem(f"{tag}_up_done")
        self.silu_done, self.h_made = chip.sem(f"{tag}_silu_done"), chip.sem(f"{tag}_h_made")
        self.h_hi, self.h_ready = chip.sem(f"{tag}_h_hi"), chip.sem(f"{tag}_h_ready")
        self.d_done, self.y_added = chip.sem(f"{tag}_d_done"), chip.sem(f"{tag}_y_added")

    def load_gu(self, sp, g):
        for m in range(2):
            sp.dma_start(self.gu_raw[m][:], self.w_in[m].rearrange("(k p) f -> p k f", p=P)[:, :, ds(g * 2 * P, 2 * P)]
                         ).then_inc(self.gu_loaded, 16)

    def load_d(self, sp, g):
        sp.dma_start(self.d_raw[:], self.w_down[ds(g * 2 * P, 2 * P), :].rearrange("(a p) d -> p a d", p=P)
                     ).then_inc(self.d_loaded, 16)

    def prefetch(self, sp):
        self.load_gu(sp, 0)
        self.load_d(sp, 0)

    def loop(self, eng, step):
        step(0, 0)
        step(1, 1)
        with by_two(eng, 2, self.STEPS - 1) as g:
            step(g, 0)
            step(g + 1, 1)
        step(self.STEPS - 1, 0)
        step(self.STEPS, 1)

    def run(self):
        nc, chip, STEPS = self.nc, self.chip, self.STEPS
        x_hi, x_lo, xT = self.x_hi, self.x_lo, self.xT

        def at_first(g):
            return isinstance(g, int) and g == 0

        def is_tail(g):
            return isinstance(g, int) and g == STEPS

        def has_next(g):
            return not (isinstance(g, int) and g >= STEPS - 1)

        with nc.Block() as block:
            @block.sync
            def _(sp):
                def step(g, slot):
                    if has_next(g):
                        sp.wait_ge(self.gu_ready, 4 * (g + 1))
                        self.load_gu(sp, g + 1)
                        sp.wait_ge(self.d_ready, 2 * (g + 1))
                        self.load_d(sp, g + 1)
                self.loop(sp, step)

            @block.tensor
            def _(pe):
                def gate_up(g, s):
                    n = 2 * g + s
                    for m in range(2):
                        pe.wait_ge(self.gu_ready, 4 * g + 2 * s + m + 1)
                        if not (at_first(g) and s == 0):
                            pe.wait_ge((self.silu_done, self.h_made)[m], n)
                        for k in range(KT):
                            last = three_pass(nc, [chip.bank(2 * m), chip.bank(2 * m + 1)], self.wgu[s][m][0][:, k, :],
                                              self.wgu[s][m][1][:, k, :], halves(x_hi, k), halves(x_lo, k),
                                              k == 0, k == KT - 1)
                        last.then_inc((self.gate_done, self.up_done)[m], 1)

                def down(g, slot, part):
                    h_hi, h_lo = self.h[slot]
                    if part == 0:
                        pe.wait_ge(self.d_ready, 2 * (g + 1))
                        pe.wait_ge(self.h_ready, 2 * (g + 1))
                    for d in range(4 * part, 4 * part + 4):
                        if not (isinstance(g, int) and g == 0 and d < 2):
                            pe.wait_ge(self.y_added, KT * g + d - 1)
                        for a in range(2):
                            last = three_pass(nc, [chip.bank(4 + 2 * (d % 2)), chip.bank(5 + 2 * (d % 2))],
                                              self.wd[0][:, a, d * P:(d + 1) * P], self.wd[1][:, a, d * P:(d + 1) * P],
                                              halves(h_hi, a), halves(h_lo, a), a == 0, a == 1)
                        last.then_inc(self.d_done, 1)

                def step(g, slot):
                    if not is_tail(g):
                        gate_up(g, 0)
                    if not at_first(g):
                        down(g - 1, 1 - slot, 0)
                    if not is_tail(g):
                        gate_up(g, 1)
                    if not at_first(g):
                        down(g - 1, 1 - slot, 1)
                self.loop(pe, step)

            @block.scalar
            def _(act):
                def round_gu(g, s):
                    for m in range(2):
                        if m == 0 and s == 0:
                            act.wait_ge(self.gu_loaded, 32 * (g + 1))
                        if m == 0 and not at_first(g):
                            act.wait_ge(self.up_done, 2 * (g - 1) + s + 1)
                        nc.scalar.activation(self.wgu[s][m][0][:, :, :], self.gu_raw[m][:, :, s * P:(s + 1) * P],
                                             ACT.Copy).then_inc(self.gu_hi, 1)

                def round_d(g):
                    act.wait_ge(self.d_loaded, 16 * (g + 1))
                    if not at_first(g):
                        act.wait_ge(self.d_done, KT * g)
                    for a in range(2):
                        nc.scalar.activation(self.wd[0][:, a, :], self.d_raw[:, a, :], ACT.Copy).then_inc(self.d_hi, 1)

                def hidden(g, s, slot):
                    n = 2 * g + s
                    act.wait_ge(self.gate_done, n + 1)
                    if not (at_first(g) and s == 0):
                        act.wait_ge(self.h_ready, n)
                    nc.scalar.activation(self.silu[:, :], chip.pair(0), ACT.Silu).then_inc(self.silu_done, 1)
                    act.wait_ge(self.h_made, n + 1)
                    if not isinstance(g, int) or g >= 2:
                        act.wait_ge(self.d_done, KT * (g - 1))
                    nc.scalar.activation(self.h[slot][0][:, s, :], self.silu[:, :], ACT.Copy).then_inc(self.h_hi, 1)

                round_gu(0, 0)
                round_gu(0, 1)

                def step(g, slot):
                    if not at_first(g):
                        round_d(g - 1)
                    if is_tail(g):
                        return
                    for s in range(2):
                        hidden(g, s, slot)
                        if has_next(g):
                            round_gu(g + 1, s)
                self.loop(act, step)

            @block.vector
            def _(dve):
                def rest_gu(g, s):
                    for m in range(2):
                        dve.wait_ge(self.gu_hi, 4 * g + 2 * s + m + 1)
                        nc.vector.tensor_tensor(self.wgu[s][m][1][:, :, :], self.gu_raw[m][:, :, s * P:(s + 1) * P],
                                                self.wgu[s][m][0][:, :, :].bitcast(F32), ALU.subtract).then_inc(self.gu_ready, 1)

                def rest_d(g):
                    for a in range(2):
                        dve.wait_ge(self.d_hi, 2 * g + a + 1)
                        nc.vector.tensor_tensor(self.wd[1][:, a, :], self.d_raw[:, a, :], self.wd[0][:, a, :].bitcast(F32),
                                                ALU.subtract).then_inc(self.d_ready, 1)

                def add(g, d):
                    dve.wait_ge(self.d_done, KT * g + d + 1)
                    if not (isinstance(g, int) and g == 0):
                        dve.wait_ge(self.y_added, KT * g + d + 1 - KT)
                    nc.vector.scalar_tensor_tensor(out=xT[:, d, :], in0=chip.pair(2 + d % 2), scalar=0.5,
                                                   in1=xT[:, d, :], op0=ALU.mult, op1=ALU.add).then_inc(self.y_added, 1)

                def make_h(g, s):
                    n = 2 * g + s
                    dve.wait_ge(self.up_done, n + 1)
                    dve.wait_ge(self.silu_done, n + 1)
                    nc.vector.tensor_tensor(self.silu[:, :], self.silu[:, :], chip.pair(1), ALU.mult).then_inc(self.h_made, 1)

                def rest_h(g, s, slot):
                    n = 2 * g + s
                    dve.wait_ge(self.h_made, n + 1)
                    dve.wait_ge(self.h_hi, n + 1)
                    nc.vector.tensor_tensor(self.h[slot][1][:, s, :], self.silu[:, :],
                                            self.h[slot][0][:, s, :].bitcast(F32), ALU.subtract).then_inc(self.h_ready, 1)

                rest_gu(0, 0)
                rest_gu(0, 1)

                def step(g, slot):
                    if not at_first(g):
                        rest_d(g - 1)
                    for s in range(2):
                        if not is_tail(g):
                            make_h(g, s)
                        if not at_first(g):
                            add(g - 1, 4 * s)
                        if not is_tail(g):
                            rest_h(g, s, slot)
                        if not at_first(g):
                            add(g - 1, 4 * s + 1)
                        if has_next(g):
                            rest_gu(g + 1, s)
                        if not at_first(g):
                            add(g - 1, 4 * s + 2)
                            add(g - 1, 4 * s + 3)
                self.loop(dve, step)


class ColumnWeights:

    def __init__(self, chip, tag, weights, raw_kb, split_kb):
        self.chip, self.nc, self.weights = chip, chip.nc, weights
        self.raw = [chip.at(f"{tag}_raw{s}", raw_kb + 4 * s, [P, KT, P]) for s in range(2)]
        self.split = [[chip.at(f"{tag}_split{s}{hl}", split_kb + 8 * s + 4 * hl, [P, KT, P], F32R) for hl in range(2)]
                      for s in range(2)]
        self.loaded = [chip.sem(f"{tag}_loaded{s}") for s in range(2)]
        self.hi, self.ready, self.used = chip.sem(f"{tag}_hi"), chip.sem(f"{tag}_ready"), chip.sem(f"{tag}_used")

    def load(self, sp, n, slot, col, cols=P):
        sp.dma_start(self.raw[slot][:, :, 0:cols],
                     self.weights.rearrange("(k p) c -> p k c", p=P)[:, :, ds(col, cols)]).then_inc(self.loaded[slot], 16)

    def round(self, act, n, slot, cols=P):
        act.wait_ge(self.loaded[slot], 8 * (n - slot) + 16)
        if not isinstance(n, int) or n >= 2:
            act.wait_ge(self.used, n - 1)
        self.nc.scalar.activation(self.split[slot][0][:, :, 0:cols], self.raw[slot][:, :, 0:cols], ACT.Copy).then_inc(self.hi, 1)

    def rest(self, dve, n, slot, cols=P):
        dve.wait_ge(self.hi, n + 1)
        self.nc.vector.tensor_tensor(self.split[slot][1][:, :, 0:cols], self.raw[slot][:, :, 0:cols],
                                     self.split[slot][0][:, :, 0:cols].bitcast(F32), ALU.subtract).then_inc(self.ready, 1)

    def product(self, pe, n, slot, outs, x_hi, x_lo, done, cols=P):
        pe.wait_ge(self.ready, n + 1)
        for k in range(KT):
            last = three_pass(self.nc, outs, self.split[slot][0][:, k, 0:cols], self.split[slot][1][:, k, 0:cols],
                              halves(x_hi, k), halves(x_lo, k), k == 0, k == KT - 1)
        last.then_inc(self.used, 1)


HEAD_TILES = 4
HY_TILES = 3 * C // P


def mixer_in_block(chip, w, x_hi, x_lo, cq, ckv, kr, v_hi, v_lo, gates, conv_w, conv_b):
    nc = chip.nc
    padded = [chip.at(f"m_padded{s}", 168 + 4.25 * s, [P, SEQ + 2]) for s in range(2)]
    conv = [chip.at(f"m_conv{s}", 177 + 4 * s, [P, SEQ]) for s in range(2)]
    s = chip.sem
    evacuated, pads, conv_step = s("m_evacuated"), s("m_pads"), s("m_conv_step")
    turned, v_rounded, settled = s("m_turned"), s("m_v_rounded"), s("m_settled")
    HY0 = HEAD_TILES
    N = HEAD_TILES + HY_TILES

    def col(n):
        return n * P if n < 3 else Q_RANK + KV_RANK

    with nc.Block() as block:
        @block.sync
        def _(sp):
            for n in range(2, HEAD_TILES):
                sp.wait_ge(w.ready, n - 1)
                w.load(sp, n, n % 2, col(n), ROPE if n == 3 else P)
            with by_two(sp, 0, HY_TILES) as j:
                for a in range(2):
                    sp.wait_ge(w.ready, HY0 + j + a - 1)
                    w.load(sp, HY0 + j + a, a, (j + a) * P + (Q_RANK + KV_RANK + ROPE))

        @block.tensor
        def _(pe):
            for n in range(HEAD_TILES):
                cols = ROPE if n == 3 else P
                if n >= 2:
                    pe.wait_ge(evacuated, n - 1)
                w.product(pe, n, n % 2, [chip.bank(2 * (n % 2), cols), chip.bank(2 * (n % 2) + 1, cols)],
                          x_hi, x_lo, None, cols)

            def product(j, slot):
                pe.wait_ge(evacuated, HY0 + j - 1)
                w.product(pe, HY0 + j, slot, [chip.bank(2 * slot), chip.bank(2 * slot + 1)], x_hi, x_lo, None)

            def turn(j, slot):
                pe.wait_ge(conv_step, 3 * (j + 1))
                if not isinstance(j, int) or j >= 2:
                    pe.wait_ge(settled, j - 1)
                for i in range(TT):
                    start = (i // 4) + 2 * P * (i % 4)
                    at = (2 + slot) * 2 * HALF + i * P
                    last = nc.tensor.transpose(chip.ps[:, at:at + P], conv[slot][:, start:start + 2 * P - 1:2],
                                               chip.ident[:, :])
                last.then_inc(turned, 1)

            product(0, 0)
            for j in range(1, 4):
                product(j, j % 2)
                turn(j - 1, (j - 1) % 2)
            with by_two(pe, 4, HY_TILES) as j:
                product(j, 0)
                turn(j - 1, 1)
                product(j + 1, 1)
                turn(j, 0)
            turn(HY_TILES - 1, 1)

        @block.scalar
        def _(act):
            w.round(act, 0, 0)
            for n in range(HEAD_TILES):
                w.round(act, n + 1, (n + 1) % 2, ROPE if n + 1 == 3 else P)
                act.wait_ge(w.used, n + 1)
                dst = (cq[:, 0, :], cq[:, 1, :], ckv[:, 0, :], kr[NOPE:QK, :])[n]
                rows = ROPE if n == 3 else P
                nc.scalar.activation(dst, chip.pair(n % 2, rows), ACT.Copy).then_inc(evacuated, 1)
            act.wait_ge(pads, 4)

            def column(j, slot):
                act.wait_ge(w.used, HY0 + j + 1)
                if not isinstance(j, int) or j >= 2:
                    act.wait_ge(conv_step, 3 * (j - 1))
                nc.scalar.activation(padded[slot][:, 1:SEQ + 1], chip.pair(slot), ACT.Copy).then_inc(evacuated, 1)

            def round_v(j, slot):
                act.wait_ge(turned, j + 1)
                nc.scalar.activation(v_hi[:, :, j * P:(j + 1) * P], chip.pair(2 + slot).rearrange("p (i c) -> p i c", i=TT),
                                     ACT.Copy).then_inc(v_rounded, 1)

            for j in range(C // P + 2):
                w.round(act, HY0 + j + 1, 1 - j % 2)
                column(j, j % 2)
                if 1 <= j <= C // P:
                    round_v(j - 1, (j - 1) % 2)
            with by_two(act, C // P + 2, HY_TILES - 2) as j:
                w.round(act, HY0 + j + 1, 1)
                column(j, 0)
                w.round(act, HY0 + j + 2, 0)
                column(j + 1, 1)
            w.round(act, N - 1, 1)
            column(HY_TILES - 2, 0)
            column(HY_TILES - 1, 1)

        @block.vector
        def _(dve):
            for k in range(2):
                nc.vector.memset(padded[k][:, 0:1], 0.0).then_inc(pads, 1)
                nc.vector.memset(padded[k][:, SEQ + 1:SEQ + 2], 0.0).then_inc(pads, 1)
            w.rest(dve, 0, 0)
            for n in range(HEAD_TILES):
                w.rest(dve, n + 1, (n + 1) % 2, ROPE if n + 1 == 3 else P)
            dve.wait_ge(pads, 4)

            def convolve(j, slot):
                dve.wait_ge(evacuated, HY0 + j + 1)
                if not isinstance(j, int) or j >= 2:
                    dve.wait_ge(turned, j - 1)
                taps = [conv_w[:, tap, ds(j, 1)] for tap in range(3)]
                nc.vector.tensor_scalar(conv[slot][:, :], padded[slot][:, 0:SEQ], taps[0], conv_b[:, ds(j, 1)],
                                        ALU.mult, ALU.add).then_inc(conv_step, 1)
                for tap in (1, 2):
                    dve.wait_ge(conv_step, 3 * j + tap)
                    nc.vector.scalar_tensor_tensor(out=conv[slot][:, :], in0=padded[slot][:, tap:tap + SEQ],
                                                   scalar=taps[tap], in1=conv[slot][:, :], op0=ALU.mult,
                                                   op1=ALU.add).then_inc(conv_step, 1)

            def tokens(slot):
                return chip.pair(2 + slot).rearrange("p (i c) -> p i c", i=TT)

            def v_low(j, slot):
                dve.wait_ge(v_rounded, j + 1)
                nc.vector.tensor_tensor(v_lo[:, :, ds(j * P, P)], tokens(slot),
                                        v_hi[:, :, ds(j * P, P)].bitcast(F32), ALU.subtract).then_inc(settled, 1)

            def gate(j, slot, dst):
                dve.wait_ge(turned, j + 1)
                nc.vector.tensor_copy(dst, tokens(slot)).then_inc(settled, 1)

            def step(group, k, slot):
                j = group * (C // P) + k
                if not (isinstance(j, int) and j >= HY_TILES - 2):
                    w.rest(dve, HY0 + j + 2, slot)
                if not (isinstance(j, int) and j == HY_TILES - 1):
                    convolve(j + 1, 1 - slot)
                if group == 0:
                    v_low(j, slot)
                else:
                    gate(j, slot, gates[group - 1][:, :, ds(k * P, P)])

            w.rest(dve, HY0 + 1, 1)
            convolve(0, 0)
            for k in range(C // P):
                step(0, k, k % 2)
            with by_two(dve, 0, C // P) as k:
                step(1, k, 0)
                step(1, k + 1, 1)
            for k in range(C // P):
                step(2, k, k % 2)


def hyena_block(chip, dram, v_hi, v_lo, gates):
    nc = chip.nc
    spec_hi = chip.at("y_spec_hi", 32, [P, 4, WT, C], F32R)
    spec_lo = chip.at("y_spec_lo", 64, [P, 4, WT, C], F32R)
    table = [chip.at(f"y_table{k}", 144 + 8 * k, [P, TT // 2, 2, 2, P], F32R) for k in range(2)]
    filt = [chip.at(f"y_filt{k}", 160 + 8 * k, [P, 4, C]) for k in range(2)]
    even = chip.at("y_even", 176, [P, 2, C])
    work = chip.at("y_work", 180, [P, 8, C])
    z = chip.at("y_z", 196, [P, 2, C])
    s = chip.sem
    table_loaded = [s(f"y_table_loaded{k}") for k in range(2)]
    filt_loaded = [s(f"y_filt_loaded{k}") for k in range(2)]
    table_used, even_copied, work_step = s("y_table_used"), s("y_even_copied"), s("y_work_step")
    spec_hi_ready, spec_lo_ready = s("y_spec_hi_ready"), s("y_spec_lo_ready")
    z_made, z_hi, z_lo = s("y_z_made"), s("y_z_hi"), s("y_z_lo")
    UNITS = 2 * WT
    STEPS = 12

    with nc.Block() as block:
        @block.sync
        def _(sp):
            for q in range(2):
                u0 = (UNITS + TT) * q

                def unit(u, slot, src, row, first=False):
                    if not first:
                        sp.wait_ge(table_used, u - 1)
                    sp.dma_start(table[slot][:].bitcast(F32), src[ds(row, P), :]).then_inc(table_loaded[slot], 16)

                def filter_tile(wt, slot, q=q):
                    if q or not isinstance(wt, int):
                        sp.wait_ge(work_step, STEPS * (WT * q + wt - 1))
                    sp.dma_start(filt[slot][:], dram["spectra"][ds((WT * q + wt) * P, P), :]).then_inc(filt_loaded[slot], 16)

                unit(u0, 0, dram["fwd"], 0, q == 0)
                unit(u0 + 1, 1, dram["fwd"], P, q == 0)
                filter_tile(0, 0)
                filter_tile(1, 1)
                unit(u0 + 2, 0, dram["fwd"], 2 * P)
                unit(u0 + 3, 1, dram["fwd"], 3 * P)
                with by_two(sp, 2, WT) as wt:
                    for a in range(2):
                        unit(u0 + 2 * wt + 2 * a, 0, dram["fwd"], (2 * wt + 2 * a) * P)
                        unit(u0 + 2 * wt + 2 * a + 1, 1, dram["fwd"], (2 * wt + 2 * a + 1) * P)
                        filter_tile(wt + a, a)
                with by_two(sp, 0, TT) as i:
                    unit(u0 + UNITS + i, 0, dram["inv"], i * P)
                    unit(u0 + UNITS + i + 1, 1, dram["inv"], (i + 1) * P)

        @block.tensor
        def _(pe):
            for q in range(2):
                u0 = (UNITS + TT) * q
                if q:
                    pe.wait_ge(z_lo, TT)

                def forward(wt, q=q, u0=u0):
                    for r in range(2):
                        pe.wait_ge(table_loaded[r], 8 * (u0 + 2 * wt) + 16)
                        if q or not isinstance(wt, int):
                            if r == 0:
                                pe.wait_ge(even_copied, WT * q + wt)
                            else:
                                pe.wait_ge(work_step, STEPS * (WT * q + wt))
                        for tt in range(TT // 2):
                            i = r * (TT // 2) + tt
                            for cs in range(2):
                                last = three_pass(nc, [chip.bank(2 * r + cs)], table[r][:, tt, cs, 0, :],
                                                  table[r][:, tt, cs, 1, :], [v_hi[:, i, :]], [v_lo[:, i, :]],
                                                  tt == 0, tt == TT // 2 - 1)
                        last.then_inc(table_used, 1)

                forward(0)
                with pe.Fori(1, WT) as wt:
                    forward(wt)

                for r in range(2):
                    for tt in range(TT // 2):
                        i = r * (TT // 2) + tt
                        pe.wait_ge(table_loaded[tt % 2], 16 * ((u0 + UNITS + i) // 2 + 1))
                        if q or i >= 4:
                            pe.wait_ge(z_made, TT * q + i - 3)
                        for wt in range(WT):
                            if i == 0:
                                pe.wait_ge(spec_lo_ready, 2 * (WT * q + wt + 1))
                            for cs in range(2):
                                kind = r + 2 * (1 - cs)
                                last = three_pass(nc, [chip.bank(4 + tt)], table[tt % 2][:, wt, cs, 0, :],
                                                  table[tt % 2][:, wt, cs, 1, :], [spec_hi[:, kind, wt, :]],
                                                  [spec_lo[:, kind, wt, :]], wt == 0 and cs == 0,
                                                  wt == WT - 1 and cs == 1)
                        last.then_inc(table_used, 1)

        @block.scalar
        def _(act):
            for q in range(2):
                u0 = (UNITS + TT) * q

                def tile(wt, q=q, u0=u0):
                    n = WT * q + wt
                    act.wait_ge(table_used, u0 + 2 * wt + 1)
                    if q or not isinstance(wt, int):
                        act.wait_ge(work_step, STEPS * n)
                    nc.scalar.activation(even[:, :, :], chip.pair(0).rearrange("p (a c) -> p a c", a=2),
                                         ACT.Copy).then_inc(even_copied, 1)
                    if q and isinstance(wt, int):
                        act.wait_ge(table_used, UNITS + TT)
                    for part in range(2):
                        act.wait_ge(work_step, STEPS * n + 10 + 2 * part)
                        nc.scalar.activation(spec_hi[:, 2 * part:2 * part + 2, ds(wt, 1), :].rearrange("p a b c -> p a (b c)"),
                                             work[:, 4 * part + 1:4 * part + 4:2, :], ACT.Copy).then_inc(spec_hi_ready, 1)
                tile(0)
                with act.Fori(1, WT) as wt:
                    tile(wt)
                if q == 0:
                    act.wait_ge(table_used, UNITS)
                    with by_two(act, 0, TT) as i:
                        for slot in range(2):
                            act.wait_ge(z_made, i + slot + 1)
                            nc.scalar.activation(v_hi[:, ds(i + slot, 1), :].rearrange("p a c -> p (a c)"),
                                                 z[:, slot, :], ACT.Copy).then_inc(z_hi, 1)

        @block.vector
        def _(dve):
            for q in range(2):
                u0 = (UNITS + TT) * q

                def op(n, k, out, in0, in1, alu, inc=True):
                    nc.vector.tensor_tensor(out, in0, in1, alu).then_inc(work_step, 1)

                def tile(wt, slot, q=q, u0=u0):
                    n = WT * q + wt
                    at = STEPS * n
                    f = filt[slot]
                    dve.wait_ge(even_copied, n + 1)
                    dve.wait_ge(table_used, u0 + 2 * wt + 2)
                    dve.wait_ge(filt_loaded[slot], 8 * (n - slot) + 16)
                    if q or not isinstance(wt, int) or wt:
                        dve.wait_ge(spec_lo_ready, 2 * n)
                        dve.wait_ge(spec_hi_ready, 2 * n)
                    odd = chip.pair(1).rearrange("p (a c) -> p a c", a=2)
                    op(n, 0, work[:, 0:2, :], even[:, :, :], odd, ALU.add)
                    op(n, 1, work[:, 2, :], even[:, 0, :], chip.bank(2), ALU.subtract)
                    op(n, 2, work[:, 3, :], chip.bank(3), even[:, 1, :], ALU.subtract)
                    dve.wait_ge(work_step, at + 3)
                    op(n, 3, work[:, 4:8, :], work[:, 0:4, :], f[:, :, :], ALU.mult)
                    dve.wait_ge(work_step, at + 4)
                    op(n, 4, work[:, 0:3:2, :], work[:, 0:3:2, :], f[:, 1:4:2, :], ALU.mult)
                    op(n, 5, work[:, 1:4:2, :], work[:, 1:4:2, :], f[:, 0:3:2, :], ALU.mult)
                    dve.wait_ge(work_step, at + 6)
                    op(n, 6, work[:, 0:3:2, :], work[:, 0:3:2, :], work[:, 1:4:2, :], ALU.add)
                    op(n, 7, work[:, 4:7:2, :], work[:, 4:7:2, :], work[:, 5:8:2, :], ALU.subtract)
                    dve.wait_ge(work_step, at + 8)
                    op(n, 8, work[:, 1, :], work[:, 0, :], work[:, 2, :], ALU.subtract)
                    op(n, 9, work[:, 3, :], work[:, 0, :], work[:, 2, :], ALU.add)
                    op(n, 10, work[:, 5, :], work[:, 4, :], work[:, 6, :], ALU.add)
                    op(n, 11, work[:, 7, :], work[:, 4, :], work[:, 6, :], ALU.subtract)
                    dve.wait_ge(work_step, at + 12)
                    for part in range(2):
                        dve.wait_ge(spec_hi_ready, 2 * n + part + 1)
                        views = [t[:, 2 * part:2 * part + 2, ds(wt, 1), :].rearrange("p a b c -> p a (b c)")
                                 for t in (spec_lo, spec_hi)]
                        nc.vector.tensor_tensor(views[0], work[:, 4 * part + 1:4 * part + 4:2, :], views[1].bitcast(F32),
                                                ALU.subtract).then_inc(spec_lo_ready, 1)

                tile(0, 0)
                tile(1, 1)
                with by_two(dve, 2, WT) as wt:
                    tile(wt, 0)
                    tile(wt + 1, 1)

                for i in range(TT):
                    dve.wait_ge(table_used, u0 + UNITS + i + 1)
                    if q == 0:
                        if i >= 2:
                            dve.wait_ge(z_hi, i - 1)
                            dve.wait_ge(z_lo, i - 1)
                        nc.vector.tensor_tensor(z[:, i % 2, :], chip.bank(4 + i % 4), gates[0][:, i, :],
                                                ALU.mult).then_inc(z_made, 1)
                        if i >= 1:
                            dve.wait_ge(z_hi, i)
                            nc.vector.tensor_tensor(v_lo[:, i - 1, :], z[:, (i - 1) % 2, :], v_hi[:, i - 1, :].bitcast(F32),
                                                    ALU.subtract).then_inc(z_lo, 1)
                        if i == TT - 1:
                            dve.wait_ge(z_made, TT)
                            dve.wait_ge(z_hi, TT)
                            nc.vector.tensor_tensor(v_lo[:, i, :], z[:, i % 2, :], v_hi[:, i, :].bitcast(F32),
                                                    ALU.subtract).then_inc(z_lo, 1)
                    else:
                        nc.vector.tensor_tensor(gates[1][:, i, :], chip.bank(4 + i % 4), gates[1][:, i, :],
                                                ALU.mult).then_inc(z_made, 1)


def attention_block(chip, dram, cq, ckv, kr, attn):
    nc = chip.nc
    cq_hi, cq_lo = (chip.at(f"a_cq{h}", 8 * h, [P, 2, SEQ], F32R) for h in range(2))
    ckv_hi, ckv_lo = (chip.at(f"a_ckv{h}", 16 + 4 * h, [P, 1, SEQ], F32R) for h in range(2))
    v_all = chip.at("a_v_all", 24, [P, TT, HEADS * VD])
    v_head = [[chip.at(f"a_v{k}{h}", 40 + 4.5 * k + 2.25 * h, [P, TT, VD + 1], F32R) for h in range(2)] for k in range(2)]
    q_head = [[chip.at(f"a_q{k}{h}", 49 + 8 * k + 4 * h, [QK, SEQ], F32R) for h in range(2)] for k in range(2)]
    k_head = [[chip.at(f"a_k{k}{h}", 65 + 8 * k + 4 * h, [QK, SEQ], F32R) for h in range(2)] for k in range(2)]
    q_row = chip.at("a_q_row", 81, [QK, SEQ])
    swapped = chip.at("a_swapped", 85, [QK, SEQ])
    probs = [chip.at(f"a_probs{k}", 89 + 4 * k, [P, SEQ]) for k in range(2)]
    wq_raw = [chip.at(f"a_wq_raw{k}", 97 + 0.75 * k, [P, 2, QK]) for k in range(2)]
    wk_raw = [chip.at(f"a_wk_raw{k}", 98.5 + 0.25 * k, [P, NOPE]) for k in range(2)]
    wq = [[chip.at(f"a_wq{k}{h}", 99 + 1.5 * k + 0.75 * h, [P, 2, QK], F32R) for h in range(2)] for k in range(2)]
    wk = [[chip.at(f"a_wk{k}{h}", 102 + 0.5 * k + 0.25 * h, [P, NOPE], F32R) for h in range(2)] for k in range(2)]
    wv_raw = chip.at("a_wv_raw", 103, [P, HEADS * VD])
    wv = [chip.at(f"a_wv{h}", 105 + 2 * h, [P, HEADS * VD], F32R) for h in range(2)]
    out_t = [chip.at(f"a_out_t{k}", 109 + k, [VD + 1, 2 * P]) for k in range(2)]
    pt = [[chip.at(f"a_pt{k}{h}", 144 + 16 * k + 8 * h, [P, TT, 2 * P], F32R) for h in range(2)] for k in range(2)]
    cos_row = chip.at("a_cos_row", 176, [QK, SEQ])
    sin_row = chip.at("a_sin_row", 180, [QK, SEQ])
    squares, root, scaled = (chip.at("a_squares", 144, [P, 2, SEQ]), chip.at("a_root", 152, [P, SEQ]),
                             chip.at("a_scaled", 156, [P, 2, SEQ]))
    squares2, root2, scaled2 = (chip.at("a_squares2", 164, [P, 2, SEQ]), chip.at("a_root2", 172, [P, SEQ]),
                                chip.at("a_scaled2", 89, [P, 2, SEQ]))
    q_norm = FeatureNorm(chip, "aq", cq, Q_RANK // P, chip.q_gain, cq_hi, cq_lo, squares, root, scaled, 0)
    kv_norm = FeatureNorm(chip, "akv", ckv, KV_RANK // P, chip.kv_gain, ckv_hi, ckv_lo, squares2, root2, scaled2, 1)

    s = chip.sem
    ropes_loaded, wv_loaded, k_swapped = s("a_ropes_loaded"), s("a_wv_loaded"), s("a_k_swapped")
    w_loaded = [s(f"a_w_loaded{k}") for k in range(2)]
    wv_hi, wv_ready, v_out, v_stored = s("a_wv_hi"), s("a_wv_ready"), s("a_v_out"), s("a_v_stored")
    k_rope_step, rope_hi, rope_ready, ones_set = (s("a_k_rope_step"), s("a_rope_hi"), s("a_rope_ready"), s("a_ones_set"))
    w_hi, w_ready = s("a_w_hi"), s("a_w_ready")
    q_out, k_out = s("a_q_out"), s("a_k_out")
    q_rowed, q_swapped, q_roped = s("a_q_rowed"), s("a_q_swapped"), s("a_q_roped")
    q_hi, q_ready, k_hi, k_ready, v_hi, v_ready = (s("a_q_hi"), s("a_q_ready"), s("a_k_hi"), s("a_k_ready"),
                                                   s("a_v_hi"), s("a_v_ready"))
    scored, negmax, exped = s("a_scored"), s("a_negmax"), s("a_exped")
    maxed = s("a_maxed")
    turned, pt_hi, pt_ready = s("a_turned"), s("a_pt_hi"), s("a_pt_ready")
    weighted, out_copied, out_turned, out_stored = (s("a_weighted"), s("a_out_copied"), s("a_out_turned"),
                                                    s("a_out_stored"))
    R = slice(NOPE, QK)
    SCALE = QK ** -0.5

    def peeled(eng, step):
        step(0, 0)
        with by_two(eng, 1, HEADS - 1) as h:
            step(h, 1)
            step(h + 1, 0)
        step(HEADS - 1, 1)

    def is_last(h):
        return isinstance(h, int) and h == HEADS - 1

    def is_first(h):
        return isinstance(h, int) and h == 0

    with nc.Block() as block:
        @block.sync
        def _(sp):
            sp.dma_start(swapped[NOPE:NOPE + 16, :], kr[NOPE + 16:QK, :]).then_inc(k_swapped, 16)
            sp.dma_start(swapped[NOPE + 16:QK, :], kr[NOPE:NOPE + 16, :]).then_inc(k_swapped, 16)
            sp.dma_start(cos_row[R, :], dram["rope"][0:ROPE, :]).then_inc(ropes_loaded, 16)
            sp.dma_start(sin_row[R, :], dram["rope"][ROPE:2 * ROPE, :]).then_inc(ropes_loaded, 16)
            w_ukv = dram["w_ukv"].rearrange("k (h t d) -> k h t d", h=HEADS, t=2)
            sp.dma_start(wv_raw[:, :].rearrange("p (h d) -> p h d", h=HEADS), w_ukv[:, :, 1, :]).then_inc(wv_loaded, 16)

            def load(h, slot):
                sp.dma_start(wq_raw[slot][:], dram["w_uq"].rearrange("(k p) c -> p k c", p=P)[:, :, ds(h * QK, QK)]
                             ).then_inc(w_loaded[slot], 16)
                sp.dma_start(wk_raw[slot][:], dram["w_ukv"][:, ds(h * 2 * VD, NOPE)]).then_inc(w_loaded[slot], 16)

            def swap(h):
                sp.wait_ge(q_rowed, h + 1)
                if is_first(h):
                    sp.wait_ge(k_rope_step, 3)
                sp.dma_start(swapped[NOPE:NOPE + 16, :], q_row[NOPE + 16:QK, :]).then_inc(q_swapped, 16)
                sp.dma_start(swapped[NOPE + 16:QK, :], q_row[NOPE:NOPE + 16, :]).then_inc(q_swapped, 16)

            load(0, 0)
            load(1, 1)
            swap(0)

            def step(h, slot):
                if not (isinstance(h, int) and h >= HEADS - 2):
                    sp.wait_ge(w_ready, 2 * (h + 1))
                    load(h + 2, slot)
                if not is_last(h):
                    swap(h + 1)
            step(0, 0)
            with by_two(sp, 1, HEADS - 3) as h:
                step(h, 1)
                step(h + 1, 0)
            for h in range(HEADS - 3, HEADS):
                step(h, h % 2)

        @block.tensor
        def _(pe):
            q_norm.tensor(pe)
            kv_norm.tensor(pe)
            pe.wait_ge(wv_ready, 1)
            pe.wait_ge(kv_norm.lo_ready, 1)
            for i in range(TT):
                if i >= 4:
                    pe.wait_ge(v_stored, i - 3)
                tok = slice(i * P, (i + 1) * P)
                three_pass(nc, [chip.bank(4 + i % 4)], ckv_hi[:, 0, tok], ckv_lo[:, 0, tok], [wv[0][:, :]], [wv[1][:, :]],
                           True, True).then_inc(v_out, 1)
            pe.wait_ge(q_norm.lo_ready, 2)

            def project_q(h, slot, pair):
                pe.wait_ge(w_ready, 2 * h + 1)
                for k in range(2):
                    last = three_pass(nc, [chip.bank(2 * pair, QK), chip.bank(2 * pair + 1, QK)], wq[slot][0][:, k, :],
                                      wq[slot][1][:, k, :], halves(cq_hi, k), halves(cq_lo, k), k == 0, k == 1)
                last.then_inc(q_out, 1)

            def project_k(h, slot, pair):
                pe.wait_ge(w_ready, 2 * h + 2)
                three_pass(nc, [chip.bank(2 * pair, NOPE), chip.bank(2 * pair + 1, NOPE)], wk[slot][0][:, :],
                           wk[slot][1][:, :], halves(ckv_hi, 0), halves(ckv_lo, 0), True, True).then_inc(k_out, 1)

            def score(h, t, slot, pair):
                if is_first(h) and t == 0:
                    pe.wait_ge(rope_ready, 2)
                if t == 0:
                    pe.wait_ge(q_ready, h + 1)
                    pe.wait_ge(k_ready, h + 1)
                start = (t // 4) + 2 * P * (t % 4)
                tok = slice(start, start + 2 * P - 1, 2)
                q, k = q_head[slot], k_head[slot]
                three_pass(nc, [chip.bank(2 * pair), chip.bank(2 * pair + 1)], q[0][:, tok], q[1][:, tok],
                           [k[0][:, n * HALF:(n + 1) * HALF] for n in range(2)],
                           [k[1][:, n * HALF:(n + 1) * HALF] for n in range(2)], True, True).then_inc(scored, 1)

            def turn(h, t):
                g = TT * h + t
                pe.wait_ge(exped, g + 1)
                for half in range(2):
                    if not (is_first(h) and t == 0):
                        pe.wait_ge(pt_ready, 2 * g + half - 1)
                    for kt in range(4):
                        last = nc.tensor.transpose(chip.bank(4 + half)[:, kt * P:(kt + 1) * P],
                                                   probs[t % 2][:, (4 * half + kt) * P:(4 * half + kt + 1) * P],
                                                   chip.ident[:, :])
                    last.then_inc(turned, 1)

            def weigh(h, b, half, slot):
                blk = 4 * h + b
                if half == 0:
                    pe.wait_ge(pt_ready, 4 * (blk + 1))
                    if is_first(h) and b == 0:
                        pe.wait_ge(ones_set, 4)
                    if b == 0:
                        pe.wait_ge(v_ready, h + 1)
                    if not (is_first(h) and b < 2):
                        pe.wait_ge(out_stored, blk - 1)
                bank = chip.bank(6 + b % 2, VD + 1, 2 * P)
                for kt in range(4 * half, 4 * half + 4):
                    last = three_pass(nc, [bank], v_head[slot][0][:, kt, :], v_head[slot][1][:, kt, :],
                                      [pt[b % 2][0][:, kt, :]], [pt[b % 2][1][:, kt, :]], kt == 0, kt == TT - 1)
                if half == 1:
                    last.then_inc(weighted, 1)

            def turn_out(h, b):
                pe.wait_ge(out_copied, 4 * h + b + 1)
                for u in range(2):
                    at = (6 + b % 2) * HALF + 2 * P + (VD + 2) * u
                    last = nc.tensor.transpose(chip.ps[:, at:at + VD + 1], out_t[b % 2][:, u * P:(u + 1) * P],
                                               chip.ident[0:VD + 1, 0:VD + 1])
                last.then_inc(out_turned, 1)

            project_q(0, 0, 1)
            project_k(0, 0, 0)
            pe.wait_ge(q_rowed, 1)
            score(0, 0, 0, 1)

            def step(h, slot):
                for t in range(TT):
                    last_head = is_last(h)
                    if t < TT - 1 or not last_head:
                        nxt = (h, t + 1, slot) if t < TT - 1 else (h + 1, 0, 1 - slot)
                        if t + 1 == 1:
                            if is_first(h):
                                pe.wait_ge(k_ready, 1)
                            else:
                                pe.wait_ge(exped, TT * h)
                        elif t + 1 == 5 and not last_head:
                            pe.wait_ge(q_rowed, h + 2)
                        elif t + 1 == 6 and not last_head:
                            pe.wait_ge(k_ready, h + 2)
                        else:
                            pe.wait_ge(exped, TT * h + t)
                        score(*nxt, t % 2)
                    if t >= 4 and t % 2 == 0:
                        turn_out(h, t // 2 - 2)
                    elif t % 2 == 0 and not is_first(h):
                        turn_out(h - 1, t // 2 + 2)
                    turn(h, t)
                    if t >= 2:
                        weigh(h, t // 2 - 1, t % 2, slot)
                    elif not is_first(h):
                        weigh(h - 1, 3, t % 2, 1 - slot)
                    if t == 3 and not last_head:
                        pe.wait_ge(exped, TT * h + 4)
                        project_q(h + 1, 1 - slot, 0)
                    if t == 4 and not last_head:
                        pe.wait_ge(exped, TT * h + 5)
                        project_k(h + 1, 1 - slot, 1)

            peeled(pe, step)
            weigh(HEADS - 1, 3, 0, 1)
            weigh(HEADS - 1, 3, 1, 1)
            turn_out(HEADS - 1, 2)
            turn_out(HEADS - 1, 3)

        @block.gpsimd
        def _(pool):
            for k in range(2):
                nc.gpsimd.memset(v_head[k][0][:, :, VD:VD + 1].bitcast(F32), 1.0).then_inc(ones_set, 1)
                nc.gpsimd.memset(v_head[k][1][:, :, VD:VD + 1].bitcast(F32), 0.0).then_inc(ones_set, 1)

        @block.scalar
        def _(act):
            q_norm.scalar(act)
            kv_norm.scalar(act)
            act.wait_ge(wv_loaded, 16)
            nc.scalar.activation(wv[0][:, :], wv_raw[:, :], ACT.Copy).then_inc(wv_hi, 1)
            act.wait_ge(k_rope_step, 3)
            for k in range(2):
                nc.scalar.activation(k_head[k][0][R, :], kr[R, :], ACT.Copy).then_inc(rope_hi, 1)
            for i in range(TT):
                act.wait_ge(v_out, i + 1)
                nc.scalar.activation(v_all[:, i, :], chip.bank(4 + i % 4), ACT.Copy).then_inc(v_stored, 1)

            def round_w(h, slot):
                act.wait_ge(w_loaded[slot], 16 * (h - slot) + 32)
                if not is_first(h):
                    act.wait_ge(k_out, h)
                nc.scalar.activation(wq[slot][0][:, :, :], wq_raw[slot][:, :, :], ACT.Copy).then_inc(w_hi, 1)
                nc.scalar.activation(wk[slot][0][:, :], wk_raw[slot][:, :], ACT.Copy).then_inc(w_hi, 1)

            def take_q(h, pair):
                act.wait_ge(q_out, h + 1)
                if not is_first(h):
                    act.wait_ge(q_ready, h)
                nc.scalar.activation(q_row[:, :], chip.pair(pair, QK), ACT.Copy, scale=SCALE).then_inc(q_rowed, 1)

            def round_k(h, slot, pair):
                act.wait_ge(k_out, h + 1)
                if not (isinstance(h, int) and h < 2):
                    act.wait_ge(scored, TT * (h - 1))
                nc.scalar.activation(k_head[slot][0][0:NOPE, :], chip.pair(pair, NOPE), ACT.Copy).then_inc(k_hi, 1)

            def round_v(h, slot):
                if not (isinstance(h, int) and h < 2):
                    act.wait_ge(weighted, 4 * (h - 1))
                nc.scalar.activation(v_head[slot][0][:, :, 0:VD], v_all[:, :, ds(h * VD, VD)], ACT.Copy).then_inc(v_hi, 1)

            def round_q(h, slot):
                act.wait_ge(q_roped, 3 * (h + 1))
                nc.scalar.activation(q_head[slot][0][:, :], q_row[:, :], ACT.Copy).then_inc(q_hi, 1)

            def exponent(h, t):
                g = TT * h + t
                pair = (t + 1) % 2
                act.wait_ge(negmax, g + 1)
                if not (is_first(h) and t < 2):
                    act.wait_ge(turned, 2 * (g - 1))
                nc.scalar.activation(probs[t % 2][:, :], chip.pair(pair), ACT.Exp,
                                     bias=chip.negmax[:, t % 2:t % 2 + 1]).then_inc(exped, 1)

            def round_pt(h, t):
                g = TT * h + t
                b, u = t // 2, t % 2
                if u == 0 and not (is_first(h) and b < 2):
                    act.wait_ge(weighted, 4 * h + b - 1)
                for half in range(2):
                    act.wait_ge(turned, 2 * g + half + 1)
                    nc.scalar.activation(pt[b % 2][0][:, 4 * half:4 * half + 4, u * P:(u + 1) * P],
                                         chip.bank(4 + half).rearrange("p (k q) -> p k q", k=4), ACT.Copy).then_inc(pt_hi, 1)

            def copy_out(h, b):
                blk = 4 * h + b
                act.wait_ge(weighted, blk + 1)
                if not (is_first(h) and b < 2):
                    act.wait_ge(out_turned, blk - 1)
                nc.scalar.activation(out_t[b % 2][:, :], chip.bank(6 + b % 2, VD + 1, 2 * P), ACT.Copy).then_inc(out_copied, 1)

            def store_out(h, b):
                act.wait_ge(out_turned, 4 * h + b + 1)
                at = (6 + b % 2) * HALF + 2 * P
                src = chip.ps[:, at:at + 2 * (VD + 2)].rearrange("p (u d) -> p u d", u=2)[:, :, 0:VD + 1]
                dst = attn[:, 2 * b:2 * b + 2, ds(h, 1), 0:VD + 1].rearrange("p u h d -> p u (h d)")
                nc.scalar.activation(dst, src, ACT.Copy).then_inc(out_stored, 1)

            round_w(0, 0)
            take_q(0, 1)
            round_k(0, 0, 0)
            round_v(0, 0)
            round_q(0, 0)
            exponent(0, 0)

            def step(h, slot):
                more = not is_last(h)
                for t in range(TT):
                    round_pt(h, t)
                    if t < TT - 1:
                        exponent(h, t + 1)
                    elif more:
                        exponent(h + 1, 0)
                    if t % 2 and t >= 3:
                        copy_out(h, (t - 3) // 2)
                    elif t == 1 and not is_first(h):
                        copy_out(h - 1, 3)
                    elif t % 2 == 0 and t >= 4:
                        store_out(h, t // 2 - 2)
                    elif t % 2 == 0 and not is_first(h):
                        store_out(h - 1, t // 2 + 2)
                    if more:
                        if t == 1:
                            round_w(h + 1, 1 - slot)
                        elif t == 3:
                            take_q(h + 1, 0)
                        elif t == 4:
                            round_k(h + 1, 1 - slot, 1)
                        elif t == 5:
                            round_v(h + 1, 1 - slot)
                        elif t == 6:
                            round_q(h + 1, 1 - slot)
            peeled(act, step)
            copy_out(HEADS - 1, 3)
            store_out(HEADS - 1, 2)
            store_out(HEADS - 1, 3)

        @block.vector
        def _(dve):
            q_norm.vector(dve)
            kv_norm.vector(dve)
            dve.wait_ge(wv_hi, 1)
            nc.vector.tensor_tensor(wv[1][:, :], wv_raw[:, :], wv[0][:, :].bitcast(F32), ALU.subtract).then_inc(wv_ready, 1)
            dve.wait_ge(ropes_loaded, 32)
            dve.wait_ge(k_swapped, 32)
            nc.vector.tensor_tensor(kr[R, :], kr[R, :], cos_row[R, :], ALU.mult).then_inc(k_rope_step, 1)
            nc.vector.tensor_tensor(swapped[R, :], swapped[R, :], sin_row[R, :], ALU.mult).then_inc(k_rope_step, 1)
            dve.wait_ge(k_rope_step, 2)
            nc.vector.tensor_tensor(kr[R, :], kr[R, :], swapped[R, :], ALU.add).then_inc(k_rope_step, 1)
            dve.wait_ge(k_rope_step, 3)
            for k in range(2):
                dve.wait_ge(rope_hi, k + 1)
                nc.vector.tensor_tensor(k_head[k][1][R, :], kr[R, :], k_head[k][0][R, :].bitcast(F32),
                                        ALU.subtract).then_inc(rope_ready, 1)

            def rest_w(h, slot):
                dve.wait_ge(w_hi, 2 * h + 1)
                nc.vector.tensor_tensor(wq[slot][1][:, :, :], wq_raw[slot][:, :, :], wq[slot][0][:, :, :].bitcast(F32),
                                        ALU.subtract).then_inc(w_ready, 1)
                dve.wait_ge(w_hi, 2 * h + 2)
                nc.vector.tensor_tensor(wk[slot][1][:, :], wk_raw[slot][:, :], wk[slot][0][:, :].bitcast(F32),
                                        ALU.subtract).then_inc(w_ready, 1)

            def rest_k(h, slot, pair):
                dve.wait_ge(k_hi, h + 1)
                nc.vector.tensor_tensor(k_head[slot][1][0:NOPE, :], chip.pair(pair, NOPE),
                                        k_head[slot][0][0:NOPE, :].bitcast(F32), ALU.subtract).then_inc(k_ready, 1)

            def rest_v(h, slot):
                dve.wait_ge(v_hi, h + 1)
                nc.vector.tensor_tensor(v_head[slot][1][:, :, 0:VD], v_all[:, :, ds(h * VD, VD)],
                                        v_head[slot][0][:, :, 0:VD].bitcast(F32), ALU.subtract).then_inc(v_ready, 1)

            def rotate_q(h):
                dve.wait_ge(q_swapped, 32 * (h + 1))
                nc.vector.tensor_tensor(q_row[R, :], q_row[R, :], cos_row[R, :], ALU.mult).then_inc(q_roped, 1)
                nc.vector.tensor_tensor(swapped[R, :], swapped[R, :], sin_row[R, :], ALU.mult).then_inc(q_roped, 1)
                dve.wait_ge(q_roped, 3 * h + 2)
                nc.vector.tensor_tensor(q_row[R, :], q_row[R, :], swapped[R, :], ALU.add).then_inc(q_roped, 1)

            def rest_q(h, slot):
                dve.wait_ge(q_hi, h + 1)
                nc.vector.tensor_tensor(q_head[slot][1][:, :], q_row[:, :], q_head[slot][0][:, :].bitcast(F32),
                                        ALU.subtract).then_inc(q_ready, 1)

            def row_max(h, t):
                g = TT * h + t
                c = slice(t % 2, t % 2 + 1)
                dve.wait_ge(scored, g + 1)
                if not (is_first(h) and t < 2):
                    dve.wait_ge(exped, g - 1)
                nc.vector.tensor_reduce(chip.rowmax[:, c], chip.pair((t + 1) % 2), AXX, ALU.max).then_inc(maxed, 1)
                dve.wait_ge(maxed, g + 1)
                nc.vector.tensor_scalar(chip.negmax[:, c], chip.rowmax[:, c], -1.0, None, ALU.mult).then_inc(negmax, 1)

            def rest_pt(h, t):
                g = TT * h + t
                b, u = t // 2, t % 2
                for half in range(2):
                    dve.wait_ge(pt_hi, 2 * g + half + 1)
                    view = [pt[b % 2][k][:, 4 * half:4 * half + 4, u * P:(u + 1) * P] for k in range(2)]
                    nc.vector.tensor_tensor(view[1], chip.bank(4 + half).rearrange("p (k q) -> p k q", k=4),
                                            view[0].bitcast(F32), ALU.subtract).then_inc(pt_ready, 1)

            rest_w(0, 0)
            rest_k(0, 0, 0)
            rest_v(0, 0)
            rotate_q(0)
            rest_q(0, 0)
            row_max(0, 0)

            def step(h, slot):
                more = not is_last(h)
                for t in range(TT):
                    if t < TT - 1:
                        row_max(h, t + 1)
                    elif more:
                        row_max(h + 1, 0)
                    rest_pt(h, t)
                    if more:
                        if t == 1:
                            rest_w(h + 1, 1 - slot)
                        elif t == 4:
                            rest_k(h + 1, 1 - slot, 1)
                        elif t == 5:
                            rotate_q(h + 1)
                            rest_v(h + 1, 1 - slot)
                        elif t == 6:
                            rest_q(h + 1, 1 - slot)
            peeled(dve, step)


def mixer_out_block(chip, dram, w, attn, hyena, xT):
    nc = chip.nc
    mix_hi = chip.at("o_mix_hi", 32, [P, GROUPS * VD // P, SEQ], F32R)
    mix_lo = chip.at("o_mix_lo", 64, [P, GROUPS * VD // P, SEQ], F32R)
    normed = chip.at("o_normed", 96, [P, TT, HEADS, VD])
    squares = chip.at("o_squares", 128, [P, TT, HEADS, VD])
    hy = hyena[:, :, :].rearrange("p i (h d) -> p i h d", h=HEADS)
    at = attn[:, :, :, 0:VD]
    weight = attn[:, :, :, VD:VD + 1].rearrange("p i h o -> p i (h o)")
    power, rstd = chip.o_power, chip.o_rstd
    s = chip.sem
    x_loaded, squared, stat, rooted, normed_ready = (s("o_x_loaded"), s("o_squared"), s("o_stat"), s("o_rooted"),
                                                     s("o_normed_ready"))
    turned, mix_hi_ready, mix_ready, added = s("o_turned"), s("o_mix_hi_ready"), s("o_mix_ready"), s("o_added")
    CT = D // P

    with nc.Block() as block:
        @block.sync
        def _(sp):
            w.load(sp, 0, 0, 0)
            w.load(sp, 1, 1, P)
            sp.dma_start(xT[:], dram["residual"].rearrange("p (k t) -> p k t", k=KT)).then_inc(x_loaded, 16)
            with by_two(sp, 2, CT) as n:
                for a in range(2):
                    sp.wait_ge(w.ready, n + a - 1)
                    w.load(sp, n + a, a, (n + a) * P)

        @block.tensor
        def _(pe):
            for ct in range(CT):
                pe.wait_ge(normed_ready, 1 + ct // 4)
                for r in range(2):
                    n = 2 * ct + r
                    if n >= 4:
                        pe.wait_ge(mix_ready, n - 3)
                    src = (normed, hy)[ct // 4]
                    for tt in range(TT // 2):
                        pair_of_heads = src[:, r * (TT // 2) + tt, 2 * (ct % 4):2 * (ct % 4) + 2, :]
                        last = nc.tensor.transpose(chip.bank(4 + n % 4)[:, tt * P:(tt + 1) * P],
                                                   pair_of_heads.rearrange("p h d -> p (h d)"), chip.ident[:, :])
                    last.then_inc(turned, 1)
            pe.wait_ge(mix_ready, 2 * CT)

            def product(n, slot):
                if not isinstance(n, int) or n >= 2:
                    pe.wait_ge(added, n - 1)
                w.product(pe, n, slot, [chip.bank(2 * slot), chip.bank(2 * slot + 1)], mix_hi, mix_lo, None)
            product(0, 0)
            product(1, 1)
            with by_two(pe, 2, CT) as n:
                product(n, 0)
                product(n + 1, 1)

        @block.scalar
        def _(act):
            nc.scalar.activation(squares[:, :, :, :], at, ACT.Square).then_inc(squared, 1)
            act.wait_ge(stat, 1)
            nc.scalar.activation(squares[:, :, :, :], hy, ACT.Square).then_inc(squared, 1)
            act.wait_ge(stat, 5)
            nc.scalar.activation(power[:, :], power[:, :], ACT.Sqrt).then_inc(rooted, 1)
            w.round(act, 0, 0)
            for ct in range(CT):
                for r in range(2):
                    n = 2 * ct + r
                    act.wait_ge(turned, n + 1)
                    nc.scalar.activation(mix_hi[:, ct, r * HALF:(r + 1) * HALF], chip.bank(4 + n % 4), ACT.Copy,
                                         scale=chip.head_gain[:, ct:ct + 1]).then_inc(mix_hi_ready, 1)
            w.round(act, 1, 1)
            with by_two(act, 2, CT) as n:
                w.round(act, n, 0)
                w.round(act, n + 1, 1)

        @block.vector
        def _(dve):
            HT = TT * HEADS
            flat = squares[:, :, :, :].rearrange("p i h d -> p (i h) d")
            a, b = power[:, 0:HT], power[:, HT:2 * HT]
            dve.wait_ge(squared, 1)
            nc.vector.tensor_reduce(a, flat, AXX, ALU.add).then_inc(stat, 1)
            wt = chip.o_weight
            nc.vector.tensor_tensor(wt[:, :].rearrange("p (i h) -> p i h", i=TT), weight, weight, ALU.mult).then_inc(stat, 1)
            dve.wait_ge(squared, 2)
            nc.vector.tensor_reduce(b, flat, AXX, ALU.add).then_inc(stat, 1)
            dve.wait_ge(stat, 3)
            nc.vector.tensor_scalar(b, b, 1.0 / VD, EPS, ALU.mult, ALU.add).then_inc(stat, 1)
            nc.vector.scalar_tensor_tensor(out=a, in0=wt[:, :], scalar=EPS * VD, in1=a, op0=ALU.mult,
                                           op1=ALU.add).then_inc(stat, 1)
            dve.wait_ge(rooted, 1)
            nc.vector.reciprocal(rstd[:, :], power[:, :]).then_inc(stat, 1)
            dve.wait_ge(stat, 6)
            for part, (src, dst) in enumerate(((at, normed[:, :, :, :]), (hy, hy))):
                scale = rstd[:, part * HT:(part + 1) * HT].unsqueeze(2).to_broadcast([P, HT, VD])
                if part == 0:
                    nc.vector.scalar_tensor_tensor(out=dst.rearrange("p i h d -> p (i h) d"), in0=src.rearrange("p i h d -> p (i h) d"),
                                                   scalar=float(math.sqrt(VD)), in1=scale, op0=ALU.mult,
                                                   op1=ALU.mult).then_inc(normed_ready, 1)
                else:
                    nc.vector.tensor_tensor(dst.rearrange("p i h d -> p (i h) d"), src.rearrange("p i h d -> p (i h) d"),
                                            scale, ALU.mult).then_inc(normed_ready, 1)
            w.rest(dve, 0, 0)
            for ct in range(CT):
                for r in range(2):
                    n = 2 * ct + r
                    dve.wait_ge(mix_hi_ready, n + 1)
                    part = slice(r * HALF, (r + 1) * HALF)
                    nc.vector.scalar_tensor_tensor(out=mix_lo[:, ct, part], in0=chip.bank(4 + n % 4),
                                                   scalar=chip.head_gain[:, ct:ct + 1], in1=mix_hi[:, ct, part].bitcast(F32),
                                                   op0=ALU.mult, op1=ALU.subtract).then_inc(mix_ready, 1)
            w.rest(dve, 1, 1)
            dve.wait_ge(x_loaded, 16)

            def add(n, slot):
                dve.wait_ge(w.used, n + 1)
                view = xT[:, ds(n, 1), :].rearrange("p k (t r) -> p (k r) t", r=2)
                nc.vector.tensor_tensor(view, chip.pair(slot).rearrange("p (r t) -> p r t", r=2), view,
                                        ALU.add).then_inc(added, 1)
            with by_two(dve, 2, CT) as n:
                w.rest(dve, n, 0)
                add(n - 2, 0)
                w.rest(dve, n + 1, 1)
                add(n - 1, 1)
            add(CT - 2, 0)
            add(CT - 1, 1)


def output_block(chip, dram, xT):
    nc = chip.nc
    gain = chip.at("e_gain", 32, [P, D])
    junk = chip.at("e_junk", 36, [P, D])
    y = [chip.at(f"e_y{k}", 40 + 4 * k, [P, D]) for k in range(2)]
    total, root = chip.e_total, chip.e_root
    s = chip.sem
    gain_loaded, turned, squared, rooted, scaled = (s("e_gain_loaded"), s("e_turned"), s("e_squared"), s("e_rooted"),
                                                    s("e_scaled"))
    rstd_ready, stored = s("e_rstd_ready"), [s("e_stored0"), s("e_stored1")]
    with nc.Block() as block:
        @block.sync
        def _(sp):
            sp.dma_start(gain[:], dram["final_norm_g"].partition_broadcast(P)).then_inc(gain_loaded, 16)
            with by_two(sp, 0, TT) as i:
                for a in range(2):
                    sp.wait_ge(scaled, i + a + 1)
                    sp.dma_start(dram["out"][ds((i + a) * P, P), :], y[a][:]).then_inc(stored[a], 16)
            for a in range(2):
                sp.wait_ge(stored[a], 16 * TT // 2)

        @block.tensor
        def _(pe):
            for i in range(TT):
                if i >= 4:
                    pe.wait_ge(scaled, i - 3)
                for k in range(KT):
                    at = (i % 4) * 2 * HALF + k * P
                    last = nc.tensor.transpose(chip.ps[:, at:at + P], xT[:, k, i * P:(i + 1) * P], chip.ident[:, :])
                last.then_inc(turned, 1)

        @block.scalar
        def _(act):
            for i in range(TT):
                act.wait_ge(turned, i + 1)
                if i:
                    act.wait_ge(squared, i)
                nc.scalar.activation(junk[:, :], chip.pair(i % 4), ACT.Square, accum_out=total[:, i:i + 1]).then_inc(squared, 1)
                act.wait_ge(squared, i + 1)
                nc.scalar.activation(root[:, i:i + 1], total[:, i:i + 1], ACT.Sqrt, bias=chip.eps[:, 0:1],
                                     scale=1.0 / D).then_inc(rooted, 1)

        @block.vector
        def _(dve):
            dve.wait_ge(gain_loaded, 16)
            for i in range(TT):
                dve.wait_ge(rooted, i + 1)
                nc.vector.reciprocal(root[:, i:i + 1], root[:, i:i + 1]).then_inc(rstd_ready, 1)
                dve.wait_ge(rstd_ready, i + 1)
                if i >= 2:
                    dve.wait_ge(stored[i % 2], 16 * (i // 2))
                nc.vector.scalar_tensor_tensor(out=y[i % 2][:, :], in0=chip.pair(i % 4), scalar=root[:, i:i + 1],
                                               in1=gain[:, :], op0=ALU.mult, op1=ALU.mult).then_inc(scaled, 1)


def encoder(nc, dram):
    with ExitStack() as ctx:
        chip = Chip(nc, ctx)
        chip.ident = chip.small("ident", [P, P])
        chip.ones = chip.small("ones", [P, P])
        chip.eps = chip.small("eps", [P, 1])
        gains = {}
        for name, tiles in (("ffn1_norm_g", KT), ("mix_norm_g", KT), ("ffn2_norm_g", KT), ("q_norm_g", 2),
                            ("kv_norm_g", 1), ("head_norm_g", KT)):
            gains[name] = chip.small(f"g_{name}", [P, tiles])
        chip.q_gain, chip.kv_gain, chip.head_gain = gains["q_norm_g"], gains["kv_norm_g"], gains["head_norm_g"]
        conv_w = chip.small("conv_w", [P, 3, HY_TILES])
        conv_b = chip.small("conv_b", [P, HY_TILES])
        chip.fw1 = chip.at("f_w1", 203, [EMB, HID])
        chip.fw2 = chip.at("f_w2", 203.25, [HID, HID])
        chip.fcol = chip.small("fcol", [HID, 3])
        chip.negmax = chip.small("negmax", [P, 2])
        chip.rowmax = chip.small("rowmax", [P, 2])
        chip.o_power = chip.small("o_power", [P, 2 * TT * HEADS])
        chip.o_rstd = chip.at("o_rstd", 201, [P, 2 * TT * HEADS])
        chip.o_weight = chip.at("o_weight", 202, [P, TT * HEADS])
        chip.e_total = chip.small("e_total", [P, TT])
        chip.e_root = chip.small("e_root", [P, TT])
        chip.consts_ready = chip.sem("consts_ready")
        columns_loaded, filled = chip.sem("columns_loaded"), chip.sem("filled")

        xT = chip.at("xT", 0, [P, KT, SEQ])
        x_hi = chip.at("x_hi", 32, [P, KT, SEQ], F32R)
        x_lo = chip.at("x_lo", 64, [P, KT, SEQ], F32R)
        x_raw = chip.at("x_raw", 32, [P, TT, D])

        with nc.Block() as block:
            @block.gpsimd
            def _(pool):
                nc.gpsimd.memset(chip.ident[:, :], 0.0).then_inc(filled, 1)
                nc.gpsimd.memset(chip.ones[:, :], 1.0).then_inc(filled, 1)
                nc.gpsimd.memset(chip.eps[:, :], EPS).then_inc(filled, 1)
                pool.wait_ge(filled, 3)
                nc.gpsimd.affine_select(out=chip.ident[:, :], in_=chip.ident[:, :], compare_op=ALU.not_equal, fill=1.0,
                                        base=0, pattern=[[-1, P]], channel_multiplier=1).then_inc(chip.consts_ready, 1)

            @block.sync
            def _(sp):
                for name, t in gains.items():
                    sp.dma_start(t[:], dram[name]).then_inc(columns_loaded, 16)
                sp.dma_start(conv_w[:], dram["hyena_conv_w"]).then_inc(columns_loaded, 16)
                sp.dma_start(conv_b[:], dram["hyena_conv_b"]).then_inc(columns_loaded, 16)
                sp.wait_ge(columns_loaded, 16 * 8)

        x_loaded = chip.sem("x_loaded")
        filters_block(chip, dram, x_raw, x_loaded)
        ffn1 = Ffn(chip, "f1", dram["ffn1_w_gate"], dram["ffn1_w_up"], dram["ffn1_w_down"], xT, x_hi, x_lo)
        input_block(chip, x_raw, x_loaded, xT, gains["ffn1_norm_g"], x_hi, x_lo, ffn1.prefetch)
        ffn1.run()

        v_hi, v_lo = (chip.at(f"v_{k}", 16 * n, [P, TT, C], F32R) for n, k in enumerate(("hi", "lo")))
        gates = [chip.at(f"gate{k}", 96 + 16 * k, [P, TT, C]) for k in range(2)]
        cq = chip.at("cq", 128, [P, 2, SEQ])
        ckv = chip.at("ckv", 136, [P, 1, SEQ])
        kr = chip.at("kr", 140, [QK, SEQ])
        attn = chip.at("attn", 184, [P, TT, HEADS, VD + 2])
        w_in = ColumnWeights(chip, "m_w", dram["w_in"], 160, 144)

        def prefetch_in(sp):
            w_in.load(sp, 0, 0, 0)
            w_in.load(sp, 1, 1, P)
        norm_block(chip, "n2", xT, gains["mix_norm_g"], x_hi, x_lo, prefetch_in,
                   dram["residual"].rearrange("p (k t) -> p k t", k=KT))
        mixer_in_block(chip, w_in, x_hi, x_lo, cq, ckv, kr, v_hi, v_lo, gates, conv_w, conv_b)
        hyena_block(chip, dram, v_hi, v_lo, gates)
        chip.recycle()
        attention_block(chip, dram, cq, ckv, kr, attn)
        w_out = ColumnWeights(chip, "o_w", dram["w_out"], 160, 144)
        mixer_out_block(chip, dram, w_out, attn, gates[1], xT)
        ffn2 = Ffn(chip, "f2", dram["ffn2_w_gate"], dram["ffn2_w_up"], dram["ffn2_w_down"], xT, x_hi, x_lo)
        norm_block(chip, "n3", xT, gains["ffn2_norm_g"], x_hi, x_lo, ffn2.prefetch)
        ffn2.run()
        output_block(chip, dram, xT)


INPUTS = ["x", "ffn1_norm_g", "ffn1_w_gate", "ffn1_w_up", "ffn1_w_down", "mix_norm_g", "w_in", "q_norm_g", "w_uq",
          "kv_norm_g", "w_ukv", "hyena_conv_w", "hyena_conv_b", "filt_w1", "filt_b1", "filt_w2", "filt_b2", "filt_w3",
          "filt_freq", "hyena_d", "head_norm_g", "w_out", "ffn2_norm_g", "ffn2_w_gate", "ffn2_w_up", "ffn2_w_down",
          "final_norm_g"]
COLUMNS = ("ffn1_norm_g", "mix_norm_g", "ffn2_norm_g", "q_norm_g", "kv_norm_g", "head_norm_g", "hyena_conv_w",
           "hyena_conv_b", "filt_b1", "filt_b2", "filt_freq")


def kernel(**inputs):
    import concourse.bacc as _bacc
    from concourse.bass_utils import run_bass_kernel_spmd as _run

    nc = _bacc.Bacc("TRN2", target_bir_lowering=False, num_devices=1)
    arrays, dram = {}, {}
    for name in INPUTS:
        a = np.ascontiguousarray(inputs[name])
        a = a.reshape(a.shape[1:]) if a.ndim > 1 else a
        if name in COLUMNS:
            a = np.ascontiguousarray(np.moveaxis(a.reshape(*a.shape[:-1], -1, min(P, a.shape[-1])), -1, 0))
        arrays[f"in_{name}"] = a
        dram[name] = nc.dram_tensor(f"in_{name}", a.shape, F32, kind="ExternalInput").ap()
    out = nc.dram_tensor("out_y", (SEQ, D), F32, kind="ExternalOutput")
    dram["out"] = out.ap()
    dram["residual"] = nc.dram_tensor("residual", (P, KT * SEQ), F32, kind="Internal").ap()
    dram["spectra"] = nc.dram_tensor("spectra", (2 * WT * P, 4 * C), F32, kind="Internal").ap()
    fwd, inv = transform_tables()
    for name, a in (("fwd", fwd), ("inv", inv), ("features", filter_features()), ("decay", filter_decay()),
                    ("rope", rope_rows())):
        dram[name] = nc.inline_tensor(a, name=f"c_{name}").ap()
    encoder(nc, dram)
    r = _run(nc, [arrays], core_ids=[0])
    return r.results[0]["out_y"].reshape(1, SEQ, D)
```

```python
import math
from contextlib import ExitStack

import numpy as np
import concourse.bass as bass
import concourse.mybir as mybir

F32 = mybir.dt.float32
F32R = mybir.dt.float32r
ACT = mybir.ActivationFunctionType
ALU = mybir.AluOpType
AXX = mybir.AxisListType.X

P = 128
SEQ = 1024
D = 1024
KT = D // P
TT = SEQ // P
HALF = 512
FFN = 2816
EPS = 1e-6
Q_RANK, KV_RANK, ROPE = 256, 128, 32
HEADS, NOPE, VD = 8, 64, 64
QK = NOPE + ROPE
C = 512
HID = 64
BANDS = 16
EMB = 2 * BANDS + 1
WT = SEQ // 2 // P
GROUPS = 16
IN_COLS = Q_RANK + KV_RANK + ROPE + 3 * C

ds = bass.ds


def by_two(eng, start, end):
    return eng.Fori(start, end - 1, 2)


def split_hi_lo(a):
    a32 = a.astype(np.float32)
    bits = a32.view(np.uint32).astype(np.uint64)
    hi = ((bits + 0x7FF + ((bits >> 12) & 1)) & 0xFFFFF000).astype(np.uint32).view(np.float32)
    return hi, (a32 - hi).astype(np.float32)


def transform_tables():
    w = np.arange(SEQ // 2) + 0.5
    t = np.arange(SEQ)
    ang = math.pi / SEQ * w[:, None] * t[None, :]
    both = np.stack([np.cos(ang), np.sin(ang)])
    hl = np.stack(split_hi_lo(both), axis=1)
    x = hl.reshape(2, 2, WT, P, TT // 2, P, 2)
    fwd = x.transpose(2, 6, 5, 4, 0, 1, 3).reshape(2 * WT * P, (TT // 2) * 4 * P)
    inv = x.transpose(6, 2, 3, 4, 0, 1, 5).reshape(2 * WT * P, (TT // 2) * 4 * P) / SEQ
    return np.ascontiguousarray(fwd, np.float32), np.ascontiguousarray(inv, np.float32)


def parity_order():
    return np.concatenate([np.arange(0, SEQ, 2), np.arange(1, SEQ, 2)])


def filter_features():
    f = np.float32
    pos = np.arange(SEQ, dtype=f)
    t = pos / f(SEQ - 1)
    bands = np.linspace(1e-4, BANDS - 1, BANDS, dtype=f)
    ang = (f(2.0 * math.pi) * pos / f(SEQ))[:, None] * bands[None, :]
    z = np.concatenate([t[:, None], np.cos(ang), -np.sin(ang)], axis=-1).astype(f)
    return np.ascontiguousarray(z[parity_order()].T)


def filter_decay():
    f = np.float32
    t = np.arange(SEQ, dtype=f) / f(SEQ - 1)
    lo, hi = math.log(1e-2) / 1.5, math.log(1e-2) / 0.3
    deltas = np.abs(np.linspace(lo, hi, C, dtype=f))
    dec = np.exp(-t[:, None] * deltas[None, :]).astype(f)
    return np.ascontiguousarray(dec[parity_order()])


def rope_rows():
    f = np.float32
    inv = (1.0 / (f(10000.0) ** (np.arange(0, ROPE, 2, dtype=f) / f(ROPE)))).astype(f)
    ang = np.arange(SEQ, dtype=f)[None, :] * inv[:, None]
    cos, sin = np.cos(ang).astype(f), np.sin(ang).astype(f)
    return np.ascontiguousarray(np.concatenate([cos, cos, -sin, sin], axis=0))


class Chip:

    def __init__(self, nc, ctx):
        self.nc, self.sems = nc, []
        self.small_at = -(-nc.sbuf_base // 64) * 64
        self.small_end = self.small_at + 3072
        self.main = self.small_end
        self.ps = ctx.enter_context(nc.psum_tensor("ps", [P, 8 * HALF], F32))

    def at(self, name, kb, shape, dtype=F32):
        return self.nc.alloc_sbuf_tensor_at(name, shape, dtype, offset=self.main + int(kb * 1024))

    def small(self, name, shape, dtype=F32):
        size = 4
        for n in shape[1:]:
            size *= n
        t = self.nc.alloc_sbuf_tensor_at(name, shape, dtype, offset=self.small_at)
        self.small_at += -(-size // 32) * 32
        assert self.small_at <= self.small_end, name
        return t

    def sem(self, name):
        self.sems.append(self.nc.alloc_semaphore(name=name))
        return self.sems[-1]

    def recycle(self):
        self.nc.clear_and_free_semaphores(self.sems)
        self.nc.all_engine_barrier()
        self.sems = []

    def bank(self, n, rows=P, cols=HALF):
        return self.ps[0:rows, n * HALF:n * HALF + cols]

    def pair(self, n, rows=P):
        return self.ps[0:rows, n * 2 * HALF:(n + 1) * 2 * HALF]


def three_pass(nc, outs, w_hi, w_lo, x_hi, x_lo, start, stop):
    for n, out in enumerate(outs):
        nc.tensor.matmul(out, w_hi, x_hi[n], start=start, stop=False)
        nc.tensor.matmul(out, w_hi, x_lo[n], start=False, stop=False)
    for n, out in enumerate(outs):
        last = nc.tensor.matmul(out, w_lo, x_hi[n], start=False, stop=stop)
    return last


def halves(x, k):
    return [x[:, k, 0:HALF], x[:, k, HALF:2 * HALF]]


class FeatureSplit:
    ADDED = KT - 2

    def __init__(self, chip, tag, src, gain, hi, lo, squares_kb, slots, root_kb, pair):
        self.nc, self.chip, self.src, self.gain, self.hi, self.lo, self.pair = chip.nc, chip, src, gain, hi, lo, pair
        self.slots = slots
        self.squares = chip.at(f"{tag}_squares", squares_kb, [P, slots, SEQ])
        self.rstd = chip.at(f"{tag}_rstd", root_kb, [P, SEQ])
        self.hi_ready, self.lo_ready = chip.sem(f"{tag}_hi_ready"), chip.sem(f"{tag}_lo_ready")
        self.squared, self.pair_added = chip.sem(f"{tag}_squared"), chip.sem(f"{tag}_pair_added")
        self.summed = chip.sem(f"{tag}_summed")
        self.rooted, self.rstd_ready = chip.sem(f"{tag}_rooted"), chip.sem(f"{tag}_rstd_ready")

    def scalar(self, act, k, src_ready, count):
        act.wait_ge(src_ready, count)
        self.round(act, k)
        self.square(act, k, src_ready, count)

    def round(self, act, k):
        self.nc.scalar.activation(self.hi[:, k, :], self.src[:, k, :], ACT.Copy,
                                  scale=self.gain[:, k:k + 1]).then_inc(self.hi_ready, 1)

    def square(self, act, k, src_ready, count):
        act.wait_ge(src_ready, count)
        if k >= self.slots:
            act.wait_ge(self.summed, (k - self.slots) // 2 + 1)
        self.nc.scalar.activation(self.squares[:, k % self.slots, :], self.src[:, k, :], ACT.Square).then_inc(self.squared, 1)

    def vector(self, dve, k):
        dve.wait_ge(self.hi_ready, k + 1)
        self.nc.vector.scalar_tensor_tensor(out=self.lo[:, k, :], in0=self.src[:, k, :], scalar=self.gain[:, k:k + 1],
                                            in1=self.hi[:, k, :].bitcast(F32), op0=ALU.mult,
                                            op1=ALU.subtract).then_inc(self.lo_ready, 1)

    def gpsimd(self, pool):
        for k in range(0, self.ADDED, 2):
            pool.wait_ge(self.squared, k + 2)
            a, b = self.squares[:, k % self.slots, :], self.squares[:, k % self.slots + 1, :]
            self.nc.gpsimd.tensor_tensor(a, a, b, ALU.add).then_inc(self.pair_added, 1)

    def tensor(self, pe, k):
        if k < self.ADDED:
            pe.wait_ge(self.pair_added, k // 2 + 1)
        else:
            pe.wait_ge(self.squared, k + 1)
        for n in range(2):
            last = self.nc.tensor.matmul(self.chip.bank(2 * self.pair + n), self.chip.ones[:, :],
                                         self.squares[:, k % self.slots, n * HALF:(n + 1) * HALF],
                                         start=(k == 0), stop=(k == KT - 1))
        last.then_inc(self.summed, 1)

    def root_of_mean(self, act):
        act.wait_ge(self.summed, KT // 2 + 1)
        self.nc.scalar.activation(self.rstd[:, :], self.chip.pair(self.pair), ACT.Sqrt, bias=self.chip.eps[:, 0:1],
                                  scale=1.0 / D).then_inc(self.rooted, 1)

    def invert(self, dve):
        dve.wait_ge(self.rooted, 1)
        self.nc.vector.reciprocal(self.rstd[:, :], self.rstd[:, :]).then_inc(self.rstd_ready, 1)
        dve.wait_ge(self.rstd_ready, 1)


class FeatureNorm:

    def __init__(self, chip, tag, src, tiles, gain, hi, lo, squares, root, scaled, pair=0):
        self.nc, self.chip, self.src, self.tiles, self.gain = chip.nc, chip, src, tiles, gain
        self.hi, self.lo, self.squares, self.root, self.scaled, self.pair = hi, lo, squares, root, scaled, pair
        self.squared = chip.sem(f"{tag}_squared")
        self.summed = chip.sem(f"{tag}_summed")
        self.rooted = chip.sem(f"{tag}_rooted")
        self.rstd_ready = chip.sem(f"{tag}_rstd_ready")
        self.y_scaled = chip.sem(f"{tag}_y_scaled")
        self.hi_ready = chip.sem(f"{tag}_hi_ready")
        self.lo_ready = chip.sem(f"{tag}_lo_ready")

    def scalar(self, act, src_ready=None):
        nc = self.nc
        for k in range(self.tiles):
            if src_ready is not None:
                act.wait_ge(src_ready, k + 1)
            if k >= 2:
                act.wait_ge(self.summed, k - 1)
            nc.scalar.activation(self.squares[:, k % 2, :], self.src[:, k, :], ACT.Square).then_inc(self.squared, 1)
        act.wait_ge(self.summed, self.tiles)
        nc.scalar.activation(self.root[:, :], self.chip.pair(self.pair), ACT.Sqrt, bias=self.chip.eps[:, 0:1],
                             scale=1.0 / (self.tiles * P)).then_inc(self.rooted, 1)
        for k in range(self.tiles):
            act.wait_ge(self.y_scaled, k + 1)
            nc.scalar.activation(self.hi[:, k, :], self.scaled[:, k % 2, :], ACT.Copy).then_inc(self.hi_ready, 1)

    def tensor(self, pe):
        nc = self.nc
        for k in range(self.tiles):
            pe.wait_ge(self.squared, k + 1)
            for n in range(2):
                last = nc.tensor.matmul(self.chip.bank(2 * self.pair + n), self.chip.ones[:, :],
                                        self.squares[:, k % 2, n * HALF:(n + 1) * HALF],
                                        start=(k == 0), stop=(k == self.tiles - 1))
            last.then_inc(self.summed, 1)

    def vector(self, dve):
        nc = self.nc
        dve.wait_ge(self.rooted, 1)
        nc.vector.reciprocal(self.root[:, :], self.root[:, :]).then_inc(self.rstd_ready, 1)
        dve.wait_ge(self.rstd_ready, 1)

        def low(k):
            dve.wait_ge(self.hi_ready, k + 1)
            nc.vector.tensor_tensor(self.lo[:, k, :], self.scaled[:, k % 2, :], self.hi[:, k, :].bitcast(F32),
                                    ALU.subtract).then_inc(self.lo_ready, 1)

        for k in range(self.tiles):
            if k >= 2:
                dve.wait_ge(self.lo_ready, k - 1)
            nc.vector.scalar_tensor_tensor(out=self.scaled[:, k % 2, :], in0=self.src[:, k, :],
                                           scalar=self.gain[:, k:k + 1], in1=self.root[:, :],
                                           op0=ALU.mult, op1=ALU.mult).then_inc(self.y_scaled, 1)
            if k >= 1:
                low(k - 1)
        low(self.tiles - 1)


def filters_block(chip, dram, xT, norm, ffn, columns):
    nc = chip.nc
    x_in = [chip.at(f"x_in{k}", kb, [P, D]) for k, kb in enumerate((32, 36, 56, 60))]
    feat = chip.at("f_feat", 40, [EMB, SEQ])
    arg = chip.at("f_arg", 44, [HID, SEQ])
    turn = chip.at("f_turn", 48, [HID, SEQ])
    h1 = chip.at("f_h1", 52, [HID, SEQ])
    h2 = chip.at("f_h2", 176, [HID, SEQ])
    w3 = chip.at("f_w3", 160, [HID, 2, 2, C])
    w3_mix = chip.at("f_w3_mix", 168, [HID, 2, 2, C])
    decay = chip.at("f_decay", 180, [P, TT, C])
    skip = chip.at("f_skip", 196, [P, 2, C])
    tap_hi = chip.at("f_tap_hi", 64, [P, 2, TT, C], F32R)
    tap_lo = chip.at("f_tap_lo", 96, [P, 2, TT, C], F32R)
    table = [chip.at(f"f_table{s}", 128 + 8 * s, [P, TT // 2, 2, 2, P], F32R) for s in range(4)]
    mixd = [chip.at(f"f_mixd{s}", 40 + 4 * s, [P, 2, C]) for s in range(2)]
    absd = [chip.at(f"f_absd{s}", 32 + 4 * s, [P, 2, C]) for s in range(2)]
    mag = [chip.at(f"f_mag{s}", 48 + 2 * s, [P, C]) for s in range(2)]
    even = chip.at("f_even", 52, [P, 2, C])
    spec = chip.at("f_spec", 56, [P, 4, C])
    h2t = [chip.at(f"f_h2t{s}", 160 + 0.5 * s, [HID, P]) for s in range(2)]
    rnorm = chip.at("f_rnorm", 161, [P, C])

    s = chip.sem
    x_loaded, x_turned, x_copied = [s(f"x_loaded{k}") for k in range(4)], s("x_turned"), s("x_copied")
    loaded, w3_loaded, skip_loaded, decay_loaded = s("f_loaded"), s("f_w3_loaded"), s("f_skip_loaded"), s("f_decay_loaded")
    linear, step, sine, w3_mixed = s("f_linear"), s("f_step"), s("f_sine"), s("f_w3_mixed")
    h2t_ready, taps_out, mixed, edge = s("f_h2t_ready"), s("f_taps_out"), s("f_mixed"), s("f_edge")
    hi_ready, lo_ready, absed, mag_ready, mag_summed = (s("f_hi_ready"), s("f_lo_ready"), s("f_absed"),
                                                        s("f_mag_ready"), s("f_mag_summed"))
    rnorm_ready, columns_loaded = s("f_rnorm_ready"), s("columns_loaded")
    table_loaded = [s(f"f_table_loaded{k}") for k in range(4)]
    table_used, even_copied, spec_step, spec_stored = (s("f_table_used"), s("f_even_copied"), s("f_spec_step"),
                                                       s("f_spec_stored"))
    chip.spec_stored = spec_stored
    SPEC_STEPS = 5
    UNITS = 2 * WT
    TILES = 2 * WT

    turns = 1.0 / (2.0 * math.pi)
    big = float(1.5 * 2 ** 23)
    c1 = 6.28125
    c2 = math.floor((2.0 * math.pi - c1) * 2 ** 20) / 2 ** 20
    c3 = 2.0 * math.pi - c1 - c2
    pi = 3.1415925

    def tap_tiles(eng, tile):
        tile(0, 0)
        tile(1, 1)
        with by_two(eng, 2, TT) as i:
            tile(i, 0)
            tile(i + 1, 1)

    def at_tile(t, i):
        return t[:, :, i, :] if isinstance(i, int) else t[:, :, ds(i, 1), :].rearrange("p a b c -> p a (b c)")

    def later(o, i, k=1):
        return bool(o) or not isinstance(i, int) or i >= k

    with nc.Block() as block:
        @block.sync
        def _(sp):
            for dst, src in ((feat, dram["features"]), (chip.fw1, dram["filt_w1"]), (chip.fw2, dram["filt_w2"]),
                             (chip.fcol[:, 0:1], dram["filt_b1"]), (chip.fcol[:, 1:2], dram["filt_b2"]),
                             (chip.fcol[:, 2:3], dram["filt_freq"])):
                sp.dma_start(dst[:], src).then_inc(loaded, 16)
            for i in range(TT):
                if i >= 4:
                    sp.wait_ge(x_turned, i - 3)
                sp.dma_start(x_in[i % 4][:], dram["x"][i * P:(i + 1) * P, :]).then_inc(x_loaded[i % 4], 16)
                if i == 3:
                    sp.dma_start(w3[:], dram["filt_w3"].rearrange("h (o r c) -> h o r c", o=2, r=2)).then_inc(w3_loaded, 16)
                    sp.dma_start(decay[:], dram["decay"].rearrange("(i p) c -> p i c", p=P)).then_inc(decay_loaded, 16)
            for dst, src in columns:
                sp.dma_start(dst[:], src).then_inc(columns_loaded, 16)
            sp.dma_start(skip[:], dram["hyena_d"].rearrange("o c -> (o c)").partition_broadcast(P)
                         ).then_inc(skip_loaded, 16)

            def load_table(n):
                row = (n % UNITS) * P
                sp.dma_start(table[n % 4][:].bitcast(F32), dram["fwd"][row:row + P, :]).then_inc(table_loaded[n % 4], 16)
            load_table(0)
            load_table(1)
            sp.wait_ge(norm.summed, KT // 2 + 1)
            load_table(2)
            load_table(3)
            for t in range(TILES):
                for n in (2 * t + 4, 2 * t + 5):
                    if n < 2 * UNITS:
                        sp.wait_ge(table_used, n - 3)
                        load_table(n)
                if t == WT:
                    sp.wait_ge(mixed, 2 * TT)
                    sp.wait_ge(taps_out, 2 * TT)
                    ffn.load_gu(sp, 0)
                    sp.wait_ge(columns_loaded, 16 * len(columns))
                sp.wait_ge(spec_step, SPEC_STEPS * (t + 1))
                sp.dma_start(dram["spectra"][t * P:(t + 1) * P, :], spec[:]).then_inc(spec_stored, 16)

        @block.gpsimd
        def _(pool):
            pool.wait_ge(w3_loaded, 16)
            nc.gpsimd.tensor_tensor(w3_mix[:, :, 0, :], w3[:, :, 0, :], w3[:, :, 1, :], ALU.add).then_inc(w3_mixed, 1)
            nc.gpsimd.tensor_tensor(w3_mix[:, :, 1, :], w3[:, :, 0, :], w3[:, :, 1, :], ALU.subtract).then_inc(w3_mixed, 1)
            pool.wait_ge(w3_mixed, 2)
            norm.gpsimd(pool)
            pool.wait_ge(sine, 2)
            for o in range(2):
                def turn_slot(i, slot, o=o):
                    if later(o, i, 2):
                        pool.wait_ge(taps_out, TT * o + i - 1)
                    nc.gpsimd.tensor_copy(h2t[slot][:, :], h2[:, ds(i * P, P)]).then_inc(h2t_ready, 1)

                tap_tiles(pool, turn_slot)

        @block.tensor
        def _(pe):
            pe.wait_ge(loaded, 16 * 6)
            pe.wait_ge(chip.consts_ready, 1)
            for n in range(2):
                last = nc.tensor.matmul(chip.bank(n, HID), chip.fw1[:, :], feat[:, n * HALF:(n + 1) * HALF],
                                        start=True, stop=True)
            last.then_inc(linear, 1)

            def turn_x(i):
                pe.wait_ge(x_loaded[i % 4], 16 * (i // 4 + 1))
                if i >= 2:
                    pe.wait_ge(x_copied, i - 1)
                for k in range(KT):
                    at = (2 + i % 2) * 2 * HALF + k * P
                    last = nc.tensor.transpose(chip.ps[:, at:at + P], x_in[i % 4][:, k * P:(k + 1) * P], chip.ident[:, :])
                last.then_inc(x_turned, 1)

            for i in range(TT):
                turn_x(i)
                if i == 5:
                    pe.wait_ge(sine, 1)
                    for n in range(2):
                        last = nc.tensor.matmul(chip.bank(2 + n, HID), chip.fw2[:, :], h1[:, n * HALF:(n + 1) * HALF],
                                                start=True, stop=True)
                    last.then_inc(linear, 1)
            pe.wait_ge(x_copied, TT)
            for k in (*range(0, norm.ADDED, 2), KT - 2, KT - 1):
                norm.tensor(pe, k)
            pe.wait_ge(w3_mixed, 2)
            pe.wait_ge(step, 14)

            for o in range(2):
                def taps(i, slot, o=o):
                    pe.wait_ge(h2t_ready, TT * o + i + 1)
                    if later(o, i, 2):
                        pe.wait_ge(mixed, TT * o + i - 1)
                    for m in range(2):
                        last = nc.tensor.matmul(chip.bank(2 * slot + m), h2t[slot][:, :], w3_mix[:, o, m, :],
                                                start=True, stop=True)
                    last.then_inc(taps_out, 1)

                def magnitudes(i, slot, first, last, o=o):
                    pe.wait_ge(mag_ready, TT * o + i + 1)
                    nc.tensor.matmul(chip.bank(7), chip.ones[:, :], mag[slot][:, :], start=first,
                                     stop=last).then_inc(mag_summed, 1)

                if o == 1:
                    pe.wait_ge(spec_step, SPEC_STEPS * (WT - 1) + 3)
                    pe.wait_ge(rnorm_ready, 1)
                taps(0, 0)
                taps(1, 1)
                taps(2, 0)
                magnitudes(0, 0, True, False)
                taps(3, 1)
                magnitudes(1, 1, False, False)
                with by_two(pe, 4, TT) as i:
                    taps(i, 0)
                    magnitudes(i - 2, 0, False, False)
                    taps(i + 1, 1)
                    magnitudes(i - 1, 1, False, False)
                magnitudes(TT - 2, 0, False, False)
                magnitudes(TT - 1, 1, False, True)

                pe.wait_ge(mixed, TT * (o + 1))
                for wt in range(WT):
                    t = WT * o + wt
                    for r in range(2):
                        n = 2 * t + r
                        pe.wait_ge(table_loaded[n % 4], 16 * (n // 4 + 1))
                        if wt and r == 0:
                            pe.wait_ge(even_copied, t)
                        elif wt:
                            pe.wait_ge(spec_step, SPEC_STEPS * (t - 1) + 3)
                        for tt in range(TT // 2):
                            if wt == 0:
                                pe.wait_ge(lo_ready, TT * o + r * (TT // 2) + tt + 1)
                            for cs in range(2):
                                last = three_pass(nc, [chip.bank(2 * r + cs)], table[n % 4][:, tt, cs, 0, :],
                                                  table[n % 4][:, tt, cs, 1, :], [tap_hi[:, cs, r * (TT // 2) + tt, :]],
                                                  [tap_lo[:, cs, r * (TT // 2) + tt, :]], tt == 0, tt == TT // 2 - 1)
                        last.then_inc(table_used, 1)

        @block.scalar
        def _(act):
            def copy_x(i):
                act.wait_ge(x_turned, i + 1)
                nc.scalar.activation(xT[:, :, i * P:(i + 1) * P], chip.pair(2 + i % 2).rearrange("p (k t) -> p k t", k=KT),
                                     ACT.Copy).then_inc(x_copied, 1)

            def sin_layer(layer):
                act.wait_ge(step, 7 * (layer + 1))
                nc.scalar.activation((h1, h2)[layer][:, :], arg[:, :], ACT.Sin).then_inc(sine, 1)

            for i in range(TT):
                copy_x(i)
                if i == 3:
                    sin_layer(0)
            for k in range(KT):
                if k == 4:
                    sin_layer(1)
                norm.square(act, k, x_copied, TT)
            norm.root_of_mean(act)
            for o in range(2):
                def tap(i, slot, o=o):
                    u = TT * o + i
                    act.wait_ge(mixed, u + 1)
                    nc.scalar.activation(at_tile(tap_hi, i), mixd[slot][:, :, :], ACT.Copy).then_inc(hi_ready, 1)
                    if later(o, i, 2):
                        act.wait_ge(mag_ready, u - 1)
                    nc.scalar.activation(absd[slot][:, :, :], mixd[slot][:, :, :], ACT.Abs).then_inc(absed, 1)
                if o == 1:
                    act.wait_ge(table_used, UNITS)
                tap_tiles(act, tap)

                for wt in range(WT):
                    t = WT * o + wt
                    act.wait_ge(table_used, 2 * t + 1)
                    if t:
                        act.wait_ge(spec_step, SPEC_STEPS * (t - 1) + 3)
                    nc.scalar.activation(even[:, :, :], chip.pair(0).rearrange("p (a c) -> p a c", a=2),
                                         ACT.Copy).then_inc(even_copied, 1)

        @block.vector
        def _(dve):
            for layer in range(2):
                at = 7 * layer
                dve.wait_ge(linear, layer + 1)
                if layer:
                    dve.wait_ge(sine, 1)
                nc.vector.tensor_scalar(arg[:, :], chip.pair(layer, HID), chip.fcol[:, layer:layer + 1],
                                        chip.fcol[:, 2:3], ALU.add, ALU.mult).then_inc(step, 1)
                dve.wait_ge(step, at + 1)
                nc.vector.tensor_scalar(turn[:, :], arg[:, :], turns, big, ALU.mult, ALU.add).then_inc(step, 1)
                dve.wait_ge(step, at + 2)
                nc.vector.tensor_scalar(turn[:, :], turn[:, :], big, None, ALU.subtract).then_inc(step, 1)
                for k, part in enumerate((c1, c2, c3)):
                    dve.wait_ge(step, at + 3 + k)
                    nc.vector.scalar_tensor_tensor(out=arg[:, :], in0=turn[:, :], scalar=-part, in1=arg[:, :],
                                                   op0=ALU.mult, op1=ALU.add).then_inc(step, 1)
                dve.wait_ge(step, at + 6)
                nc.vector.tensor_scalar(arg[:, :], arg[:, :], -pi, pi, ALU.max, ALU.min).then_inc(step, 1)

            dve.wait_ge(decay_loaded, 16)
            dve.wait_ge(sine, 2)
            dve.wait_ge(x_turned, TT)
            for o in range(2):
                def mix(i, slot, o=o):
                    u = TT * o + i
                    dve.wait_ge(taps_out, u + 1)
                    if later(o, i, 2):
                        dve.wait_ge(lo_ready, u - 1)
                        dve.wait_ge(absed, u - 1)
                    dec = decay[:, ds(i, 1), :].to_broadcast([P, 2, C])
                    done = nc.vector.tensor_tensor(mixd[slot][:, :, :], chip.pair(slot).rearrange("p (m c) -> p m c", m=2),
                                                   dec, ALU.mult)
                    if isinstance(i, int) and i == 0:
                        done.then_inc(edge, 1)
                        dve.wait_ge(edge, 3 * o + 1)
                        first = mixd[slot][0:1, :, :]
                        nc.vector.tensor_tensor(first[:, 0, :], first[:, 0, :], first[:, 1, :], ALU.add).then_inc(edge, 1)
                        dve.wait_ge(edge, 3 * o + 2)
                        nc.vector.tensor_scalar(first[:, 0, :], first[:, 0, :], 0.5, None, ALU.mult).then_inc(edge, 1)
                        dve.wait_ge(edge, 3 * o + 3)
                        nc.vector.tensor_copy(first[:, 1, :], first[:, 0, :]).then_inc(mixed, 1)
                    else:
                        done.then_inc(mixed, 1)

                def low(i, slot, o=o):
                    dve.wait_ge(mixed, TT * o + i + 1)
                    dve.wait_ge(hi_ready, TT * o + i + 1)
                    nc.vector.tensor_tensor(at_tile(tap_lo, i), mixd[slot][:, :, :], at_tile(tap_hi, i).bitcast(F32),
                                            ALU.subtract).then_inc(lo_ready, 1)

                def magnitude(i, slot, o=o):
                    dve.wait_ge(absed, TT * o + i + 1)
                    if later(o, i, 2):
                        dve.wait_ge(mag_summed, TT * o + i - 1)
                    nc.vector.tensor_tensor(mag[slot][:, :], absd[slot][:, 0, :], absd[slot][:, 1, :],
                                            ALU.max).then_inc(mag_ready, 1)

                mix(0, 0)
                mix(1, 1)
                low(0, 0)
                magnitude(0, 0)
                with by_two(dve, 2, TT) as i:
                    mix(i, 0)
                    low(i - 1, 1)
                    magnitude(i - 1, 1)
                    mix(i + 1, 1)
                    low(i, 0)
                    magnitude(i, 0)
                low(TT - 1, 1)
                magnitude(TT - 1, 1)
                dve.wait_ge(mag_summed, TT * (o + 1))
                if o == 1:
                    dve.wait_ge(spec_step, SPEC_STEPS * WT)
                nc.vector.reciprocal(rnorm[:, :], chip.bank(7)).then_inc(rnorm_ready, 1)
                dve.wait_ge(rnorm_ready, o + 1)
                if o == 0:
                    dve.wait_ge(skip_loaded, 16)

                for wt in range(WT):
                    t = WT * o + wt
                    at = SPEC_STEPS * t
                    dve.wait_ge(even_copied, t + 1)
                    dve.wait_ge(table_used, 2 * t + 2)
                    if t:
                        dve.wait_ge(spec_stored, 16 * t)
                    nc.vector.tensor_tensor(spec[:, 0:2, :], even[:, :, :],
                                            chip.pair(1).rearrange("p (a c) -> p a c", a=2), ALU.add).then_inc(spec_step, 1)
                    nc.vector.tensor_tensor(spec[:, 2, :], even[:, 0, :], chip.bank(2), ALU.subtract).then_inc(spec_step, 1)
                    nc.vector.tensor_tensor(spec[:, 3, :], chip.bank(3), even[:, 1, :], ALU.subtract).then_inc(spec_step, 1)
                    dve.wait_ge(spec_step, at + 3)
                    nc.vector.tensor_tensor(spec[:, :, :], spec[:, :, :],
                                            rnorm[:, :].unsqueeze(1).to_broadcast([P, 4, C]), ALU.mult).then_inc(spec_step, 1)
                    dve.wait_ge(spec_step, at + 4)
                    nc.vector.tensor_tensor(spec[:, 0:3:2, :], spec[:, 0:3:2, :],
                                            skip[:, o, :].unsqueeze(1).to_broadcast([P, 2, C]), ALU.add).then_inc(spec_step, 1)
                    if t == 0:
                        norm.invert(dve)


class Ffn:
    STEPS = FFN // (2 * P)

    def __init__(self, chip, tag, w_gate, w_up, w_down, xT, norm, kb):
        self.chip, self.nc, self.xT, self.norm = chip, chip.nc, xT, norm
        self.w_in = (w_gate, w_up)
        self.w_down = w_down
        self.wgu = [[[chip.at(f"{tag}_w{m}{s}{hl}", kb["wgu"] + 16 * s + 8 * m + 4 * hl, [P, KT, P], F32R) for hl in range(2)]
                     for m in range(2)] for s in range(2)]
        self.wd = [chip.at(f"{tag}_wd{hl}", kb["wd"] + 8 * hl, [P, 2, D], F32R) for hl in range(2)]
        self.gu_raw = [chip.at(f"{tag}_gu_raw{m}", kb["gu_raw"][m], [P, KT, 2 * P]) for m in range(2)]
        self.d_raw = chip.at(f"{tag}_d_raw", kb["d_raw"], [P, 2, D])
        self.h = [[chip.at(f"{tag}_h{g}{hl}", kb["h"] + 16 * g + 8 * hl, [P, 2, SEQ], F32R) for hl in range(2)]
                  for g in range(2)]
        self.h_whole = [chip.at(f"{tag}_h_whole{g}", kb["h"] + 16 * g + 8, [P, 2, SEQ]) for g in range(2)]
        self.gu_loaded, self.d_loaded = chip.sem(f"{tag}_gu_loaded"), chip.sem(f"{tag}_d_loaded")
        self.gu_hi, self.gu_ready = chip.sem(f"{tag}_gu_hi"), chip.sem(f"{tag}_gu_ready")
        self.d_hi, self.d_ready = chip.sem(f"{tag}_d_hi"), chip.sem(f"{tag}_d_ready")
        self.gate_done, self.up_done = chip.sem(f"{tag}_gate_done"), chip.sem(f"{tag}_up_done")
        self.gate_scaled, self.silu_done = chip.sem(f"{tag}_gate_scaled"), chip.sem(f"{tag}_silu_done")
        self.silu_scaled, self.h_made = chip.sem(f"{tag}_silu_scaled"), chip.sem(f"{tag}_h_made")
        self.h_hi, self.h_ready = chip.sem(f"{tag}_h_hi"), chip.sem(f"{tag}_h_ready")
        self.d_done, self.y_added = chip.sem(f"{tag}_d_done"), chip.sem(f"{tag}_y_added")

    def load_gu(self, sp, g, which=(0, 1)):
        for m in which:
            sp.dma_start(self.gu_raw[m][:], self.w_in[m].rearrange("(k p) f -> p k f", p=P)[:, :, ds(g * 2 * P, 2 * P)]
                         ).then_inc(self.gu_loaded, 16)

    def load_d(self, sp, g):
        sp.dma_start(self.d_raw[:], self.w_down[ds(g * 2 * P, 2 * P), :].rearrange("(a p) d -> p a d", p=P)
                     ).then_inc(self.d_loaded, 16)

    def round_gu(self, act, g, s, which=(0, 1)):
        for m in which:
            if m == 0 and s == 0:
                act.wait_ge(self.gu_loaded, 32 * (g + 1))
            if m == 0 and not (isinstance(g, int) and g == 0):
                act.wait_ge(self.up_done, 2 * (g - 1) + s + 1)
            self.nc.scalar.activation(self.wgu[s][m][0][:, :, :], self.gu_raw[m][:, :, s * P:(s + 1) * P],
                                      ACT.Copy).then_inc(self.gu_hi, 1)

    def rest_gu(self, dve, g, s, which=(0, 1)):
        for m in which:
            dve.wait_ge(self.gu_hi, 4 * g + 2 * s + m + 1)
            self.nc.vector.tensor_tensor(self.wgu[s][m][1][:, :, :], self.gu_raw[m][:, :, s * P:(s + 1) * P],
                                         self.wgu[s][m][0][:, :, :].bitcast(F32), ALU.subtract).then_inc(self.gu_ready, 1)

    def loop(self, eng, step):
        step(0, 0)
        step(1, 1)
        with by_two(eng, 2, self.STEPS - 1) as g:
            step(g, 0)
            step(g + 1, 1)
        step(self.STEPS - 1, 0)
        step(self.STEPS, 1)

    def run(self, split_here, after=None):
        nc, chip, STEPS, norm = self.nc, self.chip, self.STEPS, self.norm
        x_hi, x_lo, xT = norm.hi, norm.lo, self.xT

        def at_first(g):
            return isinstance(g, int) and g == 0

        def is_tail(g):
            return isinstance(g, int) and g == STEPS

        def has_next(g):
            return not (isinstance(g, int) and g >= STEPS - 1)

        with nc.Block() as block:
            @block.sync
            def _(sp):
                def step(g, slot):
                    if has_next(g):
                        sp.wait_ge(self.gu_ready, 4 * (g + 1))
                        self.load_gu(sp, g + 1)
                        sp.wait_ge(self.d_ready, 2 * (g + 1))
                        self.load_d(sp, g + 1)
                self.load_d(sp, 0)
                self.loop(sp, step)
                if after is not None:
                    sp.wait_ge(self.d_ready, 2 * STEPS)
                    for n in range(2):
                        after.weights.load(sp, n, n, n * P)

            @block.tensor
            def _(pe):
                def gate_up(g, s):
                    n = 2 * g + s
                    for m in range(2):
                        pe.wait_ge(self.gu_ready, 4 * g + 2 * s + m + 1)
                        if not (at_first(g) and s == 0):
                            pe.wait_ge((self.gate_scaled, self.h_made)[m], n)
                        elif m == 1:
                            pe.wait_ge(norm.rooted, 1)
                        for k in range(KT):
                            if split_here and m == 0 and s == 0 and at_first(g):
                                pe.wait_ge(norm.lo_ready, k + 1)
                            last = three_pass(nc, [chip.bank(2 * m), chip.bank(2 * m + 1)], self.wgu[s][m][0][:, k, :],
                                              self.wgu[s][m][1][:, k, :], halves(x_hi, k), halves(x_lo, k),
                                              k == 0, k == KT - 1)
                        last.then_inc((self.gate_done, self.up_done)[m], 1)

                def down(g, slot, part):
                    h_hi, h_lo = self.h[slot]
                    if part == 0:
                        pe.wait_ge(self.d_ready, 2 * (g + 1))
                        pe.wait_ge(self.h_ready, 2 * (g + 1))
                    for d in range(4 * part, 4 * part + 4):
                        if not (isinstance(g, int) and g == 0 and d < 2):
                            pe.wait_ge(self.y_added, KT * g + d - 1)
                        for a in range(2):
                            last = three_pass(nc, [chip.bank(4 + 2 * (d % 2)), chip.bank(5 + 2 * (d % 2))],
                                              self.wd[0][:, a, d * P:(d + 1) * P], self.wd[1][:, a, d * P:(d + 1) * P],
                                              halves(h_hi, a), halves(h_lo, a), a == 0, a == 1)
                        last.then_inc(self.d_done, 1)
                        if isinstance(g, int) and g == STEPS - 1 and after is not None and d >= 4 and d % 2:
                            after.norm.tensor(pe, d - 5)

                def step(g, slot):
                    if not is_tail(g):
                        gate_up(g, 0)
                    if not at_first(g):
                        down(g - 1, 1 - slot, 0)
                    if not is_tail(g):
                        gate_up(g, 1)
                    if not at_first(g):
                        down(g - 1, 1 - slot, 1)
                self.loop(pe, step)
                if after is not None:
                    for k in (KT - 4, KT - 2, KT - 1):
                        after.norm.tensor(pe, k)

            @block.scalar
            def _(act):
                def round_d(g):
                    act.wait_ge(self.d_loaded, 16 * (g + 1))
                    if not at_first(g):
                        act.wait_ge(self.d_done, KT * g)
                    for a in range(2):
                        nc.scalar.activation(self.wd[0][:, a, :], self.d_raw[:, a, :], ACT.Copy).then_inc(self.d_hi, 1)

                def hidden(g, s, slot):
                    n = 2 * g + s
                    h_hi, h = self.h[slot][0][:, s, :], self.h_whole[slot][:, s, :]
                    act.wait_ge(self.gate_scaled, n + 1)
                    nc.scalar.activation(h, h, ACT.Silu).then_inc(self.silu_done, 1)
                    act.wait_ge(self.h_made, n + 1)
                    if not isinstance(g, int) or g >= 2:
                        act.wait_ge(self.d_done, KT * (g - 1))
                    nc.scalar.activation(h_hi, h, ACT.Copy).then_inc(self.h_hi, 1)

                if split_here:
                    self.round_gu(act, 0, 0, (0,))
                    for k in range(KT):
                        if k == KT - 2:
                            act.wait_ge(chip.spec_stored, 16 * 2 * WT)
                        norm.round(act, k)
                        if k == KT // 2:
                            self.round_gu(act, 0, 0, (1,))
                else:
                    norm.root_of_mean(act)
                    self.round_gu(act, 0, 0)
                self.round_gu(act, 0, 1)

                def step(g, slot):
                    if not at_first(g):
                        round_d(g - 1)
                    if is_tail(g):
                        return
                    for s in range(2):
                        hidden(g, s, slot)
                        if has_next(g):
                            self.round_gu(act, g + 1, s)
                self.loop(act, step)
                if after is not None:
                    act.wait_ge(self.up_done, 2 * STEPS)
                    act.wait_ge(self.gu_ready, 4 * STEPS)
                    for k in range(KT):
                        after.norm.scalar(act, k, self.y_added, KT * (STEPS - 1) + k + 1)
                        if k in (1, 3):
                            after.weights.round(act, k // 2, k // 2)

            @block.gpsimd
            def _(pool):
                if after is not None:
                    after.norm.gpsimd(pool)

            @block.vector
            def _(dve):
                def rest_d(g):
                    for a in range(2):
                        dve.wait_ge(self.d_hi, 2 * g + a + 1)
                        nc.vector.tensor_tensor(self.wd[1][:, a, :], self.d_raw[:, a, :], self.wd[0][:, a, :].bitcast(F32),
                                                ALU.subtract).then_inc(self.d_ready, 1)

                def add(g, d):
                    dve.wait_ge(self.d_done, KT * g + d + 1)
                    if not (isinstance(g, int) and g == 0):
                        dve.wait_ge(self.y_added, KT * g + d + 1 - KT)
                    nc.vector.scalar_tensor_tensor(out=xT[:, d, :], in0=chip.pair(2 + d % 2), scalar=0.5,
                                                   in1=xT[:, d, :], op0=ALU.mult, op1=ALU.add).then_inc(self.y_added, 1)

                def scale_gate(g, s, slot):
                    n = 2 * g + s
                    dve.wait_ge(self.gate_done, n + 1)
                    if not isinstance(g, int) or g >= 2:
                        dve.wait_ge(self.d_done, KT * (g - 1))
                    nc.vector.tensor_tensor(self.h_whole[slot][:, s, :], chip.pair(0), norm.rstd[:, :],
                                            ALU.mult).then_inc(self.gate_scaled, 1)

                def make_h(g, s, slot):
                    n = 2 * g + s
                    h = self.h_whole[slot][:, s, :]
                    dve.wait_ge(self.silu_done, n + 1)
                    nc.vector.tensor_tensor(h, h, norm.rstd[:, :], ALU.mult).then_inc(self.silu_scaled, 1)
                    dve.wait_ge(self.silu_scaled, n + 1)
                    dve.wait_ge(self.up_done, n + 1)
                    nc.vector.tensor_tensor(h, h, chip.pair(1), ALU.mult).then_inc(self.h_made, 1)

                def rest_h(g, s, slot):
                    n = 2 * g + s
                    dve.wait_ge(self.h_made, n + 1)
                    dve.wait_ge(self.h_hi, n + 1)
                    nc.vector.tensor_tensor(self.h[slot][1][:, s, :], self.h_whole[slot][:, s, :], self.h[slot][0][:, s, :].bitcast(F32),
                                            ALU.subtract).then_inc(self.h_ready, 1)

                if split_here:
                    self.rest_gu(dve, 0, 0, (0,))
                    for k in range(KT):
                        norm.vector(dve, k)
                        if k == KT // 2 + 1:
                            self.rest_gu(dve, 0, 0, (1,))
                else:
                    self.rest_gu(dve, 0, 0)
                    norm.invert(dve)
                self.rest_gu(dve, 0, 1)

                def step(g, slot):
                    if not at_first(g):
                        rest_d(g - 1)
                    for s in range(2):
                        if is_tail(g):
                            for d in range(4 * s, 4 * s + 4):
                                add(g - 1, d)
                                if after is not None and d:
                                    after.norm.vector(dve, d - 1)
                                    if d in (3, 5):
                                        after.weights.rest(dve, d // 4, d // 4)
                            continue
                        scale_gate(g, s, slot)
                        make_h(g, s, slot)
                        if not at_first(g):
                            add(g - 1, 4 * s)
                        rest_h(g, s, slot)
                        if not at_first(g):
                            add(g - 1, 4 * s + 1)
                        if has_next(g):
                            self.rest_gu(dve, g + 1, s)
                        if not at_first(g):
                            add(g - 1, 4 * s + 2)
                            add(g - 1, 4 * s + 3)
                    if is_tail(g) and after is not None:
                        after.norm.vector(dve, KT - 1)
                self.loop(dve, step)


class ColumnWeights:

    def __init__(self, chip, tag, weights, raw_kb, split_kb):
        self.chip, self.nc, self.weights = chip, chip.nc, weights
        self.raw = [chip.at(f"{tag}_raw{s}", raw_kb + 4 * s, [P, KT, P]) for s in range(2)]
        self.split = [[chip.at(f"{tag}_split{s}{hl}", split_kb + 8 * s + 4 * hl, [P, KT, P], F32R) for hl in range(2)]
                      for s in range(2)]
        self.loaded = [chip.sem(f"{tag}_loaded{s}") for s in range(2)]
        self.hi, self.ready, self.used = chip.sem(f"{tag}_hi"), chip.sem(f"{tag}_ready"), chip.sem(f"{tag}_used")

    def load(self, sp, n, slot, col, cols=P):
        sp.dma_start(self.raw[slot][:, :, 0:cols],
                     self.weights.rearrange("(k p) c -> p k c", p=P)[:, :, ds(col, cols)]).then_inc(self.loaded[slot], 16)

    def round(self, act, n, slot, cols=P):
        act.wait_ge(self.loaded[slot], 8 * (n - slot) + 16)
        if not isinstance(n, int) or n >= 2:
            act.wait_ge(self.used, n - 1)
        self.nc.scalar.activation(self.split[slot][0][:, :, 0:cols], self.raw[slot][:, :, 0:cols], ACT.Copy).then_inc(self.hi, 1)

    def rest(self, dve, n, slot, cols=P):
        dve.wait_ge(self.hi, n + 1)
        self.nc.vector.tensor_tensor(self.split[slot][1][:, :, 0:cols], self.raw[slot][:, :, 0:cols],
                                     self.split[slot][0][:, :, 0:cols].bitcast(F32), ALU.subtract).then_inc(self.ready, 1)

    def product(self, pe, n, slot, outs, x_hi, x_lo, done, cols=P):
        pe.wait_ge(self.ready, n + 1)
        for k in range(KT):
            last = three_pass(self.nc, outs, self.split[slot][0][:, k, 0:cols], self.split[slot][1][:, k, 0:cols],
                              halves(x_hi, k), halves(x_lo, k), k == 0, k == KT - 1)
        last.then_inc(self.used, 1)


HEAD_TILES = 4
HY_TILES = 3 * C // P


class MixerInput:

    def __init__(self, norm, weights):
        self.norm, self.weights = norm, weights


def mixer_in_block(chip, xT, residual, w, norm, cq, ckv, kr, v_hi, v_lo, gates, conv_w, conv_b, hyena):
    nc = chip.nc
    x_hi, x_lo, rstd = norm.hi, norm.lo, norm.rstd
    spilled = chip.sem("m_spilled")
    padded = [chip.at(f"m_padded{s}", 144 + 4.25 * s, [P, SEQ + 2]) for s in range(2)]
    conv = [chip.at(f"m_conv{s}", 184 + 4 * s, [P, SEQ]) for s in range(2)]
    s = chip.sem
    evacuated, pads, conv_step = s("m_evacuated"), s("m_pads"), s("m_conv_step")
    kr_copied = s("m_kr_copied")
    turned, v_rounded, settled = s("m_turned"), s("m_v_rounded"), s("m_settled")
    HY0 = HEAD_TILES
    N = HEAD_TILES + HY_TILES

    def col(n):
        return n * P if n < 3 else Q_RANK + KV_RANK

    with nc.Block() as block:
        @block.sync
        def _(sp):
            sp.dma_start(residual, xT[:]).then_inc(spilled, 16)
            hyena.load_table(sp, 0)
            for n in range(2, HEAD_TILES):
                sp.wait_ge(w.ready, n - 1)
                w.load(sp, n, n % 2, col(n), ROPE if n == 3 else P)
            with by_two(sp, 0, HY_TILES) as j:
                for a in range(2):
                    sp.wait_ge(w.ready, HY0 + j + a - 1)
                    w.load(sp, HY0 + j + a, a, (j + a) * P + (Q_RANK + KV_RANK + ROPE))
            sp.wait_ge(spilled, 16)

        @block.tensor
        def _(pe):
            for n in range(HEAD_TILES):
                cols = ROPE if n == 3 else P
                if n >= 2:
                    pe.wait_ge(evacuated, n - 1)
                elif n == 1:
                    pe.wait_ge(norm.rooted, 1)
                w.product(pe, n, n % 2, [chip.bank(2 * (n % 2), cols), chip.bank(2 * (n % 2) + 1, cols)],
                          x_hi, x_lo, None, cols)

            def product(j, slot):
                pe.wait_ge(evacuated, HY0 + j - 1)
                w.product(pe, HY0 + j, slot, [chip.bank(2 * slot), chip.bank(2 * slot + 1)], x_hi, x_lo, None)

            def turn(j, slot):
                pe.wait_ge(conv_step, 3 * (j + 1))
                if not isinstance(j, int) or j >= 2:
                    pe.wait_ge(settled, j - 1)
                for i in range(TT):
                    start = (i // 4) + 2 * P * (i % 4)
                    at = (2 + slot) * 2 * HALF + i * P
                    last = nc.tensor.transpose(chip.ps[:, at:at + P], conv[slot][:, start:start + 2 * P - 1:2],
                                               chip.ident[:, :])
                last.then_inc(turned, 1)

            product(0, 0)
            for j in range(1, 4):
                product(j, j % 2)
                turn(j - 1, (j - 1) % 2)
            with by_two(pe, 4, HY_TILES) as j:
                product(j, 0)
                turn(j - 1, 1)
                product(j + 1, 1)
                turn(j, 0)
            turn(HY_TILES - 1, 1)

        @block.scalar
        def _(act):
            norm.root_of_mean(act)
            for n in range(1, HEAD_TILES):
                w.round(act, n + 1, (n + 1) % 2, ROPE if n + 1 == 3 else P)
            act.wait_ge(w.used, HEAD_TILES)
            nc.scalar.activation(kr[NOPE:QK, :], chip.pair(1, ROPE), ACT.Copy).then_inc(kr_copied, 1)
            act.wait_ge(spilled, 16)

            def round_v(j, slot):
                act.wait_ge(turned, j + 1)
                nc.scalar.activation(v_hi[:, :, j * P:(j + 1) * P], chip.pair(2 + slot).rearrange("p (i c) -> p i c", i=TT),
                                     ACT.Copy).then_inc(v_rounded, 1)

            for j in range(C // P + 2):
                w.round(act, HY0 + j + 1, 1 - j % 2)
                if 1 <= j <= C // P:
                    round_v(j - 1, (j - 1) % 2)
            with by_two(act, C // P + 2, HY_TILES - 2) as j:
                w.round(act, HY0 + j + 1, 1)
                w.round(act, HY0 + j + 2, 0)
            w.round(act, N - 1, 1)

        @block.vector
        def _(dve):
            for k in range(2):
                nc.vector.memset(padded[k][:, 0:1], 0.0).then_inc(pads, 1)
                nc.vector.memset(padded[k][:, SEQ + 1:SEQ + 2], 0.0).then_inc(pads, 1)
            norm.invert(dve)
            for n in range(HEAD_TILES):
                if n:
                    w.rest(dve, n + 1, (n + 1) % 2, ROPE if n + 1 == 3 else P)
                dve.wait_ge(w.used, n + 1)
                if n == 3:
                    dve.wait_ge(kr_copied, 1)
                    nc.vector.tensor_tensor(kr[NOPE:QK, :], kr[NOPE:QK, :], rstd[NOPE:QK, :],
                                            ALU.mult).then_inc(evacuated, 1)
                else:
                    dst = (cq[:, 0, :], cq[:, 1, :], ckv[:, 0, :])[n]
                    nc.vector.tensor_tensor(dst, chip.pair(n % 2), rstd[:, :], ALU.mult).then_inc(evacuated, 1)
            dve.wait_ge(pads, 4)

            def convolve(j, slot):
                dve.wait_ge(w.used, HY0 + j + 1)
                if not isinstance(j, int) or j >= 2:
                    dve.wait_ge(conv_step, 3 * (j - 1))
                nc.vector.tensor_tensor(padded[slot][:, 1:SEQ + 1], chip.pair(slot), rstd[:, :],
                                        ALU.mult).then_inc(evacuated, 1)
                dve.wait_ge(evacuated, HY0 + j + 1)
                if not isinstance(j, int) or j >= 2:
                    dve.wait_ge(turned, j - 1)
                taps = [conv_w[:, tap, ds(j, 1)] for tap in range(3)]
                nc.vector.tensor_scalar(conv[slot][:, :], padded[slot][:, 0:SEQ], taps[0], conv_b[:, ds(j, 1)],
                                        ALU.mult, ALU.add).then_inc(conv_step, 1)
                for tap in (1, 2):
                    dve.wait_ge(conv_step, 3 * j + tap)
                    nc.vector.scalar_tensor_tensor(out=conv[slot][:, :], in0=padded[slot][:, tap:tap + SEQ],
                                                   scalar=taps[tap], in1=conv[slot][:, :], op0=ALU.mult,
                                                   op1=ALU.add).then_inc(conv_step, 1)

            def tokens(slot):
                return chip.pair(2 + slot).rearrange("p (i c) -> p i c", i=TT)

            def v_low(j, slot):
                dve.wait_ge(v_rounded, j + 1)
                nc.vector.tensor_tensor(v_lo[:, :, ds(j * P, P)], tokens(slot),
                                        v_hi[:, :, ds(j * P, P)].bitcast(F32), ALU.subtract).then_inc(settled, 1)

            def gate(j, slot, dst):
                dve.wait_ge(turned, j + 1)
                nc.vector.tensor_copy(dst, tokens(slot)).then_inc(settled, 1)

            def step(group, k, slot):
                j = group * (C // P) + k
                if not (isinstance(j, int) and j >= HY_TILES - 2):
                    w.rest(dve, HY0 + j + 2, slot)
                if not (isinstance(j, int) and j == HY_TILES - 1):
                    convolve(j + 1, 1 - slot)
                if group == 0:
                    v_low(j, slot)
                else:
                    gate(j, slot, gates[group - 1][:, :, ds(k * P, P)])

            w.rest(dve, HY0 + 1, 1)
            convolve(0, 0)
            for k in range(C // P):
                step(0, k, k % 2)
            with by_two(dve, 0, C // P) as k:
                step(1, k, 0)
                step(1, k + 1, 1)
            for k in range(C // P):
                step(2, k, k % 2)


class Hyena:
    ORDER = (("f", 0, 0), ("f", 0, 1), ("f", 1, 0), ("f", 1, 1), ("i", 0, 0), ("f", 2, 0), ("f", 2, 1), ("i", 0, 1),
             ("f", 3, 0), ("f", 3, 1), ("i", 0, 2), ("i", 1, 0), ("i", 1, 1), ("i", 1, 2), ("i", 0, 3), ("i", 1, 3))
    UNITS = len(ORDER)
    SLOTS = 3
    STEPS = 12

    def __init__(self, chip, dram):
        self.chip, self.nc, self.dram = chip, chip.nc, dram
        self.table = [chip.at(f"y_table{k}", kb, [P, TT // 2, 2, 2, P], F32R) for k, kb in enumerate((192, 144, 152))]
        self.table_loaded = [chip.sem(f"y_table_loaded{k}") for k in range(self.SLOTS)]

    def load_table(self, sp, n):
        kind, a, b = self.ORDER[n % self.UNITS]
        row = (a * (2 if kind == "f" else WT) + b) * P
        src = self.dram["fwd" if kind == "f" else "inv"]
        sp.dma_start(self.table[n % self.SLOTS][:].bitcast(F32), src[row:row + P, :]).then_inc(
            self.table_loaded[n % self.SLOTS], 16)

    def run(self, v_hi, v_lo, gates):
        chip, nc, dram, UNITS, STEPS = self.chip, self.nc, self.dram, self.UNITS, self.STEPS
        spec_hi = chip.at("y_spec_hi", 32, [P, 4, WT, C], F32R)
        spec_lo = chip.at("y_spec_lo", 64, [P, 4, WT, C], F32R)
        filt = chip.at("y_filt", 160, [P, 4, C])
        even = chip.at("y_even", 168, [P, 2, C])
        work = chip.at("y_work", 172, [P, 8, C])
        z = chip.at("y_z", 188, [P, 2, C])
        s = chip.sem
        filt_loaded, table_used, even_copied, work_step = (s("y_filt_loaded"), s("y_table_used"), s("y_even_copied"),
                                                           s("y_work_step"))
        spec_hi_ready, spec_lo_ready = s("y_spec_hi_ready"), s("y_spec_lo_ready")
        out_ready, z_made, z_hi, z_lo = s("y_out_ready"), s("y_z_made"), s("y_z_hi"), s("y_z_lo")

        def after_unit(q, *unit):
            return UNITS * q + self.ORDER.index(unit) + 1

        def out_bank(i):
            return chip.bank(4 + i if i < TT // 2 else i - TT // 2)

        with nc.Block() as block:
            @block.sync
            def _(sp):
                def load_filter(n):
                    if n:
                        sp.wait_ge(work_step, STEPS * (n - 1) + 6)
                    else:
                        sp.wait_ge(chip.spec_stored, 16 * 2 * WT)
                    sp.dma_start(filt[:], dram["spectra"][n * P:(n + 1) * P, :]).then_inc(filt_loaded, 16)

                self.load_table(sp, 1)
                load_filter(0)
                self.load_table(sp, 2)
                for n in range(self.SLOTS, 2 * UNITS):
                    sp.wait_ge(table_used, n - self.SLOTS + 1)
                    self.load_table(sp, n)
                    for tile in range(1, 2 * WT):
                        q, wt = divmod(tile - 1, WT)
                        if n == after_unit(q, "f", wt, 1) + self.SLOTS:
                            load_filter(tile)

            @block.tensor
            def _(pe):
                def forward(q, wt, r, table):
                    if q and wt == 0:
                        pe.wait_ge(z_made, TT - 2 + 2 * r)
                    elif wt and r == 0:
                        pe.wait_ge(even_copied, WT * q + wt)
                    elif wt:
                        pe.wait_ge(work_step, STEPS * (WT * q + wt - 1) + 3)
                    for tt in range(TT // 2):
                        i = r * (TT // 2) + tt
                        if q and wt == 0:
                            pe.wait_ge(z_lo, i + 1)
                        for cs in range(2):
                            last = three_pass(nc, [chip.bank(2 * r + cs)], table[:, tt, cs, 0, :], table[:, tt, cs, 1, :],
                                              [v_hi[:, i, :]], [v_lo[:, i, :]], tt == 0, tt == TT // 2 - 1)
                    last.then_inc(table_used, 1)

                def inverse(q, r, wt, table):
                    if r and wt == 0:
                        pe.wait_ge(work_step, STEPS * (WT * q + WT - 1) + 3)
                    elif q and wt == 0:
                        pe.wait_ge(z_made, TT)
                    pe.wait_ge(spec_lo_ready, 2 * (WT * q + wt + 1))
                    for tt in range(TT // 2):
                        for cs in range(2):
                            kind = r + 2 * (1 - cs)
                            last = three_pass(nc, [out_bank(r * (TT // 2) + tt)], table[:, tt, cs, 0, :],
                                              table[:, tt, cs, 1, :], [spec_hi[:, kind, wt, :]], [spec_lo[:, kind, wt, :]],
                                              wt == 0 and cs == 0, wt == WT - 1 and cs == 1)
                        if wt == WT - 1 and tt < TT // 2 - 1:
                            last.then_inc(out_ready, 1)
                    last.then_inc(table_used, 1)

                for n in range(2 * UNITS):
                    kind, a, b = self.ORDER[n % UNITS]
                    pe.wait_ge(self.table_loaded[n % self.SLOTS], 16 * (n // self.SLOTS + 1))
                    (forward if kind == "f" else inverse)(n // UNITS, a, b, self.table[n % self.SLOTS])

            @block.scalar
            def _(act):
                def copy_even(n):
                    q, wt = divmod(n, WT)
                    act.wait_ge(table_used, after_unit(q, "f", wt, 0))
                    if n:
                        act.wait_ge(work_step, STEPS * (n - 1) + 3)
                    nc.scalar.activation(even[:, :, :], chip.pair(0).rearrange("p (a c) -> p a c", a=2),
                                         ACT.Copy).then_inc(even_copied, 1)

                def round_product(n):
                    q, wt = divmod(n, WT)
                    if q:
                        act.wait_ge(table_used, UNITS)
                    for part in range(2):
                        act.wait_ge(work_step, STEPS * n + 10 + 2 * part)
                        nc.scalar.activation(spec_hi[:, 2 * part:2 * part + 2, wt, :],
                                             work[:, 4 * part + 1:4 * part + 4:2, :], ACT.Copy).then_inc(spec_hi_ready, 1)

                for q in range(2):
                    copy_even(WT * q)
                    for wt in range(1, WT):
                        copy_even(WT * q + wt)
                        round_product(WT * q + wt - 1)
                    round_product(WT * q + WT - 1)
                    if q == 0:
                        for i in range(TT):
                            act.wait_ge(z_made, i + 1)
                            nc.scalar.activation(v_hi[:, i, :], z[:, i % 2, :], ACT.Copy).then_inc(z_hi, 1)

            @block.vector
            def _(dve):
                def op(out, in0, in1, alu):
                    nc.vector.tensor_tensor(out, in0, in1, alu).then_inc(work_step, 1)

                def multiply(n):
                    q, wt = divmod(n, WT)
                    at = STEPS * n
                    dve.wait_ge(even_copied, n + 1)
                    dve.wait_ge(table_used, after_unit(q, "f", wt, 1))
                    if n:
                        dve.wait_ge(spec_lo_ready, 2 * n)
                        dve.wait_ge(spec_hi_ready, 2 * n)
                    odd = chip.pair(1).rearrange("p (a c) -> p a c", a=2)
                    op(work[:, 0:2, :], even[:, :, :], odd, ALU.add)
                    op(work[:, 2, :], even[:, 0, :], chip.bank(2), ALU.subtract)
                    op(work[:, 3, :], chip.bank(3), even[:, 1, :], ALU.subtract)
                    dve.wait_ge(filt_loaded, 16 * (n + 1))
                    dve.wait_ge(work_step, at + 3)
                    op(work[:, 4:8, :], work[:, 0:4, :], filt[:, :, :], ALU.mult)
                    dve.wait_ge(work_step, at + 4)
                    op(work[:, 0:3:2, :], work[:, 0:3:2, :], filt[:, 1:4:2, :], ALU.mult)
                    op(work[:, 1:4:2, :], work[:, 1:4:2, :], filt[:, 0:3:2, :], ALU.mult)
                    dve.wait_ge(work_step, at + 6)
                    op(work[:, 0:3:2, :], work[:, 0:3:2, :], work[:, 1:4:2, :], ALU.add)
                    op(work[:, 4:7:2, :], work[:, 4:7:2, :], work[:, 5:8:2, :], ALU.subtract)
                    dve.wait_ge(work_step, at + 8)
                    op(work[:, 1, :], work[:, 0, :], work[:, 2, :], ALU.subtract)
                    op(work[:, 3, :], work[:, 0, :], work[:, 2, :], ALU.add)
                    op(work[:, 5, :], work[:, 4, :], work[:, 6, :], ALU.add)
                    op(work[:, 7, :], work[:, 4, :], work[:, 6, :], ALU.subtract)
                    dve.wait_ge(work_step, at + 12)
                    for part in range(2):
                        dve.wait_ge(spec_hi_ready, 2 * n + part + 1)
                        nc.vector.tensor_tensor(spec_lo[:, 2 * part:2 * part + 2, wt, :],
                                                work[:, 4 * part + 1:4 * part + 4:2, :],
                                                spec_hi[:, 2 * part:2 * part + 2, wt, :].bitcast(F32),
                                                ALU.subtract).then_inc(spec_lo_ready, 1)

                def z_low(i):
                    dve.wait_ge(z_made, i + 1)
                    dve.wait_ge(z_hi, i + 1)
                    nc.vector.tensor_tensor(v_lo[:, i, :], z[:, i % 2, :], v_hi[:, i, :].bitcast(F32),
                                            ALU.subtract).then_inc(z_lo, 1)

                for q in range(2):
                    for wt in range(WT):
                        multiply(WT * q + wt)
                    for i in range(TT):
                        r, tt = divmod(i, TT // 2)
                        if tt < TT // 2 - 1:
                            dve.wait_ge(out_ready, (TT - 2) * q + (TT // 2 - 1) * r + tt + 1)
                        else:
                            dve.wait_ge(table_used, after_unit(q, "i", r, WT - 1))
                        if q == 0:
                            if i >= 2:
                                dve.wait_ge(z_lo, i - 1)
                            nc.vector.tensor_tensor(z[:, i % 2, :], out_bank(i), gates[0][:, i, :],
                                                    ALU.mult).then_inc(z_made, 1)
                            if i:
                                z_low(i - 1)
                            if i == TT - 1:
                                z_low(i)
                        else:
                            nc.vector.tensor_tensor(gates[1][:, i, :], out_bank(i), gates[1][:, i, :],
                                                    ALU.mult).then_inc(z_made, 1)


def attention_block(chip, dram, cq, ckv, kr, attn):
    nc = chip.nc
    cq_hi, cq_lo = (chip.at(f"a_cq{h}", 8 * h, [P, 2, SEQ], F32R) for h in range(2))
    ckv_hi, ckv_lo = (chip.at(f"a_ckv{h}", 16 + 4 * h, [P, 1, SEQ], F32R) for h in range(2))
    v_all = chip.at("a_v_all", 24, [P, TT, HEADS * VD])
    v_head = [[chip.at(f"a_v{k}{h}", 40 + 4.5 * k + 2.25 * h, [P, TT, VD + 1], F32R) for h in range(2)] for k in range(2)]
    q_head = [[chip.at(f"a_q{k}{h}", 49 + 8 * k + 4 * h, [QK, SEQ], F32R) for h in range(2)] for k in range(2)]
    k_head = [[chip.at(f"a_k{k}{h}", 65 + 8 * k + 4 * h, [QK, SEQ], F32R) for h in range(2)] for k in range(2)]
    q_row = chip.at("a_q_row", 81, [QK, SEQ])
    swapped = chip.at("a_swapped", 85, [QK, SEQ])
    probs = [chip.at(f"a_probs{k}", 89 + 4 * k, [P, SEQ]) for k in range(2)]
    wq_raw = [chip.at(f"a_wq_raw{k}", 97 + 0.75 * k, [P, 2, QK]) for k in range(2)]
    wk_raw = [chip.at(f"a_wk_raw{k}", 98.5 + 0.25 * k, [P, NOPE]) for k in range(2)]
    wq = [[chip.at(f"a_wq{k}{h}", 99 + 1.5 * k + 0.75 * h, [P, 2, QK], F32R) for h in range(2)] for k in range(2)]
    wk = [[chip.at(f"a_wk{k}{h}", 102 + 0.5 * k + 0.25 * h, [P, NOPE], F32R) for h in range(2)] for k in range(2)]
    wv_raw = chip.at("a_wv_raw", 103, [P, HEADS * VD])
    wv = [chip.at(f"a_wv{h}", 105 + 2 * h, [P, HEADS * VD], F32R) for h in range(2)]
    out_t = [chip.at(f"a_out_t{k}", 109 + k, [VD + 1, 2 * P]) for k in range(2)]
    pt = [[chip.at(f"a_pt{k}{h}", 144 + 16 * k + 8 * h, [P, TT, 2 * P], F32R) for h in range(2)] for k in range(2)]
    cos_row = chip.at("a_cos_row", 176, [QK, SEQ])
    sin_row = chip.at("a_sin_row", 180, [QK, SEQ])
    squares, root, scaled = (chip.at("a_squares", 144, [P, 2, SEQ]), chip.at("a_root", 152, [P, SEQ]),
                             chip.at("a_scaled", 156, [P, 2, SEQ]))
    squares2, root2, scaled2 = (chip.at("a_squares2", 164, [P, 2, SEQ]), chip.at("a_root2", 172, [P, SEQ]),
                                chip.at("a_scaled2", 89, [P, 2, SEQ]))
    q_norm = FeatureNorm(chip, "aq", cq, Q_RANK // P, chip.q_gain, cq_hi, cq_lo, squares, root, scaled, 0)
    kv_norm = FeatureNorm(chip, "akv", ckv, KV_RANK // P, chip.kv_gain, ckv_hi, ckv_lo, squares2, root2, scaled2, 1)

    s = chip.sem
    ropes_loaded, wv_loaded, k_swapped = s("a_ropes_loaded"), s("a_wv_loaded"), s("a_k_swapped")
    w_loaded = [s(f"a_w_loaded{k}") for k in range(2)]
    wv_hi, wv_ready, v_out, v_stored = s("a_wv_hi"), s("a_wv_ready"), s("a_v_out"), s("a_v_stored")
    k_rope_step, rope_hi, rope_ready, ones_set = (s("a_k_rope_step"), s("a_rope_hi"), s("a_rope_ready"), s("a_ones_set"))
    w_hi, w_ready = s("a_w_hi"), s("a_w_ready")
    q_out, k_out = s("a_q_out"), s("a_k_out")
    q_rowed, q_swapped, q_roped = s("a_q_rowed"), s("a_q_swapped"), s("a_q_roped")
    q_hi, q_ready, k_hi, k_ready, v_hi, v_ready = (s("a_q_hi"), s("a_q_ready"), s("a_k_hi"), s("a_k_ready"),
                                                   s("a_v_hi"), s("a_v_ready"))
    scored, negmax, exped = s("a_scored"), s("a_negmax"), s("a_exped")
    maxed = s("a_maxed")
    turned, pt_hi, pt_ready = s("a_turned"), s("a_pt_hi"), s("a_pt_ready")
    weighted, out_copied, out_turned, out_stored = (s("a_weighted"), s("a_out_copied"), s("a_out_turned"),
                                                    s("a_out_stored"))
    R = slice(NOPE, QK)
    SCALE = QK ** -0.5
    T_Q, T_K = 1, 3

    def peeled(eng, step):
        step(0, 0)
        with by_two(eng, 1, HEADS - 1) as h:
            step(h, 1)
            step(h + 1, 0)
        step(HEADS - 1, 1)

    def is_last(h):
        return isinstance(h, int) and h == HEADS - 1

    def is_first(h):
        return isinstance(h, int) and h == 0

    with nc.Block() as block:
        @block.sync
        def _(sp):
            sp.dma_start(swapped[NOPE:NOPE + 16, :], kr[NOPE + 16:QK, :]).then_inc(k_swapped, 16)
            sp.dma_start(swapped[NOPE + 16:QK, :], kr[NOPE:NOPE + 16, :]).then_inc(k_swapped, 16)
            sp.dma_start(cos_row[R, :], dram["rope"][0:ROPE, :]).then_inc(ropes_loaded, 16)
            sp.dma_start(sin_row[R, :], dram["rope"][ROPE:2 * ROPE, :]).then_inc(ropes_loaded, 16)
            w_ukv = dram["w_ukv"].rearrange("k (h t d) -> k h t d", h=HEADS, t=2)
            sp.dma_start(wv_raw[:, :].rearrange("p (h d) -> p h d", h=HEADS), w_ukv[:, :, 1, :]).then_inc(wv_loaded, 16)

            def load(h, slot):
                sp.dma_start(wq_raw[slot][:], dram["w_uq"].rearrange("(k p) c -> p k c", p=P)[:, :, ds(h * QK, QK)]
                             ).then_inc(w_loaded[slot], 16)
                sp.dma_start(wk_raw[slot][:], dram["w_ukv"][:, ds(h * 2 * VD, NOPE)]).then_inc(w_loaded[slot], 16)

            def swap(h):
                sp.wait_ge(q_rowed, h + 1)
                if is_first(h):
                    sp.wait_ge(k_rope_step, 3)
                sp.dma_start(swapped[NOPE:NOPE + 16, :], q_row[NOPE + 16:QK, :]).then_inc(q_swapped, 16)
                sp.dma_start(swapped[NOPE + 16:QK, :], q_row[NOPE:NOPE + 16, :]).then_inc(q_swapped, 16)

            load(0, 0)
            load(1, 1)
            swap(0)

            def step(h, slot):
                if not (isinstance(h, int) and h >= HEADS - 2):
                    sp.wait_ge(w_ready, 2 * (h + 1))
                    load(h + 2, slot)
                if not is_last(h):
                    swap(h + 1)
            step(0, 0)
            with by_two(sp, 1, HEADS - 3) as h:
                step(h, 1)
                step(h + 1, 0)
            for h in range(HEADS - 3, HEADS):
                step(h, h % 2)

        @block.tensor
        def _(pe):
            q_norm.tensor(pe)
            kv_norm.tensor(pe)
            pe.wait_ge(wv_ready, 1)
            pe.wait_ge(kv_norm.lo_ready, 1)
            for i in range(TT):
                if i >= 4:
                    pe.wait_ge(v_stored, i - 3)
                tok = slice(i * P, (i + 1) * P)
                three_pass(nc, [chip.bank(4 + i % 4)], ckv_hi[:, 0, tok], ckv_lo[:, 0, tok], [wv[0][:, :]], [wv[1][:, :]],
                           True, True).then_inc(v_out, 1)
            pe.wait_ge(q_norm.lo_ready, 2)

            def project_q(h, slot, pair):
                pe.wait_ge(w_ready, 2 * h + 1)
                for k in range(2):
                    last = three_pass(nc, [chip.bank(2 * pair, QK), chip.bank(2 * pair + 1, QK)], wq[slot][0][:, k, :],
                                      wq[slot][1][:, k, :], halves(cq_hi, k), halves(cq_lo, k), k == 0, k == 1)
                last.then_inc(q_out, 1)

            def project_k(h, slot, pair):
                pe.wait_ge(w_ready, 2 * h + 2)
                three_pass(nc, [chip.bank(2 * pair, NOPE), chip.bank(2 * pair + 1, NOPE)], wk[slot][0][:, :],
                           wk[slot][1][:, :], halves(ckv_hi, 0), halves(ckv_lo, 0), True, True).then_inc(k_out, 1)

            def score(h, t, slot, pair):
                if is_first(h) and t == 0:
                    pe.wait_ge(rope_ready, 2)
                if t == 0:
                    pe.wait_ge(q_ready, h + 1)
                    pe.wait_ge(k_ready, h + 1)
                start = (t // 4) + 2 * P * (t % 4)
                tok = slice(start, start + 2 * P - 1, 2)
                q, k = q_head[slot], k_head[slot]
                three_pass(nc, [chip.bank(2 * pair), chip.bank(2 * pair + 1)], q[0][:, tok], q[1][:, tok],
                           [k[0][:, n * HALF:(n + 1) * HALF] for n in range(2)],
                           [k[1][:, n * HALF:(n + 1) * HALF] for n in range(2)], True, True).then_inc(scored, 1)

            def turn(h, t):
                g = TT * h + t
                pe.wait_ge(exped, g + 1)
                for half in range(2):
                    if not (is_first(h) and t == 0):
                        pe.wait_ge(pt_ready, 2 * g + half - 1)
                    for kt in range(4):
                        last = nc.tensor.transpose(chip.bank(4 + half)[:, kt * P:(kt + 1) * P],
                                                   probs[t % 2][:, (4 * half + kt) * P:(4 * half + kt + 1) * P],
                                                   chip.ident[:, :])
                    last.then_inc(turned, 1)

            def weigh(h, b, half, slot):
                blk = 4 * h + b
                if half == 0:
                    pe.wait_ge(pt_ready, 4 * (blk + 1))
                    if is_first(h) and b == 0:
                        pe.wait_ge(ones_set, 4)
                    if b == 0:
                        pe.wait_ge(v_ready, h + 1)
                    if not (is_first(h) and b < 2):
                        pe.wait_ge(out_stored, blk - 1)
                bank = chip.bank(6 + b % 2, VD + 1, 2 * P)
                for kt in range(4 * half, 4 * half + 4):
                    last = three_pass(nc, [bank], v_head[slot][0][:, kt, :], v_head[slot][1][:, kt, :],
                                      [pt[b % 2][0][:, kt, :]], [pt[b % 2][1][:, kt, :]], kt == 0, kt == TT - 1)
                if half == 1:
                    last.then_inc(weighted, 1)

            def turn_out(h, b):
                pe.wait_ge(out_copied, 4 * h + b + 1)
                for u in range(2):
                    at = (6 + b % 2) * HALF + 2 * P + (VD + 2) * u
                    last = nc.tensor.transpose(chip.ps[:, at:at + VD + 1], out_t[b % 2][:, u * P:(u + 1) * P],
                                               chip.ident[0:VD + 1, 0:VD + 1])
                last.then_inc(out_turned, 1)

            project_q(0, 0, 1)
            project_k(0, 0, 0)
            pe.wait_ge(q_rowed, 1)
            score(0, 0, 0, 1)

            def step(h, slot):
                for t in range(TT):
                    last_head = is_last(h)
                    if t < TT - 1 or not last_head:
                        nxt = (h, t + 1, slot) if t < TT - 1 else (h + 1, 0, 1 - slot)
                        if t + 1 == 1:
                            if is_first(h):
                                pe.wait_ge(k_ready, 1)
                            else:
                                pe.wait_ge(exped, TT * h)
                        elif t == T_Q + 1 and not last_head:
                            pe.wait_ge(q_rowed, h + 2)
                        elif t == T_K + 1 and not last_head:
                            pe.wait_ge(k_ready, h + 2)
                        else:
                            pe.wait_ge(exped, TT * h + t)
                        score(*nxt, t % 2)
                    if t >= 4 and t % 2 == 0:
                        turn_out(h, t // 2 - 2)
                    elif t % 2 == 0 and not is_first(h):
                        turn_out(h - 1, t // 2 + 2)
                    if t in (T_Q, T_K) and not last_head:
                        pe.wait_ge(exped, TT * h + t + 1)
                        (project_q if t == T_Q else project_k)(h + 1, 1 - slot, 0)
                    turn(h, t)
                    if t >= 2:
                        weigh(h, t // 2 - 1, t % 2, slot)
                    elif not is_first(h):
                        weigh(h - 1, 3, t % 2, 1 - slot)

            peeled(pe, step)
            weigh(HEADS - 1, 3, 0, 1)
            weigh(HEADS - 1, 3, 1, 1)
            turn_out(HEADS - 1, 2)
            turn_out(HEADS - 1, 3)

        @block.gpsimd
        def _(pool):
            for k in range(2):
                nc.gpsimd.memset(v_head[k][0][:, :, VD:VD + 1].bitcast(F32), 1.0).then_inc(ones_set, 1)
                nc.gpsimd.memset(v_head[k][1][:, :, VD:VD + 1].bitcast(F32), 0.0).then_inc(ones_set, 1)
            pool.wait_ge(ones_set, 4)
            pool.wait_ge(ropes_loaded, 32)

            def rotate_q(h):
                if not is_first(h):
                    pool.wait_ge(v_ready, h)
                pool.wait_ge(q_swapped, 32 * (h + 1))
                nc.gpsimd.tensor_tensor(q_row[R, :], q_row[R, :], cos_row[R, :], ALU.mult).then_inc(q_roped, 1)
                pool.wait_ge(q_roped, 3 * h + 1)
                nc.gpsimd.tensor_tensor(swapped[R, :], swapped[R, :], sin_row[R, :], ALU.mult).then_inc(q_roped, 1)
                pool.wait_ge(q_roped, 3 * h + 2)
                nc.gpsimd.tensor_tensor(q_row[R, :], q_row[R, :], swapped[R, :], ALU.add).then_inc(q_roped, 1)

            def rest_v(h, slot):
                pool.wait_ge(q_roped, 3 * h + 3)
                pool.wait_ge(v_hi, h + 1)
                nc.gpsimd.tensor_tensor(v_head[slot][1][:, :, 0:VD], v_all[:, :, ds(h * VD, VD)],
                                        v_head[slot][0][:, :, 0:VD].bitcast(F32), ALU.subtract).then_inc(v_ready, 1)

            def step(h, slot):
                rotate_q(h)
                rest_v(h, slot)
            peeled(pool, step)

        @block.scalar
        def _(act):
            q_norm.scalar(act)
            kv_norm.scalar(act)
            act.wait_ge(wv_loaded, 16)
            nc.scalar.activation(wv[0][:, :], wv_raw[:, :], ACT.Copy).then_inc(wv_hi, 1)
            act.wait_ge(k_rope_step, 3)
            for k in range(2):
                nc.scalar.activation(k_head[k][0][R, :], kr[R, :], ACT.Copy).then_inc(rope_hi, 1)
            for i in range(TT):
                act.wait_ge(v_out, i + 1)
                nc.scalar.activation(v_all[:, i, :], chip.bank(4 + i % 4), ACT.Copy).then_inc(v_stored, 1)

            def round_w(h, slot):
                act.wait_ge(w_loaded[slot], 16 * (h - slot) + 32)
                if not is_first(h):
                    act.wait_ge(k_out, h)
                nc.scalar.activation(wq[slot][0][:, :, :], wq_raw[slot][:, :, :], ACT.Copy).then_inc(w_hi, 1)
                nc.scalar.activation(wk[slot][0][:, :], wk_raw[slot][:, :], ACT.Copy).then_inc(w_hi, 1)

            def take_q(h, pair):
                act.wait_ge(q_out, h + 1)
                if not is_first(h):
                    act.wait_ge(q_ready, h)
                nc.scalar.activation(q_row[:, :], chip.pair(pair, QK), ACT.Copy, scale=SCALE).then_inc(q_rowed, 1)

            def round_k(h, slot, pair):
                act.wait_ge(k_out, h + 1)
                if not (isinstance(h, int) and h < 2):
                    act.wait_ge(scored, TT * (h - 1))
                nc.scalar.activation(k_head[slot][0][0:NOPE, :], chip.pair(pair, NOPE), ACT.Copy).then_inc(k_hi, 1)

            def round_v(h, slot):
                if not (isinstance(h, int) and h < 2):
                    act.wait_ge(weighted, 4 * (h - 1))
                nc.scalar.activation(v_head[slot][0][:, :, 0:VD], v_all[:, :, ds(h * VD, VD)], ACT.Copy).then_inc(v_hi, 1)

            def round_q(h, slot):
                act.wait_ge(q_roped, 3 * (h + 1))
                nc.scalar.activation(q_head[slot][0][:, :], q_row[:, :], ACT.Copy).then_inc(q_hi, 1)

            def exponent(h, t):
                g = TT * h + t
                pair = (t + 1) % 2
                act.wait_ge(negmax, g + 1)
                if not (is_first(h) and t < 2):
                    act.wait_ge(turned, 2 * (g - 1))
                nc.scalar.activation(probs[t % 2][:, :], chip.pair(pair), ACT.Exp,
                                     bias=chip.negmax[:, t % 2:t % 2 + 1]).then_inc(exped, 1)

            def round_pt(h, t):
                g = TT * h + t
                b, u = t // 2, t % 2
                if u == 0 and not (is_first(h) and b < 2):
                    act.wait_ge(weighted, 4 * h + b - 1)
                for half in range(2):
                    act.wait_ge(turned, 2 * g + half + 1)
                    nc.scalar.activation(pt[b % 2][0][:, 4 * half:4 * half + 4, u * P:(u + 1) * P],
                                         chip.bank(4 + half).rearrange("p (k q) -> p k q", k=4), ACT.Copy).then_inc(pt_hi, 1)

            def copy_out(h, b):
                blk = 4 * h + b
                act.wait_ge(weighted, blk + 1)
                if not (is_first(h) and b < 2):
                    act.wait_ge(out_turned, blk - 1)
                nc.scalar.activation(out_t[b % 2][:, :], chip.bank(6 + b % 2, VD + 1, 2 * P), ACT.Copy).then_inc(out_copied, 1)

            def store_out(h, b):
                act.wait_ge(out_turned, 4 * h + b + 1)
                at = (6 + b % 2) * HALF + 2 * P
                src = chip.ps[:, at:at + 2 * (VD + 2)].rearrange("p (u d) -> p u d", u=2)[:, :, 0:VD + 1]
                dst = attn[:, 2 * b:2 * b + 2, ds(h, 1), 0:VD + 1].rearrange("p u h d -> p u (h d)")
                nc.scalar.activation(dst, src, ACT.Copy).then_inc(out_stored, 1)

            round_w(0, 0)
            take_q(0, 1)
            round_k(0, 0, 0)
            round_v(0, 0)
            round_q(0, 0)
            exponent(0, 0)

            def step(h, slot):
                more = not is_last(h)
                for t in range(TT):
                    if more and t == T_Q:
                        take_q(h + 1, 0)
                    elif more and t == T_K:
                        round_k(h + 1, 1 - slot, 0)
                    round_pt(h, t)
                    if t < TT - 1:
                        exponent(h, t + 1)
                    elif more:
                        exponent(h + 1, 0)
                    if t % 2 and t >= 3:
                        copy_out(h, (t - 3) // 2)
                    elif t == 1 and not is_first(h):
                        copy_out(h - 1, 3)
                    elif t % 2 == 0 and t >= 4:
                        store_out(h, t // 2 - 2)
                    elif t % 2 == 0 and not is_first(h):
                        store_out(h - 1, t // 2 + 2)
                    if more:
                        if t == 0:
                            round_w(h + 1, 1 - slot)
                        elif t == 4:
                            round_v(h + 1, 1 - slot)
                        elif t == 5:
                            round_q(h + 1, 1 - slot)
            peeled(act, step)
            copy_out(HEADS - 1, 3)
            store_out(HEADS - 1, 2)
            store_out(HEADS - 1, 3)

        @block.vector
        def _(dve):
            q_norm.vector(dve)
            kv_norm.vector(dve)
            dve.wait_ge(wv_hi, 1)
            nc.vector.tensor_tensor(wv[1][:, :], wv_raw[:, :], wv[0][:, :].bitcast(F32), ALU.subtract).then_inc(wv_ready, 1)
            dve.wait_ge(ropes_loaded, 32)
            dve.wait_ge(k_swapped, 32)
            nc.vector.tensor_tensor(kr[R, :], kr[R, :], cos_row[R, :], ALU.mult).then_inc(k_rope_step, 1)
            nc.vector.tensor_tensor(swapped[R, :], swapped[R, :], sin_row[R, :], ALU.mult).then_inc(k_rope_step, 1)
            dve.wait_ge(k_rope_step, 2)
            nc.vector.tensor_tensor(kr[R, :], kr[R, :], swapped[R, :], ALU.add).then_inc(k_rope_step, 1)
            dve.wait_ge(k_rope_step, 3)
            for k in range(2):
                dve.wait_ge(rope_hi, k + 1)
                nc.vector.tensor_tensor(k_head[k][1][R, :], kr[R, :], k_head[k][0][R, :].bitcast(F32),
                                        ALU.subtract).then_inc(rope_ready, 1)

            def rest_w(h, slot):
                dve.wait_ge(w_hi, 2 * h + 1)
                nc.vector.tensor_tensor(wq[slot][1][:, :, :], wq_raw[slot][:, :, :], wq[slot][0][:, :, :].bitcast(F32),
                                        ALU.subtract).then_inc(w_ready, 1)
                dve.wait_ge(w_hi, 2 * h + 2)
                nc.vector.tensor_tensor(wk[slot][1][:, :], wk_raw[slot][:, :], wk[slot][0][:, :].bitcast(F32),
                                        ALU.subtract).then_inc(w_ready, 1)

            def rest_k(h, slot, pair):
                dve.wait_ge(k_hi, h + 1)
                nc.vector.tensor_tensor(k_head[slot][1][0:NOPE, :], chip.pair(pair, NOPE),
                                        k_head[slot][0][0:NOPE, :].bitcast(F32), ALU.subtract).then_inc(k_ready, 1)

            def rest_q(h, slot):
                dve.wait_ge(q_hi, h + 1)
                nc.vector.tensor_tensor(q_head[slot][1][:, :], q_row[:, :], q_head[slot][0][:, :].bitcast(F32),
                                        ALU.subtract).then_inc(q_ready, 1)

            def row_max(h, t):
                g = TT * h + t
                c = slice(t % 2, t % 2 + 1)
                dve.wait_ge(scored, g + 1)
                if not (is_first(h) and t < 2):
                    dve.wait_ge(exped, g - 1)
                nc.vector.tensor_reduce(chip.rowmax[:, c], chip.pair((t + 1) % 2), AXX, ALU.max).then_inc(maxed, 1)
                dve.wait_ge(maxed, g + 1)
                nc.vector.tensor_scalar(chip.negmax[:, c], chip.rowmax[:, c], -1.0, None, ALU.mult).then_inc(negmax, 1)

            def rest_pt(h, t):
                g = TT * h + t
                b, u = t // 2, t % 2
                for half in range(2):
                    dve.wait_ge(pt_hi, 2 * g + half + 1)
                    view = [pt[b % 2][k][:, 4 * half:4 * half + 4, u * P:(u + 1) * P] for k in range(2)]
                    nc.vector.tensor_tensor(view[1], chip.bank(4 + half).rearrange("p (k q) -> p k q", k=4),
                                            view[0].bitcast(F32), ALU.subtract).then_inc(pt_ready, 1)

            rest_w(0, 0)
            rest_k(0, 0, 0)
            rest_q(0, 0)
            row_max(0, 0)

            def step(h, slot):
                more = not is_last(h)
                for t in range(TT):
                    if t < TT - 1:
                        row_max(h, t + 1)
                    elif more:
                        row_max(h + 1, 0)
                    if more and t == T_K:
                        rest_k(h + 1, 1 - slot, 0)
                    rest_pt(h, t)
                    if more and t == 0:
                        rest_w(h + 1, 1 - slot)
                    elif more and t == 5:
                        rest_q(h + 1, 1 - slot)
            peeled(dve, step)


def mixer_out_block(chip, dram, w, attn, hyena, xT, norm, ffn):
    nc = chip.nc
    CT = D // P
    mix_hi = chip.at("o_mix_hi", 32, [P, CT, SEQ], F32R)
    mix_lo = chip.at("o_mix_lo", 64, [P, CT, SEQ], F32R)
    squares = [chip.at(f"o_squares{k}", 128 + 4 * k, [P, TT, 2, VD]) for k in range(2)]
    normed = [chip.at(f"o_normed{k}", 136 + 4 * k, [P, TT, 2, VD]) for k in range(2)]
    power, rstd, weight2 = chip.o_power, chip.o_rstd, chip.o_weight2
    hy = hyena[:, :, :].rearrange("p i (h d) -> p i h d", d=VD)
    s = chip.sem
    x_loaded, weight_squared, squared, power_ready, rooted = (s("o_x_loaded"), s("o_weight_squared"), s("o_squared"),
                                                              s("o_power_ready"), s("o_rooted"))
    summed, inverted, normed_ready = s("o_summed"), s("o_inverted"), s("o_normed_ready")
    turned, mix_hi_ready, mix_ready, added = s("o_turned"), s("o_mix_hi_ready"), s("o_mix_ready"), s("o_added")

    def heads(ct):
        return attn[:, :, 2 * ct:2 * ct + 2, 0:VD] if ct < CT // 2 else hy[:, :, 2 * ct - HEADS:2 * ct - HEADS + 2, :]

    def flat(t):
        return t[:, :, :, :].rearrange("p i h d -> p (i h) d")

    with nc.Block() as block:
        @block.sync
        def _(sp):
            w.load(sp, 0, 0, 0)
            w.load(sp, 1, 1, P)
            sp.dma_start(xT[:], dram["residual"].rearrange("p (k t) -> p k t", k=KT)).then_inc(x_loaded, 16)
            for n in range(2, CT):
                sp.wait_ge(w.ready, n - 1)
                w.load(sp, n, n % 2, n * P)
                if n == 2:
                    sp.wait_ge(normed_ready, CT // 2)
                    ffn.load_gu(sp, 0, (0,))
            sp.wait_ge(w.ready, CT)
            ffn.load_gu(sp, 0, (1,))

        @block.tensor
        def _(pe):
            def turn(ct):
                pe.wait_ge(normed_ready, ct + 1)
                for r in range(2):
                    n = 2 * ct + r
                    if n >= 4:
                        pe.wait_ge(mix_ready, n - 3)
                    for tt in range(TT // 2):
                        last = nc.tensor.transpose(chip.bank(4 + n % 4)[:, tt * P:(tt + 1) * P],
                                                   normed[ct % 2][:, r * (TT // 2) + tt, :, :].rearrange("p h d -> p (h d)"),
                                                   chip.ident[:, :])
                    last.then_inc(turned, 1)

            turn(0)
            pe.wait_ge(w.ready, 2)
            for k in range(CT):
                if k + 1 < CT:
                    turn(k + 1)
                pe.wait_ge(mix_ready, 2 * (k + 1))
                for n in range(2):
                    last = three_pass(nc, [chip.bank(2 * n), chip.bank(2 * n + 1)], w.split[n][0][:, k, :],
                                      w.split[n][1][:, k, :], halves(mix_hi, k), halves(mix_lo, k), k == 0, k == CT - 1)
                    if k == CT - 1:
                        last.then_inc(w.used, 1)
            for n in range(2, CT):
                pe.wait_ge(added, n - 1)
                w.product(pe, n, n % 2, [chip.bank(2 * (n % 2)), chip.bank(2 * (n % 2) + 1)], mix_hi, mix_lo, None)
                if n % 2:
                    norm.tensor(pe, n - 3)
            for k in (CT - 2, CT - 1):
                norm.tensor(pe, k)

        @block.scalar
        def _(act):
            def square(ct):
                if ct >= 2:
                    act.wait_ge(power_ready, ct - 1)
                nc.scalar.activation(squares[ct % 2][:, :, :, :], heads(ct), ACT.Square).then_inc(squared, 1)

            def root(ct):
                act.wait_ge(power_ready, ct + 1)
                eps = {} if ct < CT // 2 else {"bias": chip.eps[:, 0:1]}
                nc.scalar.activation(power[:, ct, :], power[:, ct, :], ACT.Sqrt, scale=1.0 / VD, **eps).then_inc(rooted, 1)

            def round_mix(ct):
                for r in range(2):
                    n = 2 * ct + r
                    act.wait_ge(turned, n + 1)
                    nc.scalar.activation(mix_hi[:, ct, r * HALF:(r + 1) * HALF], chip.bank(4 + n % 4), ACT.Copy,
                                         scale=chip.head_gain[:, ct:ct + 1]).then_inc(mix_hi_ready, 1)

            square(0)
            for ct in range(CT):
                if ct + 1 < CT:
                    square(ct + 1)
                root(ct)
                if ct < 2:
                    w.round(act, ct, ct)
                if ct:
                    round_mix(ct - 1)
            round_mix(CT - 1)
            for n in range(2, CT):
                w.round(act, n, n % 2)
                if n > 2:
                    norm.scalar(act, n - 3, added, n - 2)
            for k in range(CT - 3, CT):
                norm.scalar(act, k, added, k + 1)

        @block.gpsimd
        def _(pool):
            norm.gpsimd(pool)

        @block.vector
        def _(dve):
            weight = attn[:, :, :, VD:VD + 1].rearrange("p i h o -> p i (h o)")
            nc.vector.tensor_tensor(weight2[:, :, :], weight, weight, ALU.mult).then_inc(weight_squared, 1)
            dve.wait_ge(weight_squared, 1)

            def sum_squares(ct):
                dve.wait_ge(squared, ct + 1)
                nc.vector.tensor_reduce(power[:, ct, :], flat(squares[ct % 2]), AXX, ALU.add).then_inc(
                    summed if ct < CT // 2 else power_ready, 1)
                if ct < CT // 2:
                    dve.wait_ge(summed, ct + 1)
                    view = power[:, ct, :].rearrange("p (i h) -> p i h", h=2)
                    nc.vector.scalar_tensor_tensor(out=view, in0=weight2[:, :, 2 * ct:2 * ct + 2], scalar=EPS * VD,
                                                   in1=view, op0=ALU.mult, op1=ALU.add).then_inc(power_ready, 1)

            def normalise(ct):
                dve.wait_ge(rooted, ct + 1)
                nc.vector.reciprocal(rstd[:, ct, :], power[:, ct, :]).then_inc(inverted, 1)
                dve.wait_ge(inverted, ct + 1)
                if ct >= 2:
                    dve.wait_ge(turned, 2 * (ct - 1))
                scale = rstd[:, ct, :].rearrange("p (i h) -> p i h", h=2).unsqueeze(3).to_broadcast([P, TT, 2, VD])
                nc.vector.tensor_tensor(normed[ct % 2][:, :, :, :], heads(ct), scale, ALU.mult).then_inc(normed_ready, 1)

            def mix_low(ct):
                for r in range(2):
                    n = 2 * ct + r
                    dve.wait_ge(mix_hi_ready, n + 1)
                    part = slice(r * HALF, (r + 1) * HALF)
                    nc.vector.scalar_tensor_tensor(out=mix_lo[:, ct, part], in0=chip.bank(4 + n % 4),
                                                   scalar=chip.head_gain[:, ct:ct + 1], in1=mix_hi[:, ct, part].bitcast(F32),
                                                   op0=ALU.mult, op1=ALU.subtract).then_inc(mix_ready, 1)

            for ct in range(CT):
                sum_squares(ct)
                normalise(ct)
                if ct < 2:
                    w.rest(dve, ct, ct)
                if ct:
                    mix_low(ct - 1)
            mix_low(CT - 1)
            dve.wait_ge(x_loaded, 16)

            def add(n):
                dve.wait_ge(w.used, n + 1)
                view = xT[:, n, :].rearrange("p (t r) -> p r t", r=2)
                nc.vector.tensor_tensor(view, chip.pair(n % 2).rearrange("p (r t) -> p r t", r=2), view,
                                        ALU.add).then_inc(added, 1)
            for n in range(CT):
                add(n)
                if n >= 1:
                    norm.vector(dve, n - 1)
                if n + 2 < CT:
                    w.rest(dve, n + 2, n % 2)
            norm.vector(dve, CT - 1)


def output_block(chip, dram, xT):
    nc = chip.nc
    gain = chip.at("e_gain", 32, [P, D])
    junk = chip.at("e_junk", 36, [P, D])
    y = [chip.at(f"e_y{k}", 40 + 4 * k, [P, D]) for k in range(2)]
    total, root = chip.e_total, chip.e_root
    s = chip.sem
    gain_loaded, turned, squared, rooted, scaled = (s("e_gain_loaded"), s("e_turned"), s("e_squared"), s("e_rooted"),
                                                    s("e_scaled"))
    rstd_ready, stored = s("e_rstd_ready"), [s("e_stored0"), s("e_stored1")]
    with nc.Block() as block:
        @block.sync
        def _(sp):
            sp.dma_start(gain[:], dram["final_norm_g"].partition_broadcast(P)).then_inc(gain_loaded, 16)
            with by_two(sp, 0, TT) as i:
                for a in range(2):
                    sp.wait_ge(scaled, i + a + 1)
                    sp.dma_start(dram["out"][ds((i + a) * P, P), :], y[a][:]).then_inc(stored[a], 16)
            for a in range(2):
                sp.wait_ge(stored[a], 16 * TT // 2)

        @block.tensor
        def _(pe):
            for i in range(TT):
                if i >= 4:
                    pe.wait_ge(scaled, i - 3)
                for k in range(KT):
                    at = (i % 4) * 2 * HALF + k * P
                    last = nc.tensor.transpose(chip.ps[:, at:at + P], xT[:, k, i * P:(i + 1) * P], chip.ident[:, :])
                last.then_inc(turned, 1)

        @block.scalar
        def _(act):
            for i in range(TT):
                act.wait_ge(turned, i + 1)
                if i:
                    act.wait_ge(squared, i)
                nc.scalar.activation(junk[:, :], chip.pair(i % 4), ACT.Square, accum_out=total[:, i:i + 1]).then_inc(squared, 1)
                act.wait_ge(squared, i + 1)
                nc.scalar.activation(root[:, i:i + 1], total[:, i:i + 1], ACT.Sqrt, bias=chip.eps[:, 0:1],
                                     scale=1.0 / D).then_inc(rooted, 1)

        @block.vector
        def _(dve):
            dve.wait_ge(gain_loaded, 16)
            for i in range(TT):
                dve.wait_ge(rooted, i + 1)
                nc.vector.reciprocal(root[:, i:i + 1], root[:, i:i + 1]).then_inc(rstd_ready, 1)
                dve.wait_ge(rstd_ready, i + 1)
                if i >= 2:
                    dve.wait_ge(stored[i % 2], 16 * (i // 2))
                nc.vector.scalar_tensor_tensor(out=y[i % 2][:, :], in0=chip.pair(i % 4), scalar=root[:, i:i + 1],
                                               in1=gain[:, :], op0=ALU.mult, op1=ALU.mult).then_inc(scaled, 1)


def encoder(nc, dram):
    with ExitStack() as ctx:
        chip = Chip(nc, ctx)
        chip.ident = chip.small("ident", [P, P])
        chip.ones = chip.small("ones", [P, P])
        chip.eps = chip.small("eps", [P, 1])
        gains = {}
        for name, tiles in (("ffn1_norm_g", KT), ("mix_norm_g", KT), ("ffn2_norm_g", KT), ("q_norm_g", 2),
                            ("kv_norm_g", 1), ("head_norm_g", KT)):
            gains[name] = chip.small(f"g_{name}", [P, tiles])
        chip.q_gain, chip.kv_gain, chip.head_gain = gains["q_norm_g"], gains["kv_norm_g"], gains["head_norm_g"]
        conv_w = chip.small("conv_w", [P, 3, HY_TILES])
        conv_b = chip.small("conv_b", [P, HY_TILES])
        chip.fw1 = chip.at("f_w1", 204, [EMB, HID])
        chip.fw2 = chip.at("f_w2", 204.25, [HID, HID])
        chip.fcol = chip.small("fcol", [HID, 3])
        chip.negmax = chip.small("negmax", [P, 2])
        chip.rowmax = chip.small("rowmax", [P, 2])
        chip.o_power = chip.small("o_power", [P, KT, 2 * TT])
        chip.o_rstd = chip.at("o_rstd", 201, [P, KT, 2 * TT])
        chip.o_weight2 = chip.at("o_weight2", 202, [P, TT, HEADS])
        chip.e_total = chip.small("e_total", [P, TT])
        chip.e_root = chip.small("e_root", [P, TT])
        chip.consts_ready = chip.sem("consts_ready")
        filled = chip.sem("filled")

        xT = chip.at("xT", 0, [P, KT, SEQ])

        with nc.Block() as block:
            @block.gpsimd
            def _(pool):
                nc.gpsimd.memset(chip.ident[:, :], 0.0).then_inc(filled, 1)
                nc.gpsimd.memset(chip.ones[:, :], 1.0).then_inc(filled, 1)
                nc.gpsimd.memset(chip.eps[:, :], EPS).then_inc(filled, 1)
                pool.wait_ge(filled, 3)
                nc.gpsimd.affine_select(out=chip.ident[:, :], in_=chip.ident[:, :], compare_op=ALU.not_equal, fill=1.0,
                                        base=0, pattern=[[-1, P]], channel_multiplier=1).then_inc(chip.consts_ready, 1)

        x_hi, x_lo = (chip.at(f"x_{k}", 32 + 32 * n, [P, KT, SEQ], F32R) for n, k in enumerate(("hi", "lo")))
        norm1 = FeatureSplit(chip, "n1", xT, gains["ffn1_norm_g"], x_hi, x_lo, 144, 4, 200, 2)
        ffn1 = Ffn(chip, "f1", dram["ffn1_w_gate"], dram["ffn1_w_up"], dram["ffn1_w_down"], xT, norm1,
                   {"wgu": 96, "h": 128, "d_raw": 160, "gu_raw": (168, 176), "wd": 184})
        norm2 = FeatureSplit(chip, "n2", xT, gains["mix_norm_g"], x_hi, x_lo, 96, 4, 200, 1)
        w_in = ColumnWeights(chip, "m_w", dram["w_in"], 160, 168)
        columns = [(t, dram[name]) for name, t in gains.items()]
        columns += [(conv_w, dram["hyena_conv_w"]), (conv_b, dram["hyena_conv_b"])]
        filters_block(chip, dram, xT, norm1, ffn1, columns)
        ffn1.run(split_here=True, after=MixerInput(norm2, w_in))

        v_hi, v_lo = (chip.at(f"v_{k}", 16 * n, [P, TT, C], F32R) for n, k in enumerate(("hi", "lo")))
        gates = [chip.at(f"gate{k}", 96 + 16 * k, [P, TT, C]) for k in range(2)]
        cq = chip.at("cq", 128, [P, 2, SEQ])
        ckv = chip.at("ckv", 136, [P, 1, SEQ])
        kr = chip.at("kr", 140, [QK, SEQ])
        attn = chip.at("attn", 184, [P, TT, HEADS, VD + 2])
        hyena = Hyena(chip, dram)
        mixer_in_block(chip, xT, dram["residual"].rearrange("p (k t) -> p k t", k=KT), w_in, norm2, cq, ckv, kr,
                       v_hi, v_lo, gates, conv_w, conv_b, hyena)
        hyena.run(v_hi, v_lo, gates)
        chip.recycle()
        attention_block(chip, dram, cq, ckv, kr, attn)
        w_out = ColumnWeights(chip, "o_w", dram["w_out"], 160, 168)
        x2_hi, x2_lo = (chip.at(f"x2_{k}", 96 + 32 * n, [P, KT, SEQ], F32R) for n, k in enumerate(("hi", "lo")))
        norm3 = FeatureSplit(chip, "n3", xT, gains["ffn2_norm_g"], x2_hi, x2_lo, 184, 2, 200, 3)
        ffn2 = Ffn(chip, "f2", dram["ffn2_w_gate"], dram["ffn2_w_up"], dram["ffn2_w_down"], xT, norm3,
                   {"wgu": 32, "h": 64, "gu_raw": (192, 160), "wd": 168, "d_raw": 184})
        mixer_out_block(chip, dram, w_out, attn, gates[1], xT, norm3, ffn2)
        ffn2.run(split_here=False)
        output_block(chip, dram, xT)


INPUTS = ["x", "ffn1_norm_g", "ffn1_w_gate", "ffn1_w_up", "ffn1_w_down", "mix_norm_g", "w_in", "q_norm_g", "w_uq",
          "kv_norm_g", "w_ukv", "hyena_conv_w", "hyena_conv_b", "filt_w1", "filt_b1", "filt_w2", "filt_b2", "filt_w3",
          "filt_freq", "hyena_d", "head_norm_g", "w_out", "ffn2_norm_g", "ffn2_w_gate", "ffn2_w_up", "ffn2_w_down",
          "final_norm_g"]
COLUMNS = ("ffn1_norm_g", "mix_norm_g", "ffn2_norm_g", "q_norm_g", "kv_norm_g", "head_norm_g", "hyena_conv_w",
           "hyena_conv_b", "filt_b1", "filt_b2", "filt_freq")


def kernel(**inputs):
    import concourse.bacc as _bacc
    from concourse.bass_utils import run_bass_kernel_spmd as _run

    nc = _bacc.Bacc("TRN2", target_bir_lowering=False, num_devices=1)
    arrays, dram = {}, {}
    for name in INPUTS:
        a = np.ascontiguousarray(inputs[name])
        a = a.reshape(a.shape[1:]) if a.ndim > 1 else a
        if name in COLUMNS:
            a = np.ascontiguousarray(np.moveaxis(a.reshape(*a.shape[:-1], -1, min(P, a.shape[-1])), -1, 0))
        arrays[f"in_{name}"] = a
        dram[name] = nc.dram_tensor(f"in_{name}", a.shape, F32, kind="ExternalInput").ap()
    out = nc.dram_tensor("out_y", (SEQ, D), F32, kind="ExternalOutput")
    dram["out"] = out.ap()
    dram["residual"] = nc.dram_tensor("residual", (P, KT * SEQ), F32, kind="Internal").ap()
    dram["spectra"] = nc.dram_tensor("spectra", (2 * WT * P, 4 * C), F32, kind="Internal").ap()
    fwd, inv = transform_tables()
    for name, a in (("fwd", fwd), ("inv", inv), ("features", filter_features()), ("decay", filter_decay()),
                    ("rope", rope_rows())):
        dram[name] = nc.inline_tensor(a, name=f"c_{name}").ap()
    encoder(nc, dram)
    r = _run(nc, [arrays], core_ids=[0])
    return r.results[0]["out_y"].reshape(1, SEQ, D)
```

```python
import math
from contextlib import ExitStack

import numpy as np
import concourse.bass as bass
import concourse.mybir as mybir

F32 = mybir.dt.float32
F32R = mybir.dt.float32r
ACT = mybir.ActivationFunctionType
ALU = mybir.AluOpType
AXX = mybir.AxisListType.X

P = 128
SEQ = 1024
D = 1024
KT = D // P
TT = SEQ // P
HALF = 512
FFN = 2816
EPS = 1e-6
Q_RANK, KV_RANK, ROPE = 256, 128, 32
HEADS, NOPE, VD = 8, 64, 64
QK = NOPE + ROPE
C = 512
HID = 64
BANDS = 16
EMB = 2 * BANDS + 1
WT = SEQ // 2 // P
GROUPS = 16
IN_COLS = Q_RANK + KV_RANK + ROPE + 3 * C

ds = bass.ds


def by_two(eng, start, end):
    return eng.Fori(start, end - 1, 2)


def split_hi_lo(a):
    a32 = a.astype(np.float32)
    bits = a32.view(np.uint32).astype(np.uint64)
    hi = ((bits + 0x7FF + ((bits >> 12) & 1)) & 0xFFFFF000).astype(np.uint32).view(np.float32)
    return hi, (a32 - hi).astype(np.float32)


def transform_tables():
    w = np.arange(SEQ // 2) + 0.5
    t = np.arange(SEQ)
    ang = math.pi / SEQ * w[:, None] * t[None, :]
    both = np.stack([np.cos(ang), np.sin(ang)])
    hl = np.stack(split_hi_lo(both), axis=1)
    x = hl.reshape(2, 2, WT, P, TT // 2, P, 2)
    fwd = x.transpose(2, 6, 5, 4, 0, 1, 3).reshape(2 * WT * P, (TT // 2) * 4 * P)
    inv = x.transpose(6, 2, 3, 4, 0, 1, 5).reshape(2 * WT * P, (TT // 2) * 4 * P) / SEQ
    return np.ascontiguousarray(fwd, np.float32), np.ascontiguousarray(inv, np.float32)


def parity_order():
    return np.concatenate([np.arange(0, SEQ, 2), np.arange(1, SEQ, 2)])


def filter_features():
    f = np.float32
    pos = np.arange(SEQ, dtype=f)
    t = pos / f(SEQ - 1)
    bands = np.linspace(1e-4, BANDS - 1, BANDS, dtype=f)
    ang = (f(2.0 * math.pi) * pos / f(SEQ))[:, None] * bands[None, :]
    z = np.concatenate([t[:, None], np.cos(ang), -np.sin(ang)], axis=-1).astype(f)
    return np.ascontiguousarray(z[parity_order()].T)


def filter_decay():
    f = np.float32
    t = np.arange(SEQ, dtype=f) / f(SEQ - 1)
    lo, hi = math.log(1e-2) / 1.5, math.log(1e-2) / 0.3
    deltas = np.abs(np.linspace(lo, hi, C, dtype=f))
    dec = np.exp(-t[:, None] * deltas[None, :]).astype(f)
    return np.ascontiguousarray(dec[parity_order()])


def rope_rows():
    f = np.float32
    inv = (1.0 / (f(10000.0) ** (np.arange(0, ROPE, 2, dtype=f) / f(ROPE)))).astype(f)
    ang = np.arange(SEQ, dtype=f)[None, :] * inv[:, None]
    cos, sin = np.cos(ang).astype(f), np.sin(ang).astype(f)
    return np.ascontiguousarray(np.concatenate([cos, cos, -sin, sin], axis=0))


class Chip:

    def __init__(self, nc, ctx):
        self.nc, self.sems = nc, []
        self.small_at = -(-nc.sbuf_base // 64) * 64
        self.small_end = self.small_at + 3072
        self.main = self.small_end
        self.ps = ctx.enter_context(nc.psum_tensor("ps", [P, 8 * HALF], F32))

    def at(self, name, kb, shape, dtype=F32):
        return self.nc.alloc_sbuf_tensor_at(name, shape, dtype, offset=self.main + int(kb * 1024))

    def small(self, name, shape, dtype=F32):
        size = 4
        for n in shape[1:]:
            size *= n
        t = self.nc.alloc_sbuf_tensor_at(name, shape, dtype, offset=self.small_at)
        self.small_at += -(-size // 32) * 32
        assert self.small_at <= self.small_end, name
        return t

    def sem(self, name):
        self.sems.append(self.nc.alloc_semaphore(name=name))
        return self.sems[-1]

    def recycle(self):
        self.nc.clear_and_free_semaphores(self.sems)
        self.nc.all_engine_barrier()
        self.sems = []

    def bank(self, n, rows=P, cols=HALF):
        return self.ps[0:rows, n * HALF:n * HALF + cols]

    def pair(self, n, rows=P):
        return self.ps[0:rows, n * 2 * HALF:(n + 1) * 2 * HALF]


def three_pass(nc, outs, w_hi, w_lo, x_hi, x_lo, start, stop):
    for n, out in enumerate(outs):
        nc.tensor.matmul(out, w_hi, x_hi[n], start=start, stop=False)
        nc.tensor.matmul(out, w_hi, x_lo[n], start=False, stop=False)
    for n, out in enumerate(outs):
        last = nc.tensor.matmul(out, w_lo, x_hi[n], start=False, stop=stop)
    return last


def halves(x, k):
    return [x[:, k, 0:HALF], x[:, k, HALF:2 * HALF]]


class FeatureSplit:

    def __init__(self, chip, tag, src, gain, hi, lo, squares_kb, slots, root_kb, pair, added=KT - 2):
        self.added_tiles, self.sums = added, 1 + KT - added
        self.nc, self.chip, self.src, self.gain, self.hi, self.lo, self.pair = chip.nc, chip, src, gain, hi, lo, pair
        self.slots = slots
        self.squares = chip.at(f"{tag}_squares", squares_kb, [P, slots, SEQ])
        self.rstd = chip.at(f"{tag}_rstd", root_kb, [P, SEQ])
        self.hi_ready, self.lo_ready = chip.sem(f"{tag}_hi_ready"), chip.sem(f"{tag}_lo_ready")
        self.squared, self.added = chip.sem(f"{tag}_squared"), chip.sem(f"{tag}_squares_added")
        self.summed = chip.sem(f"{tag}_summed")
        self.rooted, self.rstd_ready = chip.sem(f"{tag}_rooted"), chip.sem(f"{tag}_rstd_ready")

    def scalar(self, act, k, src_ready, count):
        act.wait_ge(src_ready, count)
        self.round(act, k)
        self.square(act, k, src_ready, count)

    def round(self, act, k):
        self.nc.scalar.activation(self.hi[:, k, :], self.src[:, k, :], ACT.Copy,
                                  scale=self.gain[:, k:k + 1]).then_inc(self.hi_ready, 1)

    def slot(self, k):
        return self.squares[:, 0 if k == 0 else 1 + (k - 1) % (self.slots - 1), :]

    def square(self, act, k, src_ready, count):
        act.wait_ge(src_ready, count)
        before = k - (self.slots - 1)
        if before >= self.added_tiles:
            act.wait_ge(self.summed, before - self.added_tiles + 2)
        elif before >= 1:
            act.wait_ge(self.added, before)
        self.nc.scalar.activation(self.slot(k), self.src[:, k, :], ACT.Square).then_inc(self.squared, 1)

    def vector(self, dve, k):
        dve.wait_ge(self.hi_ready, k + 1)
        self.nc.vector.scalar_tensor_tensor(out=self.lo[:, k, :], in0=self.src[:, k, :], scalar=self.gain[:, k:k + 1],
                                            in1=self.hi[:, k, :].bitcast(F32), op0=ALU.mult,
                                            op1=ALU.subtract).then_inc(self.lo_ready, 1)

    def gpsimd(self, pool):
        for k in range(1, self.added_tiles):
            pool.wait_ge(self.squared, k + 1)
            if k >= 2:
                pool.wait_ge(self.added, k - 1)
            self.nc.gpsimd.tensor_tensor(self.slot(0), self.slot(0), self.slot(k), ALU.add).then_inc(self.added, 1)

    def tensor(self, pe, tiles=None):
        for k in tiles or (0, *range(self.added_tiles, KT)):
            if k == 0 and self.added_tiles > 1:
                pe.wait_ge(self.added, self.added_tiles - 1)
            else:
                pe.wait_ge(self.squared, k + 1)
            for n in range(2):
                last = self.nc.tensor.matmul(self.chip.bank(2 * self.pair + n), self.chip.ones[:, :],
                                             self.slot(k)[:, n * HALF:(n + 1) * HALF],
                                             start=(k == 0), stop=(k == KT - 1))
            last.then_inc(self.summed, 1)

    def root_of_mean(self, act):
        act.wait_ge(self.summed, self.sums)
        self.nc.scalar.activation(self.rstd[:, :], self.chip.pair(self.pair), ACT.Sqrt, bias=self.chip.eps[:, 0:1],
                                  scale=1.0 / D).then_inc(self.rooted, 1)

    def invert(self, dve):
        dve.wait_ge(self.rooted, 1)
        self.nc.vector.reciprocal(self.rstd[:, :], self.rstd[:, :]).then_inc(self.rstd_ready, 1)
        dve.wait_ge(self.rstd_ready, 1)


class LatentNorm:

    def __init__(self, chip, tag, src, tiles, gain, squares, root, pair):
        self.nc, self.chip, self.src, self.tiles, self.gain = chip.nc, chip, src, tiles, gain
        self.squares, self.root, self.pair = squares, root, pair
        self.squared, self.summed, self.rooted = (chip.sem(f"{tag}_squared"), chip.sem(f"{tag}_summed"),
                                                  chip.sem(f"{tag}_rooted"))
        self.inverted, self.scaled = chip.sem(f"{tag}_inverted"), chip.sem(f"{tag}_scaled")

    def square(self, act, k):
        self.nc.scalar.activation(self.squares[:, k, :], self.src[:, k, :], ACT.Square).then_inc(self.squared, 1)

    def sum(self, pe):
        for k in range(self.tiles):
            pe.wait_ge(self.squared, k + 1)
            for n in range(2):
                last = self.nc.tensor.matmul(self.chip.bank(2 * self.pair + n), self.chip.ones[:, :],
                                             self.squares[:, k, n * HALF:(n + 1) * HALF],
                                             start=(k == 0), stop=(k == self.tiles - 1))
        last.then_inc(self.summed, 1)

    def root_of_mean(self, act):
        act.wait_ge(self.summed, 1)
        self.nc.scalar.activation(self.root[:, :], self.chip.pair(self.pair), ACT.Sqrt, bias=self.chip.eps[:, 0:1],
                                  scale=1.0 / (self.tiles * P)).then_inc(self.rooted, 1)

    def invert(self, dve):
        dve.wait_ge(self.rooted, 1)
        self.nc.vector.reciprocal(self.root[:, :], self.root[:, :]).then_inc(self.inverted, 1)

    def scale(self, dve):
        dve.wait_ge(self.inverted, 1)
        for k in range(self.tiles):
            self.nc.vector.scalar_tensor_tensor(out=self.src[:, k, :], in0=self.src[:, k, :], scalar=self.gain[:, k:k + 1],
                                                in1=self.root[:, :], op0=ALU.mult, op1=ALU.mult).then_inc(self.scaled, 1)


def filters_block(chip, dram, xT, norm, ffn, columns):
    nc = chip.nc
    x_in = [chip.at(f"x_in{k}", kb, [P, D]) for k, kb in enumerate((32, 36, 56, 60))]
    feat = chip.at("f_feat", 40, [EMB, SEQ])
    arg = chip.at("f_arg", 44, [HID, SEQ])
    turn = chip.at("f_turn", 48, [HID, SEQ])
    h1 = chip.at("f_h1", 52, [HID, SEQ])
    h2 = chip.at("f_h2", 176, [HID, SEQ])
    w3 = chip.at("f_w3", 160, [HID, 2, 2, C])
    w3_mix = chip.at("f_w3_mix", 168, [HID, 2, 2, C])
    decay = chip.at("f_decay", 180, [P, TT, C])
    skip = chip.at("f_skip", 196, [P, 2, C])
    tap_hi = chip.at("f_tap_hi", 64, [P, 2, TT, C], F32R)
    tap_lo = chip.at("f_tap_lo", 96, [P, 2, TT, C], F32R)
    table = [chip.at(f"f_table{s}", 128 + 8 * s, [P, TT // 2, 2, 2, P], F32R) for s in range(4)]
    mixd = [chip.at(f"f_mixd{s}", 40 + 4 * s, [P, 2, C]) for s in range(2)]
    absd = [chip.at(f"f_absd{s}", 32 + 4 * s, [P, 2, C]) for s in range(2)]
    mag = [chip.at(f"f_mag{s}", 48 + 2 * s, [P, C]) for s in range(2)]
    even = chip.at("f_even", 52, [P, 2, C])
    odd = chip.at("f_odd", 36, [P, 2, C])
    spec = chip.at("f_spec", 56, [P, 4, C])
    h2t = [chip.at(f"f_h2t{s}", 160 + 0.5 * s, [HID, P]) for s in range(2)]
    rnorm = chip.at("f_rnorm", 161, [P, C])

    s = chip.sem
    x_loaded, x_turned, x_copied = [s(f"x_loaded{k}") for k in range(4)], s("x_turned"), s("x_copied")
    loaded, w3_loaded, skip_loaded, decay_loaded = s("f_loaded"), s("f_w3_loaded"), s("f_skip_loaded"), s("f_decay_loaded")
    linear, step, sine, w3_mixed = s("f_linear"), s("f_step"), s("f_sine"), s("f_w3_mixed")
    h2t_ready, taps_out, mixed, edge = s("f_h2t_ready"), s("f_taps_out"), s("f_mixed"), s("f_edge")
    hi_ready, lo_ready, absed, mag_ready, mag_summed = (s("f_hi_ready"), s("f_lo_ready"), s("f_absed"),
                                                        s("f_mag_ready"), s("f_mag_summed"))
    rnorm_ready, columns_loaded = s("f_rnorm_ready"), s("columns_loaded")
    table_loaded = [s(f"f_table_loaded{k}") for k in range(4)]
    table_used, even_scaled, spec_step, spec_stored = (s("f_table_used"), s("f_even_scaled"), s("f_spec_step"),
                                                       s("f_spec_stored"))
    chip.spec_stored = spec_stored
    SPEC_STEPS = 4
    UNITS = 2 * WT
    TILES = 2 * WT

    turns = 1.0 / (2.0 * math.pi)
    big = float(1.5 * 2 ** 23)
    c1 = 6.28125
    c2 = math.floor((2.0 * math.pi - c1) * 2 ** 20) / 2 ** 20
    c3 = 2.0 * math.pi - c1 - c2
    pi = 3.1415925

    def tap_tiles(eng, tile):
        tile(0, 0)
        tile(1, 1)
        with by_two(eng, 2, TT) as i:
            tile(i, 0)
            tile(i + 1, 1)

    def at_tile(t, i):
        return t[:, :, i, :] if isinstance(i, int) else t[:, :, ds(i, 1), :].rearrange("p a b c -> p a (b c)")

    def later(o, i, k=1):
        return bool(o) or not isinstance(i, int) or i >= k

    with nc.Block() as block:
        @block.sync
        def _(sp):
            for dst, src in ((feat, dram["features"]), (chip.fw1, dram["filt_w1"]), (chip.fw2, dram["filt_w2"]),
                             (chip.fcol[:, 0:1], dram["filt_b1"]), (chip.fcol[:, 1:2], dram["filt_b2"]),
                             (chip.fcol[:, 2:3], dram["filt_freq"])):
                sp.dma_start(dst[:], src).then_inc(loaded, 16)
            for i in range(TT):
                if i >= 4:
                    sp.wait_ge(x_turned, i - 3)
                sp.dma_start(x_in[i % 4][:], dram["x"][i * P:(i + 1) * P, :]).then_inc(x_loaded[i % 4], 16)
                if i == 3:
                    sp.dma_start(w3[:], dram["filt_w3"].rearrange("h (o r c) -> h o r c", o=2, r=2)).then_inc(w3_loaded, 16)
            sp.dma_start(decay[:], dram["decay"].rearrange("(i p) c -> p i c", p=P)).then_inc(decay_loaded, 16)
            for dst, src in columns:
                sp.dma_start(dst[:], src).then_inc(columns_loaded, 16)
            sp.dma_start(skip[:], dram["hyena_d"].rearrange("o c -> (o c)").partition_broadcast(P)
                         ).then_inc(skip_loaded, 16)

            def load_table(n):
                row = (n % UNITS) * P
                sp.dma_start(table[n % 4][:].bitcast(F32), dram["fwd"][row:row + P, :]).then_inc(table_loaded[n % 4], 16)
            load_table(0)
            load_table(1)
            sp.wait_ge(norm.summed, norm.sums)
            load_table(2)
            load_table(3)
            for t in range(TILES):
                for n in (2 * t + 4, 2 * t + 5):
                    if n < 2 * UNITS:
                        sp.wait_ge(table_used, n - 3)
                        load_table(n)
                if t == WT:
                    sp.wait_ge(mixed, 2 * TT)
                    sp.wait_ge(taps_out, 2 * TT)
                    ffn.load_gu(sp, 0)
                    sp.wait_ge(columns_loaded, 16 * len(columns))
                sp.wait_ge(spec_step, SPEC_STEPS * (t + 1))
                sp.dma_start(dram["spectra"][t * P:(t + 1) * P, :], spec[:]).then_inc(spec_stored, 16)

        @block.gpsimd
        def _(pool):
            pool.wait_ge(w3_loaded, 16)
            nc.gpsimd.tensor_tensor(w3_mix[:, :, 0, :], w3[:, :, 0, :], w3[:, :, 1, :], ALU.add).then_inc(w3_mixed, 1)
            nc.gpsimd.tensor_tensor(w3_mix[:, :, 1, :], w3[:, :, 0, :], w3[:, :, 1, :], ALU.subtract).then_inc(w3_mixed, 1)
            pool.wait_ge(w3_mixed, 2)
            pool.wait_ge(sine, 2)
            for o in range(2):
                def turn_slot(i, slot, o=o):
                    if later(o, i, 2):
                        pool.wait_ge(taps_out, TT * o + i - 1)
                    nc.gpsimd.tensor_copy(h2t[slot][:, :], h2[:, ds(i * P, P)]).then_inc(h2t_ready, 1)

                tap_tiles(pool, turn_slot)

        @block.tensor
        def _(pe):
            pe.wait_ge(loaded, 16 * 6)
            pe.wait_ge(chip.consts_ready, 1)
            for n in range(2):
                last = nc.tensor.matmul(chip.bank(n, HID), chip.fw1[:, :], feat[:, n * HALF:(n + 1) * HALF],
                                        start=True, stop=True)
            last.then_inc(linear, 1)

            def turn_x(i):
                pe.wait_ge(x_loaded[i % 4], 16 * (i // 4 + 1))
                if i >= 2:
                    pe.wait_ge(x_copied, i - 1)
                for k in range(KT):
                    at = (2 + i % 2) * 2 * HALF + k * P
                    last = nc.tensor.transpose(chip.ps[:, at:at + P], x_in[i % 4][:, k * P:(k + 1) * P], chip.ident[:, :])
                last.then_inc(x_turned, 1)

            for i in range(TT):
                turn_x(i)
                if i == 3:
                    pe.wait_ge(sine, 1)
                    for n in range(2):
                        last = nc.tensor.matmul(chip.bank(2 + n, HID), chip.fw2[:, :], h1[:, n * HALF:(n + 1) * HALF],
                                                start=True, stop=True)
                    last.then_inc(linear, 1)
            pe.wait_ge(x_copied, TT)
            norm.tensor(pe, range(0, 5))
            pe.wait_ge(w3_mixed, 2)
            pe.wait_ge(step, 14)

            for o in range(2):
                def taps(i, slot, o=o):
                    pe.wait_ge(h2t_ready, TT * o + i + 1)
                    if later(o, i, 2):
                        pe.wait_ge(mixed, TT * o + i - 1)
                    for m in range(2):
                        last = nc.tensor.matmul(chip.bank(2 * slot + m), h2t[slot][:, :], w3_mix[:, o, m, :],
                                                start=True, stop=True)
                    last.then_inc(taps_out, 1)

                def magnitudes(i, slot, first, last, o=o):
                    pe.wait_ge(mag_ready, TT * o + i + 1)
                    nc.tensor.matmul(chip.bank(7), chip.ones[:, :], mag[slot][:, :], start=first,
                                     stop=last).then_inc(mag_summed, 1)

                if o == 1:
                    pe.wait_ge(spec_step, SPEC_STEPS * (WT - 1) + 1)
                    pe.wait_ge(rnorm_ready, 1)
                taps(0, 0)
                taps(1, 1)
                taps(2, 0)
                magnitudes(0, 0, True, False)
                taps(3, 1)
                magnitudes(1, 1, False, False)
                with by_two(pe, 4, TT) as i:
                    taps(i, 0)
                    magnitudes(i - 2, 0, False, False)
                    taps(i + 1, 1)
                    magnitudes(i - 1, 1, False, False)
                magnitudes(TT - 2, 0, False, False)
                magnitudes(TT - 1, 1, False, True)
                if o == 0:
                    norm.tensor(pe, range(5, KT))

                pe.wait_ge(mixed, TT * (o + 1))
                for wt in range(WT):
                    t = WT * o + wt
                    for r in range(2):
                        n = 2 * t + r
                        pe.wait_ge(table_loaded[n % 4], 16 * (n // 4 + 1))
                        if wt and r == 0:
                            pe.wait_ge(even_scaled, 2 * t - 1)
                        elif wt:
                            pe.wait_ge(spec_step, SPEC_STEPS * (t - 1) + 1)
                        for tt in range(TT // 2):
                            if wt == 0:
                                pe.wait_ge(lo_ready, TT * o + r * (TT // 2) + tt + 1)
                            for cs in range(2):
                                last = three_pass(nc, [chip.bank(2 * r + cs)], table[n % 4][:, tt, cs, 0, :],
                                                  table[n % 4][:, tt, cs, 1, :], [tap_hi[:, cs, r * (TT // 2) + tt, :]],
                                                  [tap_lo[:, cs, r * (TT // 2) + tt, :]], tt == 0, tt == TT // 2 - 1)
                        last.then_inc(table_used, 1)

        @block.scalar
        def _(act):
            def copy_x(i):
                act.wait_ge(x_turned, i + 1)
                nc.scalar.activation(xT[:, :, i * P:(i + 1) * P], chip.pair(2 + i % 2).rearrange("p (k t) -> p k t", k=KT),
                                     ACT.Copy).then_inc(x_copied, 1)

            def sin_layer(layer):
                act.wait_ge(step, 7 * (layer + 1))
                nc.scalar.activation((h1, h2)[layer][:, :], arg[:, :], ACT.Sin).then_inc(sine, 1)

            for i in range(TT):
                copy_x(i)
                if i == 3:
                    sin_layer(0)
            for k in range(KT):
                if k == KT // 2:
                    sin_layer(1)
                norm.square(act, k, x_copied, TT)
            for o in range(2):
                def tap(i, slot, o=o):
                    u = TT * o + i
                    act.wait_ge(mixed, u + 1)
                    nc.scalar.activation(at_tile(tap_hi, i), mixd[slot][:, :, :], ACT.Copy).then_inc(hi_ready, 1)
                    if later(o, i, 2):
                        act.wait_ge(mag_ready, u - 1)
                    nc.scalar.activation(absd[slot][:, :, :], mixd[slot][:, :, :], ACT.Abs).then_inc(absed, 1)
                if o == 1:
                    act.wait_ge(table_used, UNITS)
                tap_tiles(act, tap)
                if o == 0:
                    norm.root_of_mean(act)

        @block.vector
        def _(dve):
            for layer in range(2):
                at = 7 * layer
                dve.wait_ge(linear, layer + 1)
                if layer:
                    dve.wait_ge(sine, 1)
                nc.vector.tensor_scalar(arg[:, :], chip.pair(layer, HID), chip.fcol[:, layer:layer + 1],
                                        chip.fcol[:, 2:3], ALU.add, ALU.mult).then_inc(step, 1)
                dve.wait_ge(step, at + 1)
                nc.vector.tensor_scalar(turn[:, :], arg[:, :], turns, big, ALU.mult, ALU.add).then_inc(step, 1)
                dve.wait_ge(step, at + 2)
                nc.vector.tensor_scalar(turn[:, :], turn[:, :], big, None, ALU.subtract).then_inc(step, 1)
                for k, part in enumerate((c1, c2, c3)):
                    dve.wait_ge(step, at + 3 + k)
                    nc.vector.scalar_tensor_tensor(out=arg[:, :], in0=turn[:, :], scalar=-part, in1=arg[:, :],
                                                   op0=ALU.mult, op1=ALU.add).then_inc(step, 1)
                dve.wait_ge(step, at + 6)
                nc.vector.tensor_scalar(arg[:, :], arg[:, :], -pi, pi, ALU.max, ALU.min).then_inc(step, 1)

            dve.wait_ge(decay_loaded, 16)
            dve.wait_ge(sine, 2)
            dve.wait_ge(x_turned, TT)
            for o in range(2):
                def mix(i, slot, o=o):
                    u = TT * o + i
                    dve.wait_ge(taps_out, u + 1)
                    if later(o, i, 2):
                        dve.wait_ge(lo_ready, u - 1)
                        dve.wait_ge(absed, u - 1)
                    dec = decay[:, ds(i, 1), :].to_broadcast([P, 2, C])
                    done = nc.vector.tensor_tensor(mixd[slot][:, :, :], chip.pair(slot).rearrange("p (m c) -> p m c", m=2),
                                                   dec, ALU.mult)
                    if isinstance(i, int) and i == 0:
                        done.then_inc(edge, 1)
                        dve.wait_ge(edge, 3 * o + 1)
                        first = mixd[slot][0:1, :, :]
                        nc.vector.tensor_tensor(first[:, 0, :], first[:, 0, :], first[:, 1, :], ALU.add).then_inc(edge, 1)
                        dve.wait_ge(edge, 3 * o + 2)
                        nc.vector.tensor_scalar(first[:, 0, :], first[:, 0, :], 0.5, None, ALU.mult).then_inc(edge, 1)
                        dve.wait_ge(edge, 3 * o + 3)
                        nc.vector.tensor_copy(first[:, 1, :], first[:, 0, :]).then_inc(mixed, 1)
                    else:
                        done.then_inc(mixed, 1)

                def low(i, slot, o=o):
                    dve.wait_ge(mixed, TT * o + i + 1)
                    dve.wait_ge(hi_ready, TT * o + i + 1)
                    nc.vector.tensor_tensor(at_tile(tap_lo, i), mixd[slot][:, :, :], at_tile(tap_hi, i).bitcast(F32),
                                            ALU.subtract).then_inc(lo_ready, 1)

                def magnitude(i, slot, o=o):
                    dve.wait_ge(absed, TT * o + i + 1)
                    if later(o, i, 2):
                        dve.wait_ge(mag_summed, TT * o + i - 1)
                    nc.vector.tensor_tensor(mag[slot][:, :], absd[slot][:, 0, :], absd[slot][:, 1, :],
                                            ALU.max).then_inc(mag_ready, 1)

                mix(0, 0)
                mix(1, 1)
                low(0, 0)
                magnitude(0, 0)
                with by_two(dve, 2, TT) as i:
                    mix(i, 0)
                    low(i - 1, 1)
                    magnitude(i - 1, 1)
                    mix(i + 1, 1)
                    low(i, 0)
                    magnitude(i, 0)
                low(TT - 1, 1)
                magnitude(TT - 1, 1)
                dve.wait_ge(mag_summed, TT * (o + 1))
                if o == 1:
                    dve.wait_ge(spec_step, SPEC_STEPS * WT)
                nc.vector.reciprocal(rnorm[:, :], chip.bank(7)).then_inc(rnorm_ready, 1)
                dve.wait_ge(rnorm_ready, o + 1)
                if o == 0:
                    dve.wait_ge(skip_loaded, 16)

                scale = rnorm[:, :].unsqueeze(1).to_broadcast([P, 2, C])
                for wt in range(WT):
                    t = WT * o + wt
                    at = SPEC_STEPS * t
                    dve.wait_ge(table_used, 2 * t + 1)
                    if t:
                        dve.wait_ge(spec_step, at)
                    nc.vector.tensor_tensor(even[:, :, :], chip.pair(0).rearrange("p (a c) -> p a c", a=2), scale,
                                            ALU.mult).then_inc(even_scaled, 1)
                    dve.wait_ge(even_scaled, 2 * t + 1)
                    nc.vector.tensor_tensor(even[:, 0, :], even[:, 0, :], skip[:, o, :], ALU.add).then_inc(even_scaled, 1)
                    dve.wait_ge(table_used, 2 * t + 2)
                    nc.vector.tensor_tensor(odd[:, :, :], chip.pair(1).rearrange("p (a c) -> p a c", a=2), scale,
                                            ALU.mult).then_inc(spec_step, 1)
                    dve.wait_ge(spec_step, at + 1)
                    dve.wait_ge(even_scaled, 2 * t + 2)
                    if t:
                        dve.wait_ge(spec_stored, 16 * t)
                    nc.vector.tensor_tensor(spec[:, 0:2, :], even[:, :, :], odd[:, :, :], ALU.add).then_inc(spec_step, 1)
                    nc.vector.tensor_tensor(spec[:, 2, :], even[:, 0, :], odd[:, 0, :], ALU.subtract).then_inc(spec_step, 1)
                    nc.vector.tensor_tensor(spec[:, 3, :], odd[:, 1, :], even[:, 1, :], ALU.subtract).then_inc(spec_step, 1)
                    if t == 0:
                        norm.invert(dve)


class Ffn:
    STEPS = FFN // (2 * P)

    def __init__(self, chip, tag, w_gate, w_up, w_down, xT, norm, kb):
        self.chip, self.nc, self.xT, self.norm = chip, chip.nc, xT, norm
        self.w_in = (w_gate, w_up)
        self.w_down = w_down
        self.wgu = [[[chip.at(f"{tag}_w{m}{s}{hl}", kb["wgu"] + 16 * s + 8 * m + 4 * hl, [P, KT, P], F32R) for hl in range(2)]
                     for m in range(2)] for s in range(2)]
        self.wd = [chip.at(f"{tag}_wd{hl}", kb["wd"] + 8 * hl, [P, 2, D], F32R) for hl in range(2)]
        self.gu_raw = [chip.at(f"{tag}_gu_raw{m}", kb["gu_raw"][m], [P, KT, 2 * P]) for m in range(2)]
        self.d_raw = chip.at(f"{tag}_d_raw", kb["d_raw"], [P, 2, D])
        self.h = [[chip.at(f"{tag}_h{g}{hl}", kb["h"] + 16 * g + 8 * hl, [P, 2, SEQ], F32R) for hl in range(2)]
                  for g in range(2)]
        self.wd_last = [chip.at(f"{tag}_wd_last{hl}", kb["wgu"] + 8 * hl, [P, 2, D], F32R) for hl in range(2)]
        self.h_whole = [chip.at(f"{tag}_h_whole{g}", kb["h"] + 16 * g + 8, [P, 2, SEQ]) for g in range(2)]
        self.gu_loaded, self.d_loaded = chip.sem(f"{tag}_gu_loaded"), chip.sem(f"{tag}_d_loaded")
        self.gu_hi, self.gu_ready = chip.sem(f"{tag}_gu_hi"), chip.sem(f"{tag}_gu_ready")
        self.d_hi, self.d_ready = chip.sem(f"{tag}_d_hi"), chip.sem(f"{tag}_d_ready")
        self.gate_done, self.up_done = chip.sem(f"{tag}_gate_done"), chip.sem(f"{tag}_up_done")
        self.gate_scaled, self.silu_done = chip.sem(f"{tag}_gate_scaled"), chip.sem(f"{tag}_silu_done")
        self.silu_scaled, self.h_made = chip.sem(f"{tag}_silu_scaled"), chip.sem(f"{tag}_h_made")
        self.h_hi, self.h_ready = chip.sem(f"{tag}_h_hi"), chip.sem(f"{tag}_h_ready")
        self.d_done, self.y_added = chip.sem(f"{tag}_d_done"), chip.sem(f"{tag}_y_added")

    def load_gu(self, sp, g, which=(0, 1)):
        for m in which:
            sp.dma_start(self.gu_raw[m][:], self.w_in[m].rearrange("(k p) f -> p k f", p=P)[:, :, ds(g * 2 * P, 2 * P)]
                         ).then_inc(self.gu_loaded, 16)

    def load_d(self, sp, g):
        sp.dma_start(self.d_raw[:], self.w_down[ds(g * 2 * P, 2 * P), :].rearrange("(a p) d -> p a d", p=P)
                     ).then_inc(self.d_loaded, 16)

    def round_gu(self, act, g, s, which=(0, 1)):
        for m in which:
            if m == 0 and s == 0:
                act.wait_ge(self.gu_loaded, 32 * (g + 1))
            if m == 0 and not (isinstance(g, int) and g == 0):
                act.wait_ge(self.up_done, 2 * (g - 1) + s + 1)
            self.nc.scalar.activation(self.wgu[s][m][0][:, :, :], self.gu_raw[m][:, :, s * P:(s + 1) * P],
                                      ACT.Copy).then_inc(self.gu_hi, 1)

    def rest_gu(self, dve, g, s, which=(0, 1)):
        for m in which:
            dve.wait_ge(self.gu_hi, 4 * g + 2 * s + m + 1)
            self.nc.vector.tensor_tensor(self.wgu[s][m][1][:, :, :], self.gu_raw[m][:, :, s * P:(s + 1) * P],
                                         self.wgu[s][m][0][:, :, :].bitcast(F32), ALU.subtract).then_inc(self.gu_ready, 1)

    def loop(self, eng, step):
        step(0, 0)
        step(1, 1)
        with by_two(eng, 2, self.STEPS - 1) as g:
            step(g, 0)
            step(g + 1, 1)
        step(self.STEPS - 1, 0)
        step(self.STEPS, 1)

    def run(self, split_here, after=None):
        nc, chip, STEPS, norm = self.nc, self.chip, self.STEPS, self.norm
        x_hi, x_lo, xT = norm.hi, norm.lo, self.xT

        def at_first(g):
            return isinstance(g, int) and g == 0

        def is_tail(g):
            return isinstance(g, int) and g == STEPS

        def has_next(g):
            return not (isinstance(g, int) and g >= STEPS - 1)

        def down_weights(g):
            return self.wd if has_next(g) else self.wd_last

        with nc.Block() as block:
            @block.sync
            def _(sp):
                def step(g, slot):
                    if has_next(g):
                        sp.wait_ge(self.gu_ready, 4 * (g + 1))
                        self.load_gu(sp, g + 1)
                        sp.wait_ge(self.d_ready, 2 * (g + 1))
                        self.load_d(sp, g + 1)
                self.load_d(sp, 0)
                self.loop(sp, step)
                if after is not None:
                    sp.wait_ge(self.d_ready, 2 * STEPS)
                    for n in range(2):
                        after.weights.load(sp, n, n, n * P)

            @block.tensor
            def _(pe):
                def gate_up(g, s):
                    n = 2 * g + s
                    for m in range(2):
                        pe.wait_ge(self.gu_ready, 4 * g + 2 * s + m + 1)
                        if not (at_first(g) and s == 0):
                            pe.wait_ge((self.gate_scaled, self.h_made)[m], n)
                        elif m == 1:
                            pe.wait_ge(norm.rooted, 1)
                        for k in range(KT):
                            if split_here and m == 0 and s == 0 and at_first(g):
                                pe.wait_ge(norm.lo_ready, k + 1)
                            last = three_pass(nc, [chip.bank(2 * m), chip.bank(2 * m + 1)], self.wgu[s][m][0][:, k, :],
                                              self.wgu[s][m][1][:, k, :], halves(x_hi, k), halves(x_lo, k),
                                              k == 0, k == KT - 1)
                        last.then_inc((self.gate_done, self.up_done)[m], 1)

                def down(g, slot, part):
                    h_hi, h_lo = self.h[slot]
                    if part == 0:
                        pe.wait_ge(self.d_ready, 2 * (g + 1))
                        pe.wait_ge(self.h_ready, 2 * (g + 1))
                    for d in range(4 * part, 4 * part + 4):
                        if not (isinstance(g, int) and g == 0 and d < 2):
                            pe.wait_ge(self.y_added, KT * g + d - 1)
                        w_hi, w_lo = down_weights(g)
                        for a in range(2):
                            last = three_pass(nc, [chip.bank(4 + 2 * (d % 2)), chip.bank(5 + 2 * (d % 2))],
                                              w_hi[:, a, d * P:(d + 1) * P], w_lo[:, a, d * P:(d + 1) * P],
                                              halves(h_hi, a), halves(h_lo, a), a == 0, a == 1)
                        last.then_inc(self.d_done, 1)

                def step(g, slot):
                    if not is_tail(g):
                        gate_up(g, 0)
                    if not at_first(g):
                        down(g - 1, 1 - slot, 0)
                    if not is_tail(g):
                        gate_up(g, 1)
                    if not at_first(g):
                        down(g - 1, 1 - slot, 1)
                self.loop(pe, step)
                if after is not None:
                    after.norm.tensor(pe)

            @block.scalar
            def _(act):
                def round_d(g):
                    act.wait_ge(self.d_loaded, 16 * (g + 1))
                    if not has_next(g):
                        act.wait_ge(self.up_done, 2 * g + 1)
                    elif not at_first(g):
                        act.wait_ge(self.d_done, KT * g)
                    for a in range(2):
                        nc.scalar.activation(down_weights(g)[0][:, a, :], self.d_raw[:, a, :], ACT.Copy).then_inc(self.d_hi, 1)

                def hidden(g, s, slot):
                    n = 2 * g + s
                    h_hi, h = self.h[slot][0][:, s, :], self.h_whole[slot][:, s, :]
                    act.wait_ge(self.gate_scaled, n + 1)
                    nc.scalar.activation(h, h, ACT.Silu).then_inc(self.silu_done, 1)
                    act.wait_ge(self.h_made, n + 1)
                    if not isinstance(g, int) or g >= 2:
                        act.wait_ge(self.d_done, KT * (g - 1))
                    nc.scalar.activation(h_hi, h, ACT.Copy).then_inc(self.h_hi, 1)

                if split_here:
                    self.round_gu(act, 0, 0, (0,))
                    for k in range(KT):
                        if k == KT - 2:
                            act.wait_ge(chip.spec_stored, 16 * 2 * WT)
                        norm.round(act, k)
                        if k == KT // 2:
                            self.round_gu(act, 0, 0, (1,))
                else:
                    self.round_gu(act, 0, 0)
                    norm.root_of_mean(act)
                self.round_gu(act, 0, 1)

                def step(g, slot):
                    if is_tail(g):
                        return
                    if not at_first(g):
                        round_d(g - 1)
                    for s in range(2):
                        hidden(g, s, slot)
                        if has_next(g):
                            self.round_gu(act, g + 1, s)
                        elif s == 0:
                            round_d(g)
                self.loop(act, step)
                if after is not None:
                    act.wait_ge(self.up_done, 2 * STEPS)
                    act.wait_ge(self.gu_ready, 4 * STEPS)
                    for k in range(KT):
                        after.norm.scalar(act, k, self.y_added, KT * (STEPS - 1) + k + 1)
                        if k in (1, 3):
                            after.weights.round(act, k // 2, k // 2)

            @block.gpsimd
            def _(pool):
                if after is not None:
                    after.norm.gpsimd(pool)

            @block.vector
            def _(dve):
                def rest_d(g):
                    for a in range(2):
                        dve.wait_ge(self.d_hi, 2 * g + a + 1)
                        w_hi, w_lo = down_weights(g)
                        nc.vector.tensor_tensor(w_lo[:, a, :], self.d_raw[:, a, :], w_hi[:, a, :].bitcast(F32),
                                                ALU.subtract).then_inc(self.d_ready, 1)

                def add(g, d):
                    dve.wait_ge(self.d_done, KT * g + d + 1)
                    if not (isinstance(g, int) and g == 0):
                        dve.wait_ge(self.y_added, KT * g + d + 1 - KT)
                    nc.vector.scalar_tensor_tensor(out=xT[:, d, :], in0=chip.pair(2 + d % 2), scalar=0.5,
                                                   in1=xT[:, d, :], op0=ALU.mult, op1=ALU.add).then_inc(self.y_added, 1)

                def scale_gate(g, s, slot):
                    n = 2 * g + s
                    dve.wait_ge(self.gate_done, n + 1)
                    if not isinstance(g, int) or g >= 2:
                        dve.wait_ge(self.d_done, KT * (g - 1))
                    nc.vector.tensor_tensor(self.h_whole[slot][:, s, :], chip.pair(0), norm.rstd[:, :],
                                            ALU.mult).then_inc(self.gate_scaled, 1)

                def make_h(g, s, slot):
                    n = 2 * g + s
                    h = self.h_whole[slot][:, s, :]
                    dve.wait_ge(self.silu_done, n + 1)
                    nc.vector.tensor_tensor(h, h, norm.rstd[:, :], ALU.mult).then_inc(self.silu_scaled, 1)
                    dve.wait_ge(self.silu_scaled, n + 1)
                    dve.wait_ge(self.up_done, n + 1)
                    nc.vector.tensor_tensor(h, h, chip.pair(1), ALU.mult).then_inc(self.h_made, 1)

                def rest_h(g, s, slot):
                    n = 2 * g + s
                    dve.wait_ge(self.h_made, n + 1)
                    dve.wait_ge(self.h_hi, n + 1)
                    nc.vector.tensor_tensor(self.h[slot][1][:, s, :], self.h_whole[slot][:, s, :], self.h[slot][0][:, s, :].bitcast(F32),
                                            ALU.subtract).then_inc(self.h_ready, 1)

                if split_here:
                    self.rest_gu(dve, 0, 0, (0,))
                    for k in range(KT):
                        norm.vector(dve, k)
                        if k == KT // 2 + 1:
                            self.rest_gu(dve, 0, 0, (1,))
                else:
                    self.rest_gu(dve, 0, 0)
                    norm.invert(dve)
                self.rest_gu(dve, 0, 1)

                def step(g, slot):
                    if not (at_first(g) or is_tail(g)):
                        rest_d(g - 1)
                    for s in range(2):
                        if is_tail(g):
                            for d in range(4 * s, 4 * s + 4):
                                add(g - 1, d)
                                if after is not None and d:
                                    after.norm.vector(dve, d - 1)
                                    if d in (3, 5):
                                        after.weights.rest(dve, d // 4, d // 4)
                            continue
                        scale_gate(g, s, slot)
                        make_h(g, s, slot)
                        if not at_first(g):
                            add(g - 1, 4 * s)
                        rest_h(g, s, slot)
                        if not at_first(g):
                            add(g - 1, 4 * s + 1)
                        if has_next(g):
                            self.rest_gu(dve, g + 1, s)
                        elif s == 0:
                            rest_d(g)
                        if not at_first(g):
                            add(g - 1, 4 * s + 2)
                            add(g - 1, 4 * s + 3)
                    if is_tail(g) and after is not None:
                        after.norm.vector(dve, KT - 1)
                self.loop(dve, step)


class ColumnWeights:

    def __init__(self, chip, tag, weights, raw_kb, split_kb):
        self.chip, self.nc, self.weights = chip, chip.nc, weights
        self.raw = [chip.at(f"{tag}_raw{s}", raw_kb + 4 * s, [P, KT, P]) for s in range(2)]
        self.split = [[chip.at(f"{tag}_split{s}{hl}", split_kb + 8 * s + 4 * hl, [P, KT, P], F32R) for hl in range(2)]
                      for s in range(2)]
        self.loaded = [chip.sem(f"{tag}_loaded{s}") for s in range(2)]
        self.hi, self.ready, self.used = chip.sem(f"{tag}_hi"), chip.sem(f"{tag}_ready"), chip.sem(f"{tag}_used")

    def load(self, sp, n, slot, col, cols=P):
        sp.dma_start(self.raw[slot][:, :, 0:cols],
                     self.weights.rearrange("(k p) c -> p k c", p=P)[:, :, ds(col, cols)]).then_inc(self.loaded[slot], 16)

    def round(self, act, n, slot, cols=P):
        act.wait_ge(self.loaded[slot], 8 * (n - slot) + 16)
        if not isinstance(n, int) or n >= 2:
            act.wait_ge(self.used, n - 1)
        self.nc.scalar.activation(self.split[slot][0][:, :, 0:cols], self.raw[slot][:, :, 0:cols], ACT.Copy).then_inc(self.hi, 1)

    def rest(self, dve, n, slot, cols=P):
        dve.wait_ge(self.hi, n + 1)
        self.nc.vector.tensor_tensor(self.split[slot][1][:, :, 0:cols], self.raw[slot][:, :, 0:cols],
                                     self.split[slot][0][:, :, 0:cols].bitcast(F32), ALU.subtract).then_inc(self.ready, 1)

    def product(self, pe, n, slot, outs, x_hi, x_lo, done, cols=P):
        pe.wait_ge(self.ready, n + 1)
        for k in range(KT):
            last = three_pass(self.nc, outs, self.split[slot][0][:, k, 0:cols], self.split[slot][1][:, k, 0:cols],
                              halves(x_hi, k), halves(x_lo, k), k == 0, k == KT - 1)
        last.then_inc(self.used, 1)


HEAD_TILES = 4
HY_TILES = 3 * C // P


class MixerInput:

    def __init__(self, norm, weights):
        self.norm, self.weights = norm, weights


def mixer_in_block(chip, xT, residual, w, norm, cq, ckv, kr, v_hi, v_lo, gates, conv_w, conv_b, hyena):
    nc = chip.nc
    x_hi, x_lo, rstd = norm.hi, norm.lo, norm.rstd
    spilled = chip.sem("m_spilled")
    padded = [chip.at(f"m_padded{s}", 144 + 4.25 * s, [P, SEQ + 2]) for s in range(2)]
    conv = [chip.at(f"m_conv{s}", 184 + 4 * s, [P, SEQ]) for s in range(2)]
    s = chip.sem
    evacuated, pads, conv_step = s("m_evacuated"), s("m_pads"), s("m_conv_step")
    kr_copied = s("m_kr_copied")
    latent_squares = chip.at("m_latent_squares", 112, [P, 2, SEQ])
    q_norm = LatentNorm(chip, "mq", cq, Q_RANK // P, chip.q_gain, latent_squares, chip.at("m_q_root", 120, [P, SEQ]), 2)
    kv_norm = LatentNorm(chip, "mkv", ckv, KV_RANK // P, chip.kv_gain, latent_squares,
                         chip.at("m_kv_root", 124, [P, SEQ]), 3)
    turned, v_rounded, settled = s("m_turned"), s("m_v_rounded"), s("m_settled")
    HY0 = HEAD_TILES
    N = HEAD_TILES + HY_TILES

    def col(n):
        return n * P if n < 3 else Q_RANK + KV_RANK

    with nc.Block() as block:
        @block.sync
        def _(sp):
            sp.dma_start(residual, xT[:]).then_inc(spilled, 16)
            hyena.load_table(sp, 0)
            for n in range(2, HEAD_TILES):
                sp.wait_ge(w.ready, n - 1)
                w.load(sp, n, n % 2, col(n), ROPE if n == 3 else P)
            with by_two(sp, 0, HY_TILES) as j:
                for a in range(2):
                    sp.wait_ge(w.ready, HY0 + j + a - 1)
                    w.load(sp, HY0 + j + a, a, (j + a) * P + (Q_RANK + KV_RANK + ROPE))
            sp.wait_ge(spilled, 16)

        @block.tensor
        def _(pe):
            for n in range(HEAD_TILES):
                cols = ROPE if n == 3 else P
                if n >= 2:
                    pe.wait_ge(evacuated, n - 1)
                elif n == 1:
                    pe.wait_ge(norm.rooted, 1)
                w.product(pe, n, n % 2, [chip.bank(2 * (n % 2), cols), chip.bank(2 * (n % 2) + 1, cols)],
                          x_hi, x_lo, None, cols)

            def product(j, slot):
                pe.wait_ge(evacuated, HY0 + j - 1)
                w.product(pe, HY0 + j, slot, [chip.bank(2 * slot), chip.bank(2 * slot + 1)], x_hi, x_lo, None)

            def turn(j, slot):
                pe.wait_ge(conv_step, 3 * (j + 1))
                if not isinstance(j, int) or j >= 2:
                    pe.wait_ge(settled, j - 1)
                for i in range(TT):
                    start = (i // 4) + 2 * P * (i % 4)
                    at = (2 + slot) * 2 * HALF + i * P
                    last = nc.tensor.transpose(chip.ps[:, at:at + P], conv[slot][:, start:start + 2 * P - 1:2],
                                               chip.ident[:, :])
                last.then_inc(turned, 1)

            product(0, 0)
            q_norm.sum(pe)
            product(1, 1)
            kv_norm.sum(pe)
            pe.wait_ge(q_norm.rooted, 1)
            turn(0, 0)
            product(2, 0)
            pe.wait_ge(kv_norm.rooted, 1)
            turn(1, 1)
            product(3, 1)
            turn(2, 0)
            with by_two(pe, 4, HY_TILES) as j:
                product(j, 0)
                turn(j - 1, 1)
                product(j + 1, 1)
                turn(j, 0)
            turn(HY_TILES - 1, 1)

        @block.scalar
        def _(act):
            norm.root_of_mean(act)
            for n in range(1, HEAD_TILES):
                w.round(act, n + 1, (n + 1) % 2, ROPE if n + 1 == 3 else P)
                if n >= 2:
                    act.wait_ge(evacuated, n - 1)
                    q_norm.square(act, n - 2)
            act.wait_ge(w.used, HEAD_TILES)
            nc.scalar.activation(kr[NOPE:QK, :], chip.pair(1, ROPE), ACT.Copy).then_inc(kr_copied, 1)
            act.wait_ge(spilled, 16)

            def round_v(j, slot):
                act.wait_ge(turned, j + 1)
                nc.scalar.activation(v_hi[:, :, j * P:(j + 1) * P], chip.pair(2 + slot).rearrange("p (i c) -> p i c", i=TT),
                                     ACT.Copy).then_inc(v_rounded, 1)

            for j in range(C // P + 2):
                w.round(act, HY0 + j + 1, 1 - j % 2)
                if j == 0:
                    q_norm.root_of_mean(act)
                    kv_norm.square(act, 0)
                elif j == 1:
                    kv_norm.root_of_mean(act)
                if 1 <= j <= C // P:
                    round_v(j - 1, (j - 1) % 2)
            with by_two(act, C // P + 2, HY_TILES - 2) as j:
                w.round(act, HY0 + j + 1, 1)
                w.round(act, HY0 + j + 2, 0)
            w.round(act, N - 1, 1)

        @block.vector
        def _(dve):
            for k in range(2):
                nc.vector.memset(padded[k][:, 0:1], 0.0).then_inc(pads, 1)
                nc.vector.memset(padded[k][:, SEQ + 1:SEQ + 2], 0.0).then_inc(pads, 1)
            norm.invert(dve)
            for n in range(HEAD_TILES):
                if n:
                    w.rest(dve, n + 1, (n + 1) % 2, ROPE if n + 1 == 3 else P)
                dve.wait_ge(w.used, n + 1)
                if n == 3:
                    dve.wait_ge(kr_copied, 1)
                    nc.vector.tensor_tensor(kr[NOPE:QK, :], kr[NOPE:QK, :], rstd[NOPE:QK, :],
                                            ALU.mult).then_inc(evacuated, 1)
                else:
                    dst = (cq[:, 0, :], cq[:, 1, :], ckv[:, 0, :])[n]
                    nc.vector.tensor_tensor(dst, chip.pair(n % 2), rstd[:, :], ALU.mult).then_inc(evacuated, 1)
            dve.wait_ge(pads, 4)

            def convolve(j, slot):
                dve.wait_ge(w.used, HY0 + j + 1)
                if not isinstance(j, int) or j >= 2:
                    dve.wait_ge(conv_step, 3 * (j - 1))
                nc.vector.tensor_tensor(padded[slot][:, 1:SEQ + 1], chip.pair(slot), rstd[:, :],
                                        ALU.mult).then_inc(evacuated, 1)
                dve.wait_ge(evacuated, HY0 + j + 1)
                if not isinstance(j, int) or j >= 2:
                    dve.wait_ge(turned, j - 1)
                taps = [conv_w[:, tap, ds(j, 1)] for tap in range(3)]
                nc.vector.tensor_scalar(conv[slot][:, :], padded[slot][:, 0:SEQ], taps[0], conv_b[:, ds(j, 1)],
                                        ALU.mult, ALU.add).then_inc(conv_step, 1)
                for tap in (1, 2):
                    dve.wait_ge(conv_step, 3 * j + tap)
                    nc.vector.scalar_tensor_tensor(out=conv[slot][:, :], in0=padded[slot][:, tap:tap + SEQ],
                                                   scalar=taps[tap], in1=conv[slot][:, :], op0=ALU.mult,
                                                   op1=ALU.add).then_inc(conv_step, 1)

            def tokens(slot):
                return chip.pair(2 + slot).rearrange("p (i c) -> p i c", i=TT)

            def v_low(j, slot):
                dve.wait_ge(v_rounded, j + 1)
                nc.vector.tensor_tensor(v_lo[:, :, ds(j * P, P)], tokens(slot),
                                        v_hi[:, :, ds(j * P, P)].bitcast(F32), ALU.subtract).then_inc(settled, 1)

            def gate(j, slot, dst):
                dve.wait_ge(turned, j + 1)
                nc.vector.tensor_copy(dst, tokens(slot)).then_inc(settled, 1)

            def step(group, k, slot):
                j = group * (C // P) + k
                if not (isinstance(j, int) and j >= HY_TILES - 2):
                    w.rest(dve, HY0 + j + 2, slot)
                if not (isinstance(j, int) and j == HY_TILES - 1):
                    convolve(j + 1, 1 - slot)
                if group == 0:
                    v_low(j, slot)
                else:
                    gate(j, slot, gates[group - 1][:, :, ds(k * P, P)])

            w.rest(dve, HY0 + 1, 1)
            convolve(0, 0)
            latents = (q_norm.invert, q_norm.scale, kv_norm.invert, kv_norm.scale)
            for k in range(C // P):
                step(0, k, k % 2)
                latents[k](dve)
            with by_two(dve, 0, C // P) as k:
                step(1, k, 0)
                step(1, k + 1, 1)
            for k in range(C // P):
                step(2, k, k % 2)


class AttentionInput:

    def __init__(self, chip, dram, cq, ckv):
        self.chip, self.nc, self.dram, self.cq, self.ckv = chip, chip.nc, dram, cq, ckv
        self.cq_hi, self.cq_lo = (chip.at(f"a_cq{h}", 8 * h, [P, 2, SEQ], F32R) for h in range(2))
        self.ckv_hi, self.ckv_lo = (chip.at(f"a_ckv{h}", 16 + 4 * h, [P, 1, SEQ], F32R) for h in range(2))
        self.wq_raw = [chip.at(f"a_wq_raw{k}", 97 + 0.75 * k, [P, 2, QK]) for k in range(2)]
        self.wk_raw = [chip.at(f"a_wk_raw{k}", 98.5 + 0.25 * k, [P, NOPE]) for k in range(2)]
        self.wq = [[chip.at(f"a_wq{k}{h}", 99 + 1.5 * k + 0.75 * h, [P, 2, QK], F32R) for h in range(2)] for k in range(2)]
        self.wk = [[chip.at(f"a_wk{k}{h}", 102 + 0.5 * k + 0.25 * h, [P, NOPE], F32R) for h in range(2)] for k in range(2)]
        self.wv_raw = chip.at("a_wv_raw", 103, [P, HEADS * VD])
        self.wv = [chip.at(f"a_wv{h}", 105 + 2 * h, [P, HEADS * VD], F32R) for h in range(2)]
        self.loaded, self.hi, self.ready = chip.sem("ai_loaded"), chip.sem("ai_hi"), chip.sem("ai_ready")
        self.parts = [(self.wq[0][0][:, :, :], self.wq[0][1][:, :, :], self.wq_raw[0][:, :, :]),
                      (self.wk[0][0][:, :], self.wk[0][1][:, :], self.wk_raw[0][:, :]),
                      (self.wv[0][:, :], self.wv[1][:, :], self.wv_raw[:, :]),
                      (self.cq_hi[:, 0, :], self.cq_lo[:, 0, :], cq[:, 0, :]),
                      (self.cq_hi[:, 1, :], self.cq_lo[:, 1, :], cq[:, 1, :]),
                      (self.ckv_hi[:, 0, :], self.ckv_lo[:, 0, :], ckv[:, 0, :])]

    def load(self, sp):
        w_ukv = self.dram["w_ukv"].rearrange("k (h t d) -> k h t d", h=HEADS, t=2)
        sp.dma_start(self.wq_raw[0][:], self.dram["w_uq"].rearrange("(k p) c -> p k c", p=P)[:, :, 0:QK]
                     ).then_inc(self.loaded, 16)
        sp.dma_start(self.wk_raw[0][:], self.dram["w_ukv"][:, 0:NOPE]).then_inc(self.loaded, 16)
        sp.dma_start(self.wv_raw[:, :].rearrange("p (h d) -> p h d", h=HEADS), w_ukv[:, :, 1, :]).then_inc(self.loaded, 16)

    def round(self, act):
        act.wait_ge(self.loaded, 48)
        for hi, lo, src in self.parts:
            self.nc.scalar.activation(hi, src, ACT.Copy).then_inc(self.hi, 1)

    def rest(self, dve):
        for n, (hi, lo, src) in enumerate(self.parts):
            dve.wait_ge(self.hi, n + 1)
            self.nc.vector.tensor_tensor(lo, src, hi.bitcast(F32), ALU.subtract).then_inc(self.ready, 1)


class Hyena:
    ORDER = (("f", 0, 0), ("f", 0, 1), ("f", 1, 0), ("f", 1, 1), ("f", 2, 0), ("i", 0, 0), ("f", 2, 1), ("i", 0, 1),
             ("f", 3, 0), ("f", 3, 1), ("i", 0, 2), ("i", 1, 0), ("i", 1, 1), ("i", 1, 2), ("i", 0, 3), ("i", 1, 3))
    UNITS = len(ORDER)
    SLOTS = 3
    STEPS, POOL_STEPS = 9, 3

    def __init__(self, chip, dram):
        self.chip, self.nc, self.dram = chip, chip.nc, dram
        self.table = [chip.at(f"y_table{k}", kb, [P, TT // 2, 2, 2, P], F32R) for k, kb in enumerate((192, 144, 152))]
        self.table_loaded = [chip.sem(f"y_table_loaded{k}") for k in range(self.SLOTS)]

    def load_table(self, sp, n):
        kind, a, b = self.ORDER[n % self.UNITS]
        row = (a * (2 if kind == "f" else WT) + b) * P
        src = self.dram["fwd" if kind == "f" else "inv"]
        sp.dma_start(self.table[n % self.SLOTS][:].bitcast(F32), src[row:row + P, :]).then_inc(
            self.table_loaded[n % self.SLOTS], 16)

    def run(self, v_hi, v_lo, gates, after):
        chip, nc, dram, UNITS, STEPS = self.chip, self.nc, self.dram, self.UNITS, self.STEPS
        spec_hi = chip.at("y_spec_hi", 32, [P, 4, WT, C], F32R)
        spec_lo = chip.at("y_spec_lo", 64, [P, 4, WT, C], F32R)
        filt = chip.at("y_filt", 160, [P, 4, C])
        even = chip.at("y_even", 168, [P, 2, C])
        work = chip.at("y_work", 172, [P, 8, C])
        z = chip.at("y_z", 188, [P, 2, C])
        s = chip.sem
        filt_loaded, table_used, even_copied, work_step = (s("y_filt_loaded"), s("y_table_used"), s("y_even_copied"),
                                                           s("y_work_step"))
        pool_step = s("y_pool_step")
        spec_hi_ready, spec_lo_ready = s("y_spec_hi_ready"), s("y_spec_lo_ready")
        out_ready, z_made, z_hi, z_lo = s("y_out_ready"), s("y_z_made"), s("y_z_hi"), s("y_z_lo")

        def after_unit(q, *unit):
            return UNITS * q + self.ORDER.index(unit) + 1

        def out_bank(i):
            return chip.bank(4 + i if i < TT // 2 else i - TT // 2)

        with nc.Block() as block:
            @block.sync
            def _(sp):
                def load_filter(n):
                    if n:
                        sp.wait_ge(work_step, STEPS * (n - 1) + 5)
                        sp.wait_ge(pool_step, self.POOL_STEPS * (n - 1) + 1)
                    else:
                        sp.wait_ge(chip.spec_stored, 16 * 2 * WT)
                    sp.dma_start(filt[:], dram["spectra"][n * P:(n + 1) * P, :]).then_inc(filt_loaded, 16)

                self.load_table(sp, 1)
                load_filter(0)
                self.load_table(sp, 2)
                for n in range(self.SLOTS, 2 * UNITS):
                    sp.wait_ge(table_used, n - self.SLOTS + 1)
                    self.load_table(sp, n)
                    for tile in range(1, 2 * WT):
                        q, wt = divmod(tile - 1, WT)
                        if n == after_unit(q, "f", wt, 1) + self.SLOTS:
                            load_filter(tile)
                    if n == UNITS + self.SLOTS:
                        after.load(sp)

            @block.tensor
            def _(pe):
                def forward(q, wt, r, table):
                    if q and wt == 0:
                        pe.wait_ge(z_made, TT - 2 + 2 * r)
                    elif wt and r == 0:
                        pe.wait_ge(even_copied, WT * q + wt)
                    elif wt:
                        pe.wait_ge(work_step, STEPS * (WT * q + wt - 1) + 3)
                    for tt in range(TT // 2):
                        i = r * (TT // 2) + tt
                        if q and wt == 0:
                            pe.wait_ge(z_lo, i + 1)
                        for cs in range(2):
                            last = three_pass(nc, [chip.bank(2 * r + cs)], table[:, tt, cs, 0, :], table[:, tt, cs, 1, :],
                                              [v_hi[:, i, :]], [v_lo[:, i, :]], tt == 0, tt == TT // 2 - 1)
                    last.then_inc(table_used, 1)

                def inverse(q, r, wt, table):
                    if r and wt == 0:
                        pe.wait_ge(work_step, STEPS * (WT * q + WT - 1) + 3)
                    elif q and wt == 0:
                        pe.wait_ge(z_made, TT)
                    pe.wait_ge(spec_lo_ready, 2 * (WT * q + wt + 1))
                    for tt in range(TT // 2):
                        for cs in range(2):
                            kind = r + 2 * (1 - cs)
                            last = three_pass(nc, [out_bank(r * (TT // 2) + tt)], table[:, tt, cs, 0, :],
                                              table[:, tt, cs, 1, :], [spec_hi[:, kind, wt, :]], [spec_lo[:, kind, wt, :]],
                                              wt == 0 and cs == 0, wt == WT - 1 and cs == 1)
                        if wt == WT - 1 and tt < TT // 2 - 1:
                            last.then_inc(out_ready, 1)
                    last.then_inc(table_used, 1)

                for n in range(2 * UNITS):
                    kind, a, b = self.ORDER[n % UNITS]
                    pe.wait_ge(self.table_loaded[n % self.SLOTS], 16 * (n // self.SLOTS + 1))
                    (forward if kind == "f" else inverse)(n // UNITS, a, b, self.table[n % self.SLOTS])

            @block.scalar
            def _(act):
                def copy_even(n):
                    q, wt = divmod(n, WT)
                    act.wait_ge(table_used, after_unit(q, "f", wt, 0))
                    if n:
                        act.wait_ge(work_step, STEPS * (n - 1) + 3)
                    nc.scalar.activation(even[:, :, :], chip.pair(0).rearrange("p (a c) -> p a c", a=2),
                                         ACT.Copy).then_inc(even_copied, 1)

                def round_product(n):
                    q, wt = divmod(n, WT)
                    if q:
                        act.wait_ge(table_used, UNITS)
                    for part in range(2):
                        if part == 0:
                            act.wait_ge(work_step, STEPS * (n + 1))
                        else:
                            act.wait_ge(pool_step, self.POOL_STEPS * (n + 1))
                        nc.scalar.activation(spec_hi[:, 2 * part:2 * part + 2, wt, :],
                                             work[:, 4 * part + 1:4 * part + 4:2, :], ACT.Copy).then_inc(spec_hi_ready, 1)

                for q in range(2):
                    copy_even(WT * q)
                    for wt in range(1, WT):
                        copy_even(WT * q + wt)
                        round_product(WT * q + wt - 1)
                    round_product(WT * q + WT - 1)
                    if q == 0:
                        for i in range(TT):
                            act.wait_ge(z_made, i + 1)
                            nc.scalar.activation(v_hi[:, i, :], z[:, i % 2, :], ACT.Copy).then_inc(z_hi, 1)
                act.wait_ge(table_used, after_unit(1, "f", WT - 1, 1))
                after.round(act)

            @block.gpsimd
            def _(pool):
                def op(out, in0, in1, alu):
                    nc.gpsimd.tensor_tensor(out, in0, in1, alu).then_inc(pool_step, 1)

                for n in range(2 * WT):
                    at = self.POOL_STEPS * n
                    pool.wait_ge(filt_loaded, 16 * (n + 1))
                    pool.wait_ge(work_step, STEPS * n + 4)
                    op(work[:, 1:4:2, :], work[:, 1:4:2, :], filt[:, 0:3:2, :], ALU.mult)
                    pool.wait_ge(pool_step, at + 1)
                    pool.wait_ge(work_step, STEPS * n + 6)
                    op(work[:, 5, :], work[:, 4, :], work[:, 6, :], ALU.add)
                    pool.wait_ge(pool_step, at + 2)
                    op(work[:, 7, :], work[:, 4, :], work[:, 6, :], ALU.subtract)
                    pool.wait_ge(pool_step, at + 3)

            @block.vector
            def _(dve):
                def op(out, in0, in1, alu):
                    nc.vector.tensor_tensor(out, in0, in1, alu).then_inc(work_step, 1)

                def multiply(n):
                    q, wt = divmod(n, WT)
                    at = STEPS * n
                    dve.wait_ge(even_copied, n + 1)
                    dve.wait_ge(table_used, after_unit(q, "f", wt, 1))
                    if n:
                        dve.wait_ge(spec_lo_ready, 2 * n)
                        dve.wait_ge(spec_hi_ready, 2 * n)
                    odd = chip.pair(1).rearrange("p (a c) -> p a c", a=2)
                    op(work[:, 0:2, :], even[:, :, :], odd, ALU.add)
                    op(work[:, 2, :], even[:, 0, :], chip.bank(2), ALU.subtract)
                    op(work[:, 3, :], chip.bank(3), even[:, 1, :], ALU.subtract)
                    dve.wait_ge(filt_loaded, 16 * (n + 1))
                    dve.wait_ge(work_step, at + 3)
                    op(work[:, 4:8, :], work[:, 0:4, :], filt[:, :, :], ALU.mult)
                    dve.wait_ge(work_step, at + 4)
                    op(work[:, 0:3:2, :], work[:, 0:3:2, :], filt[:, 1:4:2, :], ALU.mult)
                    op(work[:, 4:7:2, :], work[:, 4:7:2, :], work[:, 5:8:2, :], ALU.subtract)
                    dve.wait_ge(work_step, at + 5)
                    dve.wait_ge(pool_step, self.POOL_STEPS * n + 1)
                    op(work[:, 0:3:2, :], work[:, 0:3:2, :], work[:, 1:4:2, :], ALU.add)
                    dve.wait_ge(work_step, at + 7)
                    op(work[:, 1, :], work[:, 0, :], work[:, 2, :], ALU.subtract)
                    op(work[:, 3, :], work[:, 0, :], work[:, 2, :], ALU.add)
                    dve.wait_ge(work_step, at + 9)
                    dve.wait_ge(pool_step, self.POOL_STEPS * (n + 1))
                    for part in range(2):
                        dve.wait_ge(spec_hi_ready, 2 * n + part + 1)
                        nc.vector.tensor_tensor(spec_lo[:, 2 * part:2 * part + 2, wt, :],
                                                work[:, 4 * part + 1:4 * part + 4:2, :],
                                                spec_hi[:, 2 * part:2 * part + 2, wt, :].bitcast(F32),
                                                ALU.subtract).then_inc(spec_lo_ready, 1)

                def z_low(i):
                    dve.wait_ge(z_made, i + 1)
                    dve.wait_ge(z_hi, i + 1)
                    nc.vector.tensor_tensor(v_lo[:, i, :], z[:, i % 2, :], v_hi[:, i, :].bitcast(F32),
                                            ALU.subtract).then_inc(z_lo, 1)

                for q in range(2):
                    for wt in range(WT):
                        multiply(WT * q + wt)
                    if q:
                        after.rest(dve)
                    for i in range(TT):
                        r, tt = divmod(i, TT // 2)
                        if tt < TT // 2 - 1:
                            dve.wait_ge(out_ready, (TT - 2) * q + (TT // 2 - 1) * r + tt + 1)
                        else:
                            dve.wait_ge(table_used, after_unit(q, "i", r, WT - 1))
                        if q == 0:
                            if i >= 2:
                                dve.wait_ge(z_lo, i - 1)
                            nc.vector.tensor_tensor(z[:, i % 2, :], out_bank(i), gates[0][:, i, :],
                                                    ALU.mult).then_inc(z_made, 1)
                            if i:
                                z_low(i - 1)
                            if i == TT - 1:
                                z_low(i)
                        else:
                            nc.vector.tensor_tensor(gates[1][:, i, :], out_bank(i), gates[1][:, i, :],
                                                    ALU.mult).then_inc(z_made, 1)


def attention_block(chip, dram, given, kr, attn):
    nc = chip.nc
    cq_hi, cq_lo, ckv_hi, ckv_lo = given.cq_hi, given.cq_lo, given.ckv_hi, given.ckv_lo
    wq_raw, wk_raw, wq, wk, wv = given.wq_raw, given.wk_raw, given.wq, given.wk, given.wv
    v_all = chip.at("a_v_all", 24, [P, TT, HEADS * VD])
    v_head = [chip.at(f"a_v{k}", 40 + 4 * k, [P, TT, 2 * VD], F32R) for k in range(2)]
    q_head = [[chip.at(f"a_q{k}{h}", 49 + 8 * k + 4 * h, [QK, SEQ], F32R) for h in range(2)] for k in range(2)]
    k_head = [[chip.at(f"a_k{k}{h}", 65 + 8 * k + 4 * h, [QK, SEQ], F32R) for h in range(2)] for k in range(2)]
    q_row = chip.at("a_q_row", 81, [QK, SEQ])
    swapped = chip.at("a_swapped", 85, [QK, SEQ])
    probs = [chip.at(f"a_probs{k}", 89 + 4 * k, [P, SEQ]) for k in range(2)]
    out_t = [chip.at(f"a_out_t{k}", 109 + k, [P, 2 * P]) for k in range(2)]
    fold = chip.at("a_fold", 111, [P, VD])
    pt = [[chip.at(f"a_pt{k}{h}", 144 + 16 * k + 8 * h, [P, TT, 2 * P], F32R) for h in range(2)] for k in range(2)]
    cos_row = chip.at("a_cos_row", 176, [QK, SEQ])
    sin_row = chip.at("a_sin_row", 180, [QK, SEQ])

    s = chip.sem
    ropes_loaded, k_swapped = s("a_ropes_loaded"), s("a_k_swapped")
    w_loaded = [s(f"a_w_loaded{k}") for k in range(2)]
    v_out, v_stored, fold_made = s("a_v_out"), s("a_v_stored"), s("a_fold_made")
    k_rope_step, rope_hi, rope_ready, sums_kept = (s("a_k_rope_step"), s("a_rope_hi"), s("a_rope_ready"), s("a_sums_kept"))
    w_hi, w_ready = s("a_w_hi"), s("a_w_ready")
    q_out, k_out = s("a_q_out"), s("a_k_out")
    q_rowed, q_swapped, q_roped = s("a_q_rowed"), s("a_q_swapped"), s("a_q_roped")
    q_hi, q_ready, k_hi, k_ready, v_hi, v_ready = (s("a_q_hi"), s("a_q_ready"), s("a_k_hi"), s("a_k_ready"),
                                                   s("a_v_hi"), s("a_v_ready"))
    scored, negmax, exped = s("a_scored"), s("a_negmax"), s("a_exped")
    maxed = s("a_maxed")
    turned, pt_hi, pt_ready = s("a_turned"), s("a_pt_hi"), s("a_pt_ready")
    weighted, out_copied, out_turned, out_stored = (s("a_weighted"), s("a_out_copied"), s("a_out_turned"),
                                                    s("a_out_stored"))
    R = slice(NOPE, QK)
    SCALE = QK ** -0.5
    T_Q, T_K = 1, 3

    def peeled(eng, step):
        step(0, 0)
        with by_two(eng, 1, HEADS - 1) as h:
            step(h, 1)
            step(h + 1, 0)
        step(HEADS - 1, 1)

    def is_last(h):
        return isinstance(h, int) and h == HEADS - 1

    def is_first(h):
        return isinstance(h, int) and h == 0

    def rotate_q(eng, ops, h):
        eng.wait_ge(q_swapped, 32 * (h + 1))
        ops.tensor_tensor(q_row[R, :], q_row[R, :], cos_row[R, :], ALU.mult).then_inc(q_roped, 1)
        eng.wait_ge(q_roped, 3 * h + 1)
        ops.tensor_tensor(swapped[R, :], swapped[R, :], sin_row[R, :], ALU.mult).then_inc(q_roped, 1)
        eng.wait_ge(q_roped, 3 * h + 2)
        ops.tensor_tensor(q_row[R, :], q_row[R, :], swapped[R, :], ALU.add).then_inc(q_roped, 1)

    with nc.Block() as block:
        @block.sync
        def _(sp):
            def load(h, slot):
                sp.dma_start(wq_raw[slot][:], dram["w_uq"].rearrange("(k p) c -> p k c", p=P)[:, :, ds(h * QK, QK)]
                             ).then_inc(w_loaded[slot], 16)
                sp.dma_start(wk_raw[slot][:], dram["w_ukv"][:, ds(h * 2 * VD, NOPE)]).then_inc(w_loaded[slot], 16)

            sp.dma_start(swapped[NOPE:NOPE + 16, :], kr[NOPE + 16:QK, :]).then_inc(k_swapped, 16)
            sp.dma_start(swapped[NOPE + 16:QK, :], kr[NOPE:NOPE + 16, :]).then_inc(k_swapped, 16)
            sp.dma_start(cos_row[R, :], dram["rope"][0:ROPE, :]).then_inc(ropes_loaded, 16)
            sp.dma_start(sin_row[R, :], dram["rope"][ROPE:2 * ROPE, :]).then_inc(ropes_loaded, 16)
            def swap(h):
                sp.wait_ge(q_rowed, h + 1)
                if is_first(h):
                    sp.wait_ge(k_rope_step, 3)
                sp.dma_start(swapped[NOPE:NOPE + 16, :], q_row[NOPE + 16:QK, :]).then_inc(q_swapped, 16)
                sp.dma_start(swapped[NOPE + 16:QK, :], q_row[NOPE:NOPE + 16, :]).then_inc(q_swapped, 16)

            load(1, 1)
            swap(0)

            def step(h, slot):
                if not (isinstance(h, int) and h >= HEADS - 2):
                    if not is_first(h):
                        sp.wait_ge(w_ready, 2 * h)
                    load(h + 2, slot)
                if not is_last(h):
                    swap(h + 1)
            step(0, 0)
            with by_two(sp, 1, HEADS - 3) as h:
                step(h, 1)
                step(h + 1, 0)
            for h in range(HEADS - 3, HEADS):
                step(h, h % 2)

        @block.tensor
        def _(pe):
            def project_v():
                for i in range(TT):
                    if i >= 4:
                        pe.wait_ge(v_stored, i - 3)
                    tok = slice(i * P, (i + 1) * P)
                    three_pass(nc, [chip.bank(4 + i % 4)], ckv_hi[:, 0, tok], ckv_lo[:, 0, tok], [wv[0][:, :]],
                               [wv[1][:, :]], True, True).then_inc(v_out, 1)

            def project_q(h, slot, pair):
                if not is_first(h):
                    pe.wait_ge(w_ready, 2 * h - 1)
                for k in range(2):
                    last = three_pass(nc, [chip.bank(2 * pair, QK), chip.bank(2 * pair + 1, QK)], wq[slot][0][:, k, :],
                                      wq[slot][1][:, k, :], halves(cq_hi, k), halves(cq_lo, k), k == 0, k == 1)
                last.then_inc(q_out, 1)

            def project_k(h, slot, pair):
                if not is_first(h):
                    pe.wait_ge(w_ready, 2 * h)
                three_pass(nc, [chip.bank(2 * pair, NOPE), chip.bank(2 * pair + 1, NOPE)], wk[slot][0][:, :],
                           wk[slot][1][:, :], halves(ckv_hi, 0), halves(ckv_lo, 0), True, True).then_inc(k_out, 1)

            def score(h, t, slot, pair):
                if is_first(h) and t == 0:
                    pe.wait_ge(rope_ready, 2)
                if t == 0:
                    pe.wait_ge(q_ready, h + 1)
                    pe.wait_ge(k_ready, h + 1)
                start = (t // 4) + 2 * P * (t % 4)
                tok = slice(start, start + 2 * P - 1, 2)
                q, k = q_head[slot], k_head[slot]
                three_pass(nc, [chip.bank(2 * pair), chip.bank(2 * pair + 1)], q[0][:, tok], q[1][:, tok],
                           [k[0][:, n * HALF:(n + 1) * HALF] for n in range(2)],
                           [k[1][:, n * HALF:(n + 1) * HALF] for n in range(2)], True, True).then_inc(scored, 1)

            def turn(h, t):
                g = TT * h + t
                pe.wait_ge(exped, g + 1)
                for half in range(2):
                    if not (is_first(h) and t == 0):
                        pe.wait_ge(pt_ready, 2 * g + half - 1)
                    for kt in range(4):
                        last = nc.tensor.transpose(chip.bank(4 + half)[:, kt * P:(kt + 1) * P],
                                                   probs[t % 2][:, (4 * half + kt) * P:(4 * half + kt + 1) * P],
                                                   chip.ident[:, :])
                    last.then_inc(turned, 1)

            def weigh(h, b, half, slot):
                blk = 4 * h + b
                if half == 0:
                    pe.wait_ge(pt_ready, 4 * (blk + 1))
                    if b == 0:
                        pe.wait_ge(v_ready, h + 1)
                    if not (is_first(h) and b < 2):
                        pe.wait_ge(out_stored, blk - 1)
                out, out_hi = chip.bank(6 + b % 2, P, 2 * P), chip.bank(6 + b % 2, VD, 2 * P)
                for kt in range(4 * half, 4 * half + 4):
                    v, v_hi = v_head[slot][:, kt, :], v_head[slot][:, kt, 0:VD]
                    if kt == 0:
                        nc.tensor.matmul(out, v, pt[b % 2][0][:, kt, :], start=True, stop=False)
                        nc.tensor.matmul(out_hi, v_hi, pt[b % 2][1][:, kt, :], start=False, stop=False)
                    else:
                        nc.tensor.matmul(out_hi, v_hi, pt[b % 2][1][:, kt, :], start=False, stop=False)
                        last = nc.tensor.matmul(out, v, pt[b % 2][0][:, kt, :], start=False, stop=(kt == TT - 1))
                if half == 1:
                    last.then_inc(weighted, 1)

            def turn_out(h, b):
                if is_first(h) and b == 0:
                    pe.wait_ge(fold_made, 1)
                pe.wait_ge(out_copied, 4 * h + b + 1)
                for u in range(2):
                    at = (6 + b % 2) * HALF + 2 * P + VD * u
                    last = nc.tensor.matmul(chip.ps[:, at:at + VD], out_t[b % 2][:, u * P:(u + 1) * P], fold[:, :],
                                            start=True, stop=True)
                last.then_inc(out_turned, 1)

            project_q(0, 0, 1)
            project_k(0, 0, 0)
            project_v()
            pe.wait_ge(q_rowed, 1)
            score(0, 0, 0, 1)

            def step(h, slot):
                for t in range(TT):
                    last_head = is_last(h)
                    if t < TT - 1 or not last_head:
                        nxt = (h, t + 1, slot) if t < TT - 1 else (h + 1, 0, 1 - slot)
                        if t + 1 == 1:
                            if is_first(h):
                                pe.wait_ge(k_ready, 1)
                            else:
                                pe.wait_ge(exped, TT * h)
                        elif t == T_Q + 1 and not last_head:
                            pe.wait_ge(q_rowed, h + 2)
                        elif t == T_K + 1 and not last_head:
                            pe.wait_ge(k_ready, h + 2)
                        else:
                            pe.wait_ge(exped, TT * h + t)
                        score(*nxt, t % 2)
                    if t >= 4 and t % 2 == 0:
                        turn_out(h, t // 2 - 2)
                    elif t % 2 == 0 and not is_first(h):
                        turn_out(h - 1, t // 2 + 2)
                    if t in (T_Q, T_K) and not last_head:
                        pe.wait_ge(exped, TT * h + t + 1)
                        (project_q if t == T_Q else project_k)(h + 1, 1 - slot, 0)
                    turn(h, t)
                    if t >= 2:
                        weigh(h, t // 2 - 1, t % 2, slot)
                    elif not is_first(h):
                        weigh(h - 1, 3, t % 2, 1 - slot)

            peeled(pe, step)
            weigh(HEADS - 1, 3, 0, 1)
            weigh(HEADS - 1, 3, 1, 1)
            turn_out(HEADS - 1, 2)
            turn_out(HEADS - 1, 3)

        @block.gpsimd
        def _(pool):
            pool.wait_ge(ropes_loaded, 32)

            def rest_v(h, slot):
                pool.wait_ge(q_roped, 3 * h + 3)
                pool.wait_ge(v_hi, h + 1)
                nc.gpsimd.tensor_tensor(v_head[slot][:, :, VD:2 * VD], v_all[:, :, ds(h * VD, VD)],
                                        v_head[slot][:, :, 0:VD].bitcast(F32), ALU.subtract).then_inc(v_ready, 1)

            def step(h, slot):
                if not is_first(h):
                    pool.wait_ge(v_ready, h)
                    rotate_q(pool, nc.gpsimd, h)
                rest_v(h, slot)
            peeled(pool, step)

        @block.scalar
        def _(act):

            def round_w(h, slot):
                act.wait_ge(w_loaded[slot], 16 * (h - 2) + 32 if slot == 0 else 16 * (h - 1) + 32)
                act.wait_ge(k_out, h)
                nc.scalar.activation(wq[slot][0][:, :, :], wq_raw[slot][:, :, :], ACT.Copy).then_inc(w_hi, 1)
                nc.scalar.activation(wk[slot][0][:, :], wk_raw[slot][:, :], ACT.Copy).then_inc(w_hi, 1)

            def take_q(h, pair):
                act.wait_ge(q_out, h + 1)
                if not is_first(h):
                    act.wait_ge(q_ready, h)
                nc.scalar.activation(q_row[:, :], chip.pair(pair, QK), ACT.Copy, scale=SCALE).then_inc(q_rowed, 1)

            def round_k(h, slot, pair):
                act.wait_ge(k_out, h + 1)
                if not (isinstance(h, int) and h < 2):
                    act.wait_ge(scored, TT * (h - 1))
                nc.scalar.activation(k_head[slot][0][0:NOPE, :], chip.pair(pair, NOPE), ACT.Copy).then_inc(k_hi, 1)

            def round_v(h, slot):
                if not (isinstance(h, int) and h < 2):
                    act.wait_ge(weighted, 4 * (h - 1))
                nc.scalar.activation(v_head[slot][:, :, 0:VD], v_all[:, :, ds(h * VD, VD)], ACT.Copy).then_inc(v_hi, 1)

            def round_q(h, slot):
                act.wait_ge(q_roped, 3 * (h + 1))
                nc.scalar.activation(q_head[slot][0][:, :], q_row[:, :], ACT.Copy).then_inc(q_hi, 1)

            def exponent(h, t, slot):
                g = TT * h + t
                pair = (t + 1) % 2
                act.wait_ge(negmax, g + 1)
                if not (is_first(h) and t < 2):
                    act.wait_ge(turned, 2 * (g - 1))
                if t == 0 and not (isinstance(h, int) and h < 2):
                    act.wait_ge(sums_kept, h - 1)
                at = slot * TT + t
                nc.scalar.activation(probs[t % 2][:, :], chip.pair(pair), ACT.Exp, bias=chip.negmax[:, t % 2:t % 2 + 1],
                                     accum_out=chip.rowsum[:, at:at + 1]).then_inc(exped, 1)

            def round_pt(h, t):
                g = TT * h + t
                b, u = t // 2, t % 2
                if u == 0 and not (is_first(h) and b < 2):
                    act.wait_ge(weighted, 4 * h + b - 1)
                for half in range(2):
                    act.wait_ge(turned, 2 * g + half + 1)
                    nc.scalar.activation(pt[b % 2][0][:, 4 * half:4 * half + 4, u * P:(u + 1) * P],
                                         chip.bank(4 + half).rearrange("p (k q) -> p k q", k=4), ACT.Copy).then_inc(pt_hi, 1)

            def copy_out(h, b):
                blk = 4 * h + b
                act.wait_ge(weighted, blk + 1)
                if not (is_first(h) and b < 2):
                    act.wait_ge(out_turned, blk - 1)
                nc.scalar.activation(out_t[b % 2][:, :], chip.bank(6 + b % 2, P, 2 * P), ACT.Copy).then_inc(out_copied, 1)

            take_q(0, 1)
            round_k(0, 0, 0)
            act.wait_ge(k_rope_step, 3)
            for k in range(2):
                nc.scalar.activation(k_head[k][0][R, :], kr[R, :], ACT.Copy).then_inc(rope_hi, 1)
            for i in range(TT):
                act.wait_ge(v_out, i + 1)
                nc.scalar.activation(v_all[:, i, :], chip.bank(4 + i % 4), ACT.Copy).then_inc(v_stored, 1)
            act.wait_ge(v_stored, TT)
            round_v(0, 0)
            round_q(0, 0)
            exponent(0, 0, 0)

            def step(h, slot):
                more = not is_last(h)
                for t in range(TT):
                    if more and t == T_Q:
                        take_q(h + 1, 0)
                    elif more and t == T_K:
                        round_k(h + 1, 1 - slot, 0)
                    round_pt(h, t)
                    if t < TT - 1:
                        exponent(h, t + 1, slot)
                    elif more:
                        exponent(h + 1, 0, 1 - slot)
                    if t % 2 and t >= 3:
                        copy_out(h, (t - 3) // 2)
                    elif t == 1 and not is_first(h):
                        copy_out(h - 1, 3)
                    if more:
                        if t == 0:
                            round_w(h + 1, 1 - slot)
                        elif t == 4:
                            round_v(h + 1, 1 - slot)
                        elif t == 5:
                            round_q(h + 1, 1 - slot)
            peeled(act, step)
            copy_out(HEADS - 1, 3)

        @block.vector
        def _(dve):
            def rest_w(h, slot):
                dve.wait_ge(w_hi, 2 * h - 1)
                nc.vector.tensor_tensor(wq[slot][1][:, :, :], wq_raw[slot][:, :, :], wq[slot][0][:, :, :].bitcast(F32),
                                        ALU.subtract).then_inc(w_ready, 1)
                dve.wait_ge(w_hi, 2 * h)
                nc.vector.tensor_tensor(wk[slot][1][:, :], wk_raw[slot][:, :], wk[slot][0][:, :].bitcast(F32),
                                        ALU.subtract).then_inc(w_ready, 1)

            dve.wait_ge(ropes_loaded, 32)
            dve.wait_ge(k_swapped, 32)
            nc.vector.tensor_tensor(kr[R, :], kr[R, :], cos_row[R, :], ALU.mult).then_inc(k_rope_step, 1)
            nc.vector.tensor_tensor(swapped[R, :], swapped[R, :], sin_row[R, :], ALU.mult).then_inc(k_rope_step, 1)
            dve.wait_ge(k_rope_step, 2)
            nc.vector.tensor_tensor(kr[R, :], kr[R, :], swapped[R, :], ALU.add).then_inc(k_rope_step, 1)
            dve.wait_ge(k_rope_step, 3)
            for k in range(2):
                dve.wait_ge(rope_hi, k + 1)
                nc.vector.tensor_tensor(k_head[k][1][R, :], kr[R, :], k_head[k][0][R, :].bitcast(F32),
                                        ALU.subtract).then_inc(rope_ready, 1)

            def rest_k(h, slot, pair):
                dve.wait_ge(k_hi, h + 1)
                nc.vector.tensor_tensor(k_head[slot][1][0:NOPE, :], chip.pair(pair, NOPE),
                                        k_head[slot][0][0:NOPE, :].bitcast(F32), ALU.subtract).then_inc(k_ready, 1)

            def rest_q(h, slot):
                dve.wait_ge(q_hi, h + 1)
                nc.vector.tensor_tensor(q_head[slot][1][:, :], q_row[:, :], q_head[slot][0][:, :].bitcast(F32),
                                        ALU.subtract).then_inc(q_ready, 1)

            def row_max(h, t):
                g = TT * h + t
                c = slice(t % 2, t % 2 + 1)
                dve.wait_ge(scored, g + 1)
                if not (is_first(h) and t < 2):
                    dve.wait_ge(exped, g - 1)
                nc.vector.tensor_reduce(chip.rowmax[:, c], chip.pair((t + 1) % 2), AXX, ALU.max).then_inc(maxed, 1)
                dve.wait_ge(maxed, g + 1)
                nc.vector.tensor_scalar(chip.negmax[:, c], chip.rowmax[:, c], -1.0, None, ALU.mult).then_inc(negmax, 1)

            def rest_pt(h, t):
                g = TT * h + t
                b, u = t // 2, t % 2
                for half in range(2):
                    dve.wait_ge(pt_hi, 2 * g + half + 1)
                    view = [pt[b % 2][k][:, 4 * half:4 * half + 4, u * P:(u + 1) * P] for k in range(2)]
                    nc.vector.tensor_tensor(view[1], chip.bank(4 + half).rearrange("p (k q) -> p k q", k=4),
                                            view[0].bitcast(F32), ALU.subtract).then_inc(pt_ready, 1)

            def store_out(h, b):
                dve.wait_ge(out_turned, 4 * h + b + 1)
                at = (6 + b % 2) * HALF + 2 * P
                src = chip.ps[:, at:at + 2 * VD].rearrange("p (u d) -> p u d", u=2)
                dst = attn[:, 2 * b:2 * b + 2, ds(h, 1), 0:VD].rearrange("p u h d -> p u (h d)")
                nc.vector.tensor_copy(dst, src).then_inc(out_stored, 1)

            nc.vector.tensor_tensor(fold[:, :], chip.ident[:, 0:VD], chip.ident[:, VD:2 * VD], ALU.add).then_inc(fold_made, 1)
            rest_k(0, 0, 0)
            rotate_q(dve, nc.vector, 0)
            rest_q(0, 0)
            row_max(0, 0)

            def step(h, slot):
                more = not is_last(h)
                for t in range(TT):
                    if t < TT - 1:
                        row_max(h, t + 1)
                    elif more:
                        row_max(h + 1, 0)
                    if more and t == T_K:
                        rest_k(h + 1, 1 - slot, 0)
                    rest_pt(h, t)
                    if t % 2 == 0 and t >= 4:
                        store_out(h, t // 2 - 2)
                    elif t % 2 == 0 and not is_first(h):
                        store_out(h - 1, t // 2 + 2)
                    if more and t == 0:
                        rest_w(h + 1, 1 - slot)
                    elif more and t == 5:
                        rest_q(h + 1, 1 - slot)
                dve.wait_ge(exped, TT * (h + 1))
                nc.vector.tensor_copy(attn[:, :, ds(h, 1), VD:VD + 1].rearrange("p i h o -> p i (h o)"),
                                      chip.rowsum[:, slot * TT:(slot + 1) * TT].unsqueeze(2)).then_inc(sums_kept, 1)
            peeled(dve, step)
            store_out(HEADS - 1, 2)
            store_out(HEADS - 1, 3)


def mixer_out_block(chip, dram, w, attn, hyena, xT, norm, ffn):
    nc = chip.nc
    CT = D // P
    mix_hi = chip.at("o_mix_hi", 32, [P, CT, SEQ], F32R)
    mix_lo = chip.at("o_mix_lo", 64, [P, CT, SEQ], F32R)
    squares = [chip.at(f"o_squares{k}", 128 + 4 * k, [P, TT, 2, VD]) for k in range(2)]
    normed = [chip.at(f"o_normed{k}", 136 + 4 * k, [P, TT, 2, VD]) for k in range(2)]
    power, rstd, weight2 = chip.o_power, chip.o_rstd, chip.o_weight2
    hy = hyena[:, :, :].rearrange("p i (h d) -> p i h d", d=VD)
    s = chip.sem
    x_loaded, weight_squared, squared, power_ready, rooted = (s("o_x_loaded"), s("o_weight_squared"), s("o_squared"),
                                                              s("o_power_ready"), s("o_rooted"))
    summed, inverted, normed_ready = s("o_summed"), s("o_inverted"), s("o_normed_ready")
    turned, mix_hi_ready, mix_ready, added = s("o_turned"), s("o_mix_hi_ready"), s("o_mix_ready"), s("o_added")

    def heads(ct):
        return attn[:, :, 2 * ct:2 * ct + 2, 0:VD] if ct < CT // 2 else hy[:, :, 2 * ct - HEADS:2 * ct - HEADS + 2, :]

    def flat(t):
        return t[:, :, :, :].rearrange("p i h d -> p (i h) d")

    with nc.Block() as block:
        @block.sync
        def _(sp):
            w.load(sp, 0, 0, 0)
            w.load(sp, 1, 1, P)
            sp.dma_start(xT[:], dram["residual"].rearrange("p (k t) -> p k t", k=KT)).then_inc(x_loaded, 16)
            for n in range(2, CT):
                sp.wait_ge(w.ready, n - 1)
                w.load(sp, n, n % 2, n * P)
                if n == 2:
                    sp.wait_ge(normed_ready, CT // 2)
                    ffn.load_gu(sp, 0, (0,))
            sp.wait_ge(w.ready, CT)
            ffn.load_gu(sp, 0, (1,))

        @block.tensor
        def _(pe):
            def turn(ct):
                pe.wait_ge(normed_ready, ct + 1)
                for r in range(2):
                    n = 2 * ct + r
                    if n >= 4:
                        pe.wait_ge(mix_ready, n - 3)
                    for tt in range(TT // 2):
                        last = nc.tensor.transpose(chip.bank(4 + n % 4)[:, tt * P:(tt + 1) * P],
                                                   normed[ct % 2][:, r * (TT // 2) + tt, :, :].rearrange("p h d -> p (h d)"),
                                                   chip.ident[:, :])
                    last.then_inc(turned, 1)

            turn(0)
            for k in range(CT):
                if k + 1 < CT:
                    turn(k + 1)
                pe.wait_ge(mix_ready, 2 * (k + 1))
                for n in range(2):
                    pe.wait_ge(w.ready, n + 1)
                    last = three_pass(nc, [chip.bank(2 * n), chip.bank(2 * n + 1)], w.split[n][0][:, k, :],
                                      w.split[n][1][:, k, :], halves(mix_hi, k), halves(mix_lo, k), k == 0, k == CT - 1)
                    if k == CT - 1:
                        last.then_inc(w.used, 1)
            for n in range(2, CT):
                pe.wait_ge(added, n - 1)
                w.product(pe, n, n % 2, [chip.bank(2 * (n % 2)), chip.bank(2 * (n % 2) + 1)], mix_hi, mix_lo, None)
            norm.tensor(pe)

        @block.scalar
        def _(act):
            def square(ct):
                if ct >= 2:
                    act.wait_ge(power_ready, ct - 1)
                nc.scalar.activation(squares[ct % 2][:, :, :, :], heads(ct), ACT.Square).then_inc(squared, 1)

            def root(ct):
                act.wait_ge(power_ready, ct + 1)
                eps = {} if ct < CT // 2 else {"bias": chip.eps[:, 0:1]}
                nc.scalar.activation(power[:, ct, :], power[:, ct, :], ACT.Sqrt, scale=1.0 / VD, **eps).then_inc(rooted, 1)

            def round_mix(ct):
                for r in range(2):
                    n = 2 * ct + r
                    act.wait_ge(turned, n + 1)
                    nc.scalar.activation(mix_hi[:, ct, r * HALF:(r + 1) * HALF], chip.bank(4 + n % 4), ACT.Copy,
                                         scale=chip.head_gain[:, ct:ct + 1]).then_inc(mix_hi_ready, 1)

            square(0)
            for ct in range(CT):
                if ct + 1 < CT:
                    square(ct + 1)
                root(ct)
                if ct == 0:
                    w.round(act, 0, 0)
                else:
                    round_mix(ct - 1)
                if ct == 1:
                    w.round(act, 1, 1)
            round_mix(CT - 1)
            for n in range(2, CT):
                w.round(act, n, n % 2)
                if n > 2:
                    norm.scalar(act, n - 3, added, n - 2)
            for k in range(CT - 3, CT):
                norm.scalar(act, k, added, k + 1)

        @block.gpsimd
        def _(pool):
            norm.gpsimd(pool)

        @block.vector
        def _(dve):
            weight = attn[:, :, :, VD:VD + 1].rearrange("p i h o -> p i (h o)")
            nc.vector.tensor_tensor(weight2[:, :, :], weight, weight, ALU.mult).then_inc(weight_squared, 1)
            dve.wait_ge(weight_squared, 1)

            def sum_squares(ct):
                dve.wait_ge(squared, ct + 1)
                nc.vector.tensor_reduce(power[:, ct, :], flat(squares[ct % 2]), AXX, ALU.add).then_inc(
                    summed if ct < CT // 2 else power_ready, 1)
                if ct < CT // 2:
                    dve.wait_ge(summed, ct + 1)
                    view = power[:, ct, :].rearrange("p (i h) -> p i h", h=2)
                    nc.vector.scalar_tensor_tensor(out=view, in0=weight2[:, :, 2 * ct:2 * ct + 2], scalar=EPS * VD,
                                                   in1=view, op0=ALU.mult, op1=ALU.add).then_inc(power_ready, 1)

            def normalise(ct):
                dve.wait_ge(rooted, ct + 1)
                nc.vector.reciprocal(rstd[:, ct, :], power[:, ct, :]).then_inc(inverted, 1)
                dve.wait_ge(inverted, ct + 1)
                if ct >= 2:
                    dve.wait_ge(turned, 2 * (ct - 1))
                scale = rstd[:, ct, :].rearrange("p (i h) -> p i h", h=2).unsqueeze(3).to_broadcast([P, TT, 2, VD])
                nc.vector.tensor_tensor(normed[ct % 2][:, :, :, :], heads(ct), scale, ALU.mult).then_inc(normed_ready, 1)

            def mix_low(ct):
                for r in range(2):
                    n = 2 * ct + r
                    dve.wait_ge(mix_hi_ready, n + 1)
                    part = slice(r * HALF, (r + 1) * HALF)
                    nc.vector.scalar_tensor_tensor(out=mix_lo[:, ct, part], in0=chip.bank(4 + n % 4),
                                                   scalar=chip.head_gain[:, ct:ct + 1], in1=mix_hi[:, ct, part].bitcast(F32),
                                                   op0=ALU.mult, op1=ALU.subtract).then_inc(mix_ready, 1)

            for ct in range(CT):
                sum_squares(ct)
                normalise(ct)
                if ct == 0:
                    w.rest(dve, 0, 0)
                else:
                    mix_low(ct - 1)
                if ct == 1:
                    w.rest(dve, 1, 1)
            mix_low(CT - 1)
            dve.wait_ge(x_loaded, 16)

            def add(n):
                dve.wait_ge(w.used, n + 1)
                view = xT[:, n, :].rearrange("p (t r) -> p r t", r=2)
                nc.vector.tensor_tensor(view, chip.pair(n % 2).rearrange("p (r t) -> p r t", r=2), view,
                                        ALU.add).then_inc(added, 1)
            for n in range(CT):
                add(n)
                if n >= 1:
                    norm.vector(dve, n - 1)
                if n + 2 < CT:
                    w.rest(dve, n + 2, n % 2)
            norm.vector(dve, CT - 1)


def output_block(chip, dram, xT):
    nc = chip.nc
    gain = chip.at("e_gain", 32, [P, D])
    junk = chip.at("e_junk", 36, [P, D])
    Y = 4
    y = [chip.at(f"e_y{k}", 40 + 4 * k, [P, D]) for k in range(Y)]
    total, root = chip.e_total, chip.e_root
    s = chip.sem
    gain_loaded, turned, squared, rooted, scaled = (s("e_gain_loaded"), s("e_turned"), s("e_squared"), s("e_rooted"),
                                                    s("e_scaled"))
    rstd_ready, stored = s("e_rstd_ready"), [s(f"e_stored{k}") for k in range(Y)]
    with nc.Block() as block:
        @block.sync
        def _(sp):
            sp.dma_start(gain[:], dram["final_norm_g"].partition_broadcast(P)).then_inc(gain_loaded, 16)
            for i in range(TT):
                sp.wait_ge(scaled, i + 1)
                sp.dma_start(dram["out"][i * P:(i + 1) * P, :], y[i % Y][:]).then_inc(stored[i % Y], 16)
            for a in range(Y):
                sp.wait_ge(stored[a], 16 * TT // Y)

        @block.tensor
        def _(pe):
            for i in range(TT):
                if i >= 4:
                    pe.wait_ge(scaled, i - 3)
                for k in range(KT):
                    at = (i % 4) * 2 * HALF + k * P
                    last = nc.tensor.transpose(chip.ps[:, at:at + P], xT[:, k, i * P:(i + 1) * P], chip.ident[:, :])
                last.then_inc(turned, 1)

        @block.scalar
        def _(act):
            for i in range(TT):
                act.wait_ge(turned, i + 1)
                if i:
                    act.wait_ge(squared, i)
                nc.scalar.activation(junk[:, :], chip.pair(i % 4), ACT.Square, accum_out=total[:, i:i + 1]).then_inc(squared, 1)
                act.wait_ge(squared, i + 1)
                nc.scalar.activation(root[:, i:i + 1], total[:, i:i + 1], ACT.Sqrt, bias=chip.eps[:, 0:1],
                                     scale=1.0 / D).then_inc(rooted, 1)

        @block.vector
        def _(dve):
            dve.wait_ge(gain_loaded, 16)
            for i in range(TT):
                dve.wait_ge(rooted, i + 1)
                nc.vector.reciprocal(root[:, i:i + 1], root[:, i:i + 1]).then_inc(rstd_ready, 1)
                dve.wait_ge(rstd_ready, i + 1)
                if i >= Y:
                    dve.wait_ge(stored[i % Y], 16 * (i // Y))
                nc.vector.scalar_tensor_tensor(out=y[i % Y][:, :], in0=chip.pair(i % 4), scalar=root[:, i:i + 1],
                                               in1=gain[:, :], op0=ALU.mult, op1=ALU.mult).then_inc(scaled, 1)


def encoder(nc, dram):
    with ExitStack() as ctx:
        chip = Chip(nc, ctx)
        chip.ident = chip.small("ident", [P, P])
        chip.ones = chip.small("ones", [P, P])
        chip.eps = chip.small("eps", [P, 1])
        gains = {}
        for name, tiles in (("ffn1_norm_g", KT), ("mix_norm_g", KT), ("ffn2_norm_g", KT), ("q_norm_g", 2),
                            ("kv_norm_g", 1), ("head_norm_g", KT)):
            gains[name] = chip.small(f"g_{name}", [P, tiles])
        chip.q_gain, chip.kv_gain, chip.head_gain = gains["q_norm_g"], gains["kv_norm_g"], gains["head_norm_g"]
        conv_w = chip.small("conv_w", [P, 3, HY_TILES])
        conv_b = chip.small("conv_b", [P, HY_TILES])
        chip.fw1 = chip.at("f_w1", 204, [EMB, HID])
        chip.fw2 = chip.at("f_w2", 204.25, [HID, HID])
        chip.fcol = chip.small("fcol", [HID, 3])
        chip.negmax = chip.small("negmax", [P, 2])
        chip.rowmax = chip.small("rowmax", [P, 2])
        chip.rowsum = chip.small("rowsum", [P, 2 * TT])
        chip.o_power = chip.small("o_power", [P, KT, 2 * TT])
        chip.o_rstd = chip.at("o_rstd", 201, [P, KT, 2 * TT])
        chip.o_weight2 = chip.at("o_weight2", 202, [P, TT, HEADS])
        chip.e_total = chip.small("e_total", [P, TT])
        chip.e_root = chip.small("e_root", [P, TT])
        chip.consts_ready = chip.sem("consts_ready")
        filled = chip.sem("filled")

        xT = chip.at("xT", 0, [P, KT, SEQ])

        with nc.Block() as block:
            @block.gpsimd
            def _(pool):
                nc.gpsimd.memset(chip.ident[:, :], 0.0).then_inc(filled, 1)
                nc.gpsimd.memset(chip.ones[:, :], 1.0).then_inc(filled, 1)
                nc.gpsimd.memset(chip.eps[:, :], EPS).then_inc(filled, 1)
                pool.wait_ge(filled, 3)
                nc.gpsimd.affine_select(out=chip.ident[:, :], in_=chip.ident[:, :], compare_op=ALU.not_equal, fill=1.0,
                                        base=0, pattern=[[-1, P]], channel_multiplier=1).then_inc(chip.consts_ready, 1)

        x_hi, x_lo = (chip.at(f"x_{k}", 32 + 32 * n, [P, KT, SEQ], F32R) for n, k in enumerate(("hi", "lo")))
        norm1 = FeatureSplit(chip, "n1", xT, gains["ffn1_norm_g"], x_hi, x_lo, 144, 4, 200, 2, added=1)
        ffn1 = Ffn(chip, "f1", dram["ffn1_w_gate"], dram["ffn1_w_up"], dram["ffn1_w_down"], xT, norm1,
                   {"wgu": 96, "h": 128, "d_raw": 160, "gu_raw": (168, 176), "wd": 184})
        norm2 = FeatureSplit(chip, "n2", xT, gains["mix_norm_g"], x_hi, x_lo, 112, 4, 200, 1)
        w_in = ColumnWeights(chip, "m_w", dram["w_in"], 160, 168)
        columns = [(t, dram[name]) for name, t in gains.items()]
        columns += [(conv_w, dram["hyena_conv_w"]), (conv_b, dram["hyena_conv_b"])]
        filters_block(chip, dram, xT, norm1, ffn1, columns)
        ffn1.run(split_here=True, after=MixerInput(norm2, w_in))

        v_hi, v_lo = (chip.at(f"v_{k}", 16 * n, [P, TT, C], F32R) for n, k in enumerate(("hi", "lo")))
        gates = [chip.at(f"gate{k}", 96 + 16 * k, [P, TT, C]) for k in range(2)]
        cq = chip.at("cq", 128, [P, 2, SEQ])
        ckv = chip.at("ckv", 136, [P, 1, SEQ])
        kr = chip.at("kr", 140, [QK, SEQ])
        attn = chip.at("attn", 184, [P, TT, HEADS, VD + 2])
        hyena = Hyena(chip, dram)
        mixer_in_block(chip, xT, dram["residual"].rearrange("p (k t) -> p k t", k=KT), w_in, norm2, cq, ckv, kr,
                       v_hi, v_lo, gates, conv_w, conv_b, hyena)
        attention_input = AttentionInput(chip, dram, cq, ckv)
        hyena.run(v_hi, v_lo, gates, attention_input)
        chip.recycle()
        attention_block(chip, dram, attention_input, kr, attn)
        w_out = ColumnWeights(chip, "o_w", dram["w_out"], 160, 168)
        x2_hi, x2_lo = (chip.at(f"x2_{k}", 96 + 32 * n, [P, KT, SEQ], F32R) for n, k in enumerate(("hi", "lo")))
        norm3 = FeatureSplit(chip, "n3", xT, gains["ffn2_norm_g"], x2_hi, x2_lo, 184, 2, 200, 3)
        ffn2 = Ffn(chip, "f2", dram["ffn2_w_gate"], dram["ffn2_w_up"], dram["ffn2_w_down"], xT, norm3,
                   {"wgu": 32, "h": 64, "gu_raw": (192, 160), "wd": 168, "d_raw": 184})
        mixer_out_block(chip, dram, w_out, attn, gates[1], xT, norm3, ffn2)
        ffn2.run(split_here=False)
        output_block(chip, dram, xT)


INPUTS = ["x", "ffn1_norm_g", "ffn1_w_gate", "ffn1_w_up", "ffn1_w_down", "mix_norm_g", "w_in", "q_norm_g", "w_uq",
          "kv_norm_g", "w_ukv", "hyena_conv_w", "hyena_conv_b", "filt_w1", "filt_b1", "filt_w2", "filt_b2", "filt_w3",
          "filt_freq", "hyena_d", "head_norm_g", "w_out", "ffn2_norm_g", "ffn2_w_gate", "ffn2_w_up", "ffn2_w_down",
          "final_norm_g"]
COLUMNS = ("ffn1_norm_g", "mix_norm_g", "ffn2_norm_g", "q_norm_g", "kv_norm_g", "head_norm_g", "hyena_conv_w",
           "hyena_conv_b", "filt_b1", "filt_b2", "filt_freq")


def kernel(**inputs):
    import concourse.bacc as _bacc
    from concourse.bass_utils import run_bass_kernel_spmd as _run

    nc = _bacc.Bacc("TRN2", target_bir_lowering=False, num_devices=1)
    arrays, dram = {}, {}
    for name in INPUTS:
        a = np.ascontiguousarray(inputs[name])
        a = a.reshape(a.shape[1:]) if a.ndim > 1 else a
        if name in COLUMNS:
            a = np.ascontiguousarray(np.moveaxis(a.reshape(*a.shape[:-1], -1, min(P, a.shape[-1])), -1, 0))
        arrays[f"in_{name}"] = a
        dram[name] = nc.dram_tensor(f"in_{name}", a.shape, F32, kind="ExternalInput").ap()
    out = nc.dram_tensor("out_y", (SEQ, D), F32, kind="ExternalOutput")
    dram["out"] = out.ap()
    dram["residual"] = nc.dram_tensor("residual", (P, KT * SEQ), F32, kind="Internal").ap()
    dram["spectra"] = nc.dram_tensor("spectra", (2 * WT * P, 4 * C), F32, kind="Internal").ap()
    fwd, inv = transform_tables()
    for name, a in (("fwd", fwd), ("inv", inv), ("features", filter_features()), ("decay", filter_decay()),
                    ("rope", rope_rows())):
        dram[name] = nc.inline_tensor(a, name=f"c_{name}").ap()
    encoder(nc, dram)
    r = _run(nc, [arrays], core_ids=[0])
    return r.results[0]["out_y"].reshape(1, SEQ, D)
```
